# Optimizing a Trainium2 kernel written in Bass

```python
import math
import numpy as np
import jax
import jax.numpy as jnp
from jax import lax

D_MODEL = 2048
BATCH = 1
SEQ = 256
DEPTH = 1

HEAD_DIM = 128
N_SB_HEADS = 8
N_NSA_HEADS = 8
N_NSA_KV = 2
NSA_GROUP = N_NSA_HEADS // N_NSA_KV
SB_WIDTH = N_SB_HEADS * HEAD_DIM
NSA_WIDTH = N_NSA_HEADS * HEAD_DIM
KV_WIDTH = N_NSA_KV * HEAD_DIM
MIX_WIDTH = SB_WIDTH + NSA_WIDTH
N_GATES = 3 * N_NSA_HEADS
IN_SPLITS = (SB_WIDTH, SB_WIDTH, SB_WIDTH, NSA_WIDTH, KV_WIDTH, KV_WIDTH, KV_WIDTH, KV_WIDTH, KV_WIDTH, KV_WIDTH, N_GATES)
IN_COLS = sum(IN_SPLITS)
Q_BLOCK = 128
CMP_BLOCK = 32
CMP_STRIDE = 16
CMP_HIDDEN = 256
SEL_BLOCK = 64
N_SELECT = 16
SEL_Q_CHUNK = 32
WINDOW = 512
N_BUCKETS = 32
MAX_DISTANCE = 128
PEER_HEADS = 8
PEER_N_KEYS = 128
PEER_N_EXPERTS = PEER_N_KEYS * PEER_N_KEYS
PEER_D_KEY = 256
PEER_TOPK = 16
PEER_TOKEN_CHUNK = 128
EPS = 1e-6
NEG = -1e30
BIG = 1e30

kernel_name = 'hybrid_sb_nsa_peer_layer'

def rms_norm(x, g):
    xf = x.astype(jnp.float32)
    y = xf * lax.rsqrt(jnp.mean(xf * xf, axis=-1, keepdims=True) + EPS)
    return (y * g.astype(jnp.float32)).astype(x.dtype)

def masked_softmax(s, valid):
    p = jax.nn.softmax(jnp.where(valid, s, NEG), axis=-1)
    return jnp.where(valid, p, 0.0)

def t5_bucket(dist):
    max_exact = N_BUCKETS // 2
    d = jnp.maximum(dist, 0)
    log_ratio = jnp.log(jnp.maximum(d, 1).astype(jnp.float32) / max_exact) / math.log(MAX_DISTANCE / max_exact)
    large = jnp.minimum(max_exact + (log_ratio * (N_BUCKETS - max_exact)).astype(jnp.int32), N_BUCKETS - 1)
    return jnp.where(d < max_exact, d, large)

def rel_bias_grid(table, dist):
    b = jnp.take(table, t5_bucket(dist), axis=0)
    return jnp.moveaxis(b, -1, 0).reshape(N_NSA_KV, NSA_GROUP, *dist.shape)

def stick_breaking_attention(q, k, v):
    B, H, T, Dh = q.shape
    scale = Dh ** -0.5
    kpos = jnp.arange(T)

    def block(i):
        qb = lax.dynamic_slice_in_dim(q, i * Q_BLOCK, Q_BLOCK, axis=2)
        qpos = i * Q_BLOCK + jnp.arange(Q_BLOCK)
        z = jnp.einsum('bhqd,bhkd->bhqk', qb, k, preferred_element_type=jnp.float32) * scale
        before = kpos[None, :] < qpos[:, None]
        log_keep = jnp.where(before, -jax.nn.softplus(z), 0.0)
        log_between = lax.cumsum(log_keep, axis=3, reverse=True) - log_keep
        a = jnp.where(before, jnp.exp(jax.nn.log_sigmoid(z) + log_between), 0.0)
        return jnp.einsum('bhqk,bhkd->bqhd', a.astype(v.dtype), v)

    out = lax.map(block, jnp.arange(T // Q_BLOCK))
    return jnp.moveaxis(out, 0, 1).reshape(B, T, H * Dh)

def compress_blocks(kv, pe, w1, w2):
    B, T, G, Dh = kv.shape
    nc = (T - CMP_BLOCK) // CMP_STRIDE + 1
    idx = jnp.arange(nc)[:, None] * CMP_STRIDE + jnp.arange(CMP_BLOCK)[None, :]
    blocks = kv[:, idx] + pe[None, None, :, None, :]
    flat = jnp.moveaxis(blocks, 3, 2).reshape(B, nc, G, CMP_BLOCK * Dh)
    return jax.nn.gelu(flat @ w1) @ w2

def block_overlap(nc, nb):
    c0 = np.arange(nc)[:, None] * CMP_STRIDE
    s0 = np.arange(nb)[None, :] * SEL_BLOCK
    ov = np.minimum(c0 + CMP_BLOCK, s0 + SEL_BLOCK) - np.maximum(c0, s0)
    return jnp.asarray(np.clip(ov, 0, None).astype(np.float32) / np.float32(CMP_BLOCK))

def compressed_attention(q, kc, vc, table):
    B, G, R, T, Dh = q.shape
    nc = kc.shape[2]
    nb = T // SEL_BLOCK
    scale = Dh ** -0.5
    c_end = jnp.arange(nc) * CMP_STRIDE + CMP_BLOCK - 1
    overlap = block_overlap(nc, nb)

    def block(i):
        qb = lax.dynamic_slice_in_dim(q, i * Q_BLOCK, Q_BLOCK, axis=3)
        qpos = i * Q_BLOCK + jnp.arange(Q_BLOCK)
        dist = qpos[:, None] - c_end[None, :]
        s = jnp.einsum('bgrqd,bgcd->bgrqc', qb, kc, preferred_element_type=jnp.float32) * scale + rel_bias_grid(table, dist)
        p = masked_softmax(s, dist >= 0)
        o = jnp.einsum('bgrqc,bgcd->bgrqd', p.astype(vc.dtype), vc)
        imp = jnp.einsum('bgrqc,cn->bgqn', p, overlap)
        return o, imp

    o, imp = lax.map(block, jnp.arange(T // Q_BLOCK))
    return (jnp.moveaxis(o, 0, 3).reshape(B, G, R, T, Dh), jnp.moveaxis(imp, 0, 2).reshape(B, G, T, nb))

def selected_attention(q, k, v, imp, table):
    B, G, R, T, Dh = q.shape
    nb = T // SEL_BLOCK
    n_sel = min(N_SELECT, nb)
    scale = Dh ** -0.5
    blk = jnp.arange(nb)
    cur = jnp.arange(T) // SEL_BLOCK
    forced = (blk[None, :] == 0) | (blk[None, :] == cur[:, None]) | (blk[None, :] == cur[:, None] - 1)
    future = blk[None, :] > cur[:, None]
    score = jnp.where(forced, BIG, jnp.where(future, NEG, imp))
    _, sel = lax.top_k(score, n_sel)
    kb = k.reshape(B, G, nb, SEL_BLOCK, Dh)
    vb = v.reshape(B, G, nb, SEL_BLOCK, Dh)
    gather = jax.vmap(jax.vmap(lambda blocks, ix: blocks[ix]))
    tab_gr = jnp.swapaxes(table.reshape(N_BUCKETS, G, R), 0, 1)
    g_index = jnp.arange(G)[None, :, None, None]
    n_keys = n_sel * SEL_BLOCK

    def chunk(i):
        qc = lax.dynamic_slice_in_dim(q, i * SEL_Q_CHUNK, SEL_Q_CHUNK, axis=3)
        ic = lax.dynamic_slice_in_dim(sel, i * SEL_Q_CHUNK, SEL_Q_CHUNK, axis=2)
        qpos = i * SEL_Q_CHUNK + jnp.arange(SEL_Q_CHUNK)
        kg = gather(kb, ic).reshape(B, G, SEL_Q_CHUNK, n_keys, Dh)
        vg = gather(vb, ic).reshape(B, G, SEL_Q_CHUNK, n_keys, Dh)
        kpos = (ic[..., None] * SEL_BLOCK + jnp.arange(SEL_BLOCK)).reshape(B, G, SEL_Q_CHUNK, n_keys)
        dist = qpos[None, None, :, None] - kpos
        bias = jnp.moveaxis(tab_gr[g_index, t5_bucket(dist)], -1, 2)
        s = jnp.einsum('bgrqd,bgqkd->bgrqk', qc, kg, preferred_element_type=jnp.float32) * scale + bias
        p = masked_softmax(s, (dist >= 0)[:, :, None])
        return jnp.einsum('bgrqk,bgqkd->bgrqd', p.astype(vg.dtype), vg)

    o = lax.map(chunk, jnp.arange(T // SEL_Q_CHUNK))
    return jnp.moveaxis(o, 0, 3).reshape(B, G, R, T, Dh)

def window_attention(q, k, v, table):
    B, G, R, T, Dh = q.shape
    scale = Dh ** -0.5
    span = WINDOW + Q_BLOCK
    kp = jnp.pad(k, ((0, 0), (0, 0), (WINDOW, 0), (0, 0)))
    vp = jnp.pad(v, ((0, 0), (0, 0), (WINDOW, 0), (0, 0)))

    def block(i):
        qb = lax.dynamic_slice_in_dim(q, i * Q_BLOCK, Q_BLOCK, axis=3)
        kb = lax.dynamic_slice_in_dim(kp, i * Q_BLOCK, span, axis=2)
        vb = lax.dynamic_slice_in_dim(vp, i * Q_BLOCK, span, axis=2)
        qpos = i * Q_BLOCK + jnp.arange(Q_BLOCK)
        kpos = i * Q_BLOCK - WINDOW + jnp.arange(span)
        dist = qpos[:, None] - kpos[None, :]
        valid = (dist >= 0) & (dist < WINDOW) & (kpos[None, :] >= 0)
        s = jnp.einsum('bgrqd,bgkd->bgrqk', qb, kb, preferred_element_type=jnp.float32) * scale + rel_bias_grid(table, dist)
        p = masked_softmax(s, valid)
        return jnp.einsum('bgrqk,bgkd->bgrqd', p.astype(vb.dtype), vb)

    o = lax.map(block, jnp.arange(T // Q_BLOCK))
    return jnp.moveaxis(o, 0, 3).reshape(B, G, R, T, Dh)

def hybrid_mixer(h, w_in, cmp_pe, cmp_k_w1, cmp_k_w2, cmp_v_w1, cmp_v_w2, q_norm_g, k_norm_g,
                 rel_bias_table, sb_out_g, nsa_out_g, w_out):
    B, T, _ = h.shape
    G, R, Dh = N_NSA_KV, NSA_GROUP, HEAD_DIM
    cuts = [int(c) for c in np.cumsum(IN_SPLITS)[:-1]]
    q_sb, k_sb, v_sb, q_nsa, k_cmp, v_cmp, k_slc, v_slc, k_win, v_win, gate_logits = jnp.split(h @ w_in, cuts, axis=-1)

    sb_heads = lambda t: t.reshape(B, T, N_SB_HEADS, Dh).transpose(0, 2, 1, 3)
    o_sb = stick_breaking_attention(sb_heads(q_sb), sb_heads(k_sb), sb_heads(v_sb))

    kv_heads = lambda t: t.reshape(B, T, G, Dh)
    to_bgtd = lambda t: t.transpose(0, 2, 1, 3)
    q = rms_norm(q_nsa.reshape(B, T, G, R, Dh), q_norm_g).transpose(0, 2, 3, 1, 4)
    kc = to_bgtd(rms_norm(compress_blocks(kv_heads(k_cmp), cmp_pe, cmp_k_w1, cmp_k_w2), k_norm_g))
    vc = to_bgtd(compress_blocks(kv_heads(v_cmp), cmp_pe, cmp_v_w1, cmp_v_w2))
    o_cmp, importance = compressed_attention(q, kc, vc, rel_bias_table)
    o_slc = selected_attention(q, to_bgtd(rms_norm(kv_heads(k_slc), k_norm_g)), to_bgtd(kv_heads(v_slc)), importance, rel_bias_table)
    o_win = window_attention(q, to_bgtd(rms_norm(kv_heads(k_win), k_norm_g)), to_bgtd(kv_heads(v_win)), rel_bias_table)
    gates = jax.nn.sigmoid(gate_logits).reshape(B, T, G, R, 3).transpose(0, 2, 3, 1, 4)
    o_nsa = gates[..., 0:1] * o_cmp + gates[..., 1:2] * o_slc + gates[..., 2:3] * o_win
    o_nsa = o_nsa.transpose(0, 3, 1, 2, 4).reshape(B, T, NSA_WIDTH)

    mixed = jnp.concatenate([rms_norm(o_sb, sb_out_g), rms_norm(o_nsa, nsa_out_g)], axis=-1)
    return mixed @ w_out

def peer_ffn(h, w_query, sub_keys, expert_u, expert_v):
    B, T, D = h.shape
    n_tok = B * T
    C = PEER_TOKEN_CHUNK
    half = PEER_D_KEY // 2

    def chunk(xc):
        qc = (xc @ w_query).reshape(C, PEER_HEADS, 2, half)
        s = jnp.einsum('chpd,hpnd->chpn', qc, sub_keys, preferred_element_type=jnp.float32)
        top_s, top_i = lax.top_k(s, PEER_TOPK)
        cand_s = (top_s[:, :, 0, :, None] + top_s[:, :, 1, None, :]).reshape(C, PEER_HEADS, PEER_TOPK * PEER_TOPK)
        cand_i = (top_i[:, :, 0, :, None] * PEER_N_KEYS + top_i[:, :, 1, None, :]).reshape(C, PEER_HEADS, PEER_TOPK * PEER_TOPK)
        best_s, best_pos = lax.top_k(cand_s, PEER_TOPK)
        expert_idx = jnp.take_along_axis(cand_i, best_pos, axis=-1)
        g = jax.nn.softmax(best_s, axis=-1)
        u = expert_u[expert_idx]
        vv = expert_v[expert_idx]
        act = jax.nn.gelu(jnp.einsum('chkd,cd->chk', u, xc, preferred_element_type=jnp.float32))
        return jnp.einsum('chk,chkd->cd', (g * act).astype(vv.dtype), vv)

    out = lax.map(chunk, h.reshape(n_tok // C, C, D))
    return out.reshape(B, T, D)

def setup_inputs(seed: int = 0) -> dict:
    key = jax.random.key(seed)
    ks = jax.random.split(key, 19)
    f32 = jnp.float32
    L = DEPTH

    def nrm(k, shape, scale):
        return jax.random.normal(k, shape, f32) * scale

    def gain(k, shape):
        return 1.0 + 0.02 * jax.random.normal(k, shape, f32)

    return {
        'x': nrm(ks[0], (BATCH, SEQ, D_MODEL), 1.0),
        'norm1_g': gain(ks[1], (L, D_MODEL)),
        'w_in': nrm(ks[2], (L, D_MODEL, IN_COLS), D_MODEL ** -0.5),
        'cmp_pe': nrm(ks[3], (L, CMP_BLOCK, HEAD_DIM), 0.2),
        'cmp_k_w1': nrm(ks[4], (L, CMP_BLOCK * HEAD_DIM, CMP_HIDDEN), (CMP_BLOCK * HEAD_DIM) ** -0.5),
        'cmp_k_w2': nrm(ks[5], (L, CMP_HIDDEN, HEAD_DIM), CMP_HIDDEN ** -0.5),
        'cmp_v_w1': nrm(ks[6], (L, CMP_BLOCK * HEAD_DIM, CMP_HIDDEN), (CMP_BLOCK * HEAD_DIM) ** -0.5),
        'cmp_v_w2': nrm(ks[7], (L, CMP_HIDDEN, HEAD_DIM), CMP_HIDDEN ** -0.5),
        'q_norm_g': gain(ks[8], (L, HEAD_DIM)),
        'k_norm_g': gain(ks[9], (L, HEAD_DIM)),
        'rel_bias_table': nrm(ks[10], (N_BUCKETS, N_NSA_HEADS), 0.5),
        'sb_out_g': gain(ks[11], (L, SB_WIDTH)),
        'nsa_out_g': gain(ks[12], (L, NSA_WIDTH)),
        'w_out': nrm(ks[13], (L, MIX_WIDTH, D_MODEL), MIX_WIDTH ** -0.5),
        'norm2_g': gain(ks[14], (L, D_MODEL)),
        'peer_w_query': nrm(ks[15], (L, D_MODEL, PEER_HEADS * PEER_D_KEY), D_MODEL ** -0.5),
        'peer_sub_keys': nrm(ks[16], (L, PEER_HEADS, 2, PEER_N_KEYS, PEER_D_KEY // 2), (PEER_D_KEY // 2) ** -0.5),
        'peer_expert_u': nrm(ks[17], (L, PEER_N_EXPERTS, D_MODEL), D_MODEL ** -0.5),
        'peer_expert_v': nrm(ks[18], (L, PEER_N_EXPERTS, D_MODEL), 0.5),
    }

def reference(x, norm1_g, w_in, cmp_pe, cmp_k_w1, cmp_k_w2, cmp_v_w1, cmp_v_w2, q_norm_g, k_norm_g,
              rel_bias_table, sb_out_g, nsa_out_g, w_out, norm2_g, peer_w_query, peer_sub_keys,
              peer_expert_u, peer_expert_v):
    for l in range(DEPTH):
        h = rms_norm(x, norm1_g[l])
        x = x + hybrid_mixer(h, w_in[l], cmp_pe[l], cmp_k_w1[l], cmp_k_w2[l], cmp_v_w1[l], cmp_v_w2[l],
                             q_norm_g[l], k_norm_g[l], rel_bias_table, sb_out_g[l], nsa_out_g[l], w_out[l])
        h = rms_norm(x, norm2_g[l])
        x = x + peer_ffn(h, peer_w_query[l], peer_sub_keys[l], peer_expert_u[l], peer_expert_v[l])
    return x


_drawn_inputs = setup_inputs


def setup_inputs(seed=0):
    import zlib

    import numpy as np

    out = dict(_drawn_inputs(seed))
    spreads = {}
    factors = {'q_norm_g': 3.388,
     'k_norm_g': 3.317,
     'sb_out_g': 28.928,
     'nsa_out_g': 29.453,
     'norm2_g': 16.037}
    for name, (base, spread) in spreads.items():
        noise = np.random.default_rng([zlib.crc32(name.encode()), seed]).standard_normal(out[name].shape)
        drawn = base * np.exp(spread * noise) if base else spread * noise
        out[name] = jnp.asarray(drawn.astype(out[name].dtype))
    for name, factor in factors.items():
        out[name] = (out[name] * factor).astype(out[name].dtype)
    return out
```

```python
from contextlib import ExitStack

import numpy as np

import concourse.bass as bass
from concourse import mybir

ALU = mybir.AluOpType
ACT = mybir.ActivationFunctionType
F32 = mybir.dt.float32
F32R = mybir.dt.float32r
U32 = mybir.dt.uint32
AX_X = mybir.AxisListType.X

P = 128
T = 256
D = 2048
TT = T // P
KC = D // P
HD = 128
NH = 8
NG = 2
GROUP = NH // NG
IN_COLS = 5656
EPS = 1e-6
NEG = -1e30
SCALE = HD ** -0.5
CMP_BLOCK, CMP_STRIDE, CMP_HIDDEN = 32, 16, 256
NC = (T - CMP_BLOCK) // CMP_STRIDE + 1
N_BUCKETS, MAX_DISTANCE = 32, 128
NKEYS = 128
TOPK = 16
HP = 2 * NH
NE = NKEYS * NKEYS

COL_QSB, COL_KSB, COL_VSB, COL_Q = 0, 1024, 2048, 3072
COL_KCMP, COL_VCMP, COL_KSLC, COL_VSLC, COL_KWIN, COL_VWIN, COL_GATE = 4096, 4352, 4608, 4864, 5120, 5376, 5632
N_GATES = IN_COLS - COL_GATE

G_NORM1, G_NORM2, G_MIX, G_Q, G_K, G_PE = 0, 16, 32, 48, 49, 50
G_ALL = G_PE + CMP_BLOCK

RAW = 4
SPLIT = 2
STEP = 1024
CHUNK = 512
W_IN_CHUNKS = COL_GATE // CHUNK
STEPS_PER_CHUNK = D * CHUNK // P // STEP
TAIL_STEPS = 4
TAIL_K = KC // TAIL_STEPS
W_CHUNKS = D // CHUNK
CMP_STEPS = 2 * CMP_BLOCK * HD * CMP_HIDDEN // P // STEP
CMP_L = STEP // CMP_HIDDEN
E_STEPS = 2 * NE // P

RAW_IN = 0
RAW_TAIL = RAW_IN + W_IN_CHUNKS * STEPS_PER_CHUNK
RAW_CMP = RAW_TAIL + TAIL_STEPS
RAW_OUT = RAW_CMP + CMP_STEPS
RAW_QUERY = RAW_OUT + W_CHUNKS * STEPS_PER_CHUNK
RAW_U = RAW_QUERY + W_CHUNKS * STEPS_PER_CHUNK
RAW_V = RAW_U + E_STEPS

SP_IN = 0
SP_TAIL = SP_IN + W_IN_CHUNKS * STEPS_PER_CHUNK
SP_OUT = SP_TAIL + TAIL_STEPS
SP_QUERY = SP_OUT + W_CHUNKS * STEPS_PER_CHUNK
SP_U = SP_QUERY + W_CHUNKS * STEPS_PER_CHUNK
SP_V = SP_U + E_STEPS

CH_IN, CH_TAIL, CH_OUT = 0, W_IN_CHUNKS, W_IN_CHUNKS + 1
CH_QUERY = CH_OUT + W_CHUNKS

BIAS_W = 512
NE_T = NE // P
TOKENS_PER_BANK = 4
BUILD_STEPS = T // TOKENS_PER_BANK


def bucket_onehot():
    dist = np.maximum(T - np.arange(BIAS_W), 0)
    exact = N_BUCKETS // 2
    ratio = np.log(np.maximum(dist, 1).astype(np.float32) / np.float32(exact)) / np.float32(np.log(MAX_DISTANCE / exact))
    large = np.minimum(exact + (ratio * (N_BUCKETS - exact)).astype(np.int32), N_BUCKETS - 1)
    bucket = np.where(dist < exact, dist, large)
    return (np.arange(N_BUCKETS)[:, None] == bucket[None, :]).astype(np.float32)


def layer(nc, x, norm1_g, w_in, cmp_pe, cmp_k_w1, cmp_k_w2, cmp_v_w1, cmp_v_w2, q_norm_g, k_norm_g,
          rel_bias_table, sb_out_g, nsa_out_g, w_out, norm2_g, peer_w_query, peer_sub_keys,
          peer_expert_u, peer_expert_v, onehot, out):
    with ExitStack() as ctx:
        def sb(name, shape, dt=F32):
            return ctx.enter_context(nc.sbuf_tensor(name, shape, dt))

        sems = {}

        def sem(name):
            if name not in sems:
                sems[name] = ctx.enter_context(nc.semaphore(name))
            return sems[name]

        x1_dram = nc.dram_tensor("x1_dram", [T, D], F32, kind="Internal").ap()
        bias_dram = nc.dram_tensor("bias_dram", [NH, P, BIAS_W + 1], F32, kind="Internal").ap()

        big = sb("big", [P, NE_T * T])
        raw = sb("raw", [P, RAW, STEP])
        split_hi = sb("split_hi", [P, SPLIT, STEP], F32R)
        split_lo = sb("split_lo", [P, SPLIT, STEP], F32R)
        ht = sb("ht", [P, KC, 2 * T], F32R)
        ident = sb("ident", [P, P])
        iota = sb("iota", [P, P])
        neg_tri = sb("neg_tri", [P, P])
        neg_ones = sb("neg_ones", [P, P])
        before = sb("before", [P, P])
        gain_cols = sb("gain_cols", [P, G_ALL])
        picked = sb("picked", [P, 3, T])
        s_sum = sb("s_sum", [P, 2, T])
        w_hi = sb("w_hi", [P, 2, T], F32R)
        w_lo = sb("w_lo", [P, 2, T], F32R)
        small = sb("small", [P, 520])
        ps = ctx.enter_context(nc.psum_tensor("ps", [P, 8, 512], F32))
        psf = ps[:, :, :].rearrange("p b n -> p (b n)")

        at = [0]

        def tiny(n):
            at[0] += n
            assert at[0] <= 520
            return small[:, at[0] - n:at[0]]

        ssq = tiny(8)
        rstd = tiny(8)
        gates = tiny(TT * N_GATES)
        nssq = tiny(24)
        nrstd = tiny(24)
        row_max = tiny(16)
        row_sum = tiny(16)
        coef = tiny(16)
        has_block = tiny(1)
        cmp_p = tiny(16 * NC)
        kssq = tiny(2)
        krstd = tiny(2)
        minus_half = tiny(24)

        at_big = [0]

        def part(n, at=None):
            a = at_big[0] if at is None else at
            at_big[0] = a + n
            assert a + n <= NE_T * T
            return big[:, a:a + n]

        X = part(TT * D).rearrange("p (t d) -> p t d", t=TT)
        A_PROJ = TT * D
        PROJ = part(TT * IN_COLS).rearrange("p (t n) -> p t n", t=TT)
        MIX = part(TT * D).rearrange("p (t d) -> p t d", t=TT)
        A_XN = A_PROJ + TT * IN_COLS + TT * D
        XN = part(TT * D).rearrange("p (t d) -> p t d", t=TT)
        QKT = part(4 * 512, A_XN).rearrange("p (h n) -> p h n", h=4)
        T1f = part(4 * 384)
        T2f = part(4 * 384)
        T1 = T1f.rearrange("p (h n) -> p h n", h=4)
        T2 = T2f.rearrange("p (h n) -> p h n", h=4)
        T2b = T2f.rearrange("p (b n) -> p b n", b=12)
        A_T1 = A_XN + 2048
        PCT = big[:, A_T1:A_T1 + 2048].rearrange("p (b n) -> p b n", b=16)
        BIAS = part(NH * 384).rearrange("p (h n) -> p h n", h=NH)
        A_QT = at_big[0]
        QT = part(NH * T).rearrange("p (h n) -> p h n", h=NH)
        KT = part(2 * NG * T).rearrange("p (b g n) -> p b g n", b=2, g=NG)
        KVC = part(2 * NG * T).rearrange("p (b g n) -> p b g n", b=2, g=NG)
        W2S = part(512).rearrange("p (w n) -> p w n", w=4)
        SQ = big[:, A_QT:A_QT + 2048]
        SQK = big[:, A_QT + 2048:A_QT + 3072]
        gain_rows = MIX[:, 0, 1536:1536 + P]
        HG = big[:, A_XN:A_XN + 512].rearrange("p (v n) -> p v n", v=2)
        HGT = big[:, A_XN + 512:A_XN + 768].rearrange("p (w n) -> p w n", w=4)
        KCV = big[:, A_XN + 768:A_XN + 1280].rearrange("p (v g n) -> p v g n", v=2, g=NG)
        KCT = big[:, A_XN + 1280:A_XN + 1312].rearrange("p (g n) -> p g n", g=NG)
        KSQ = big[:, A_XN + 1312:A_XN + 1568].rearrange("p (g n) -> p g n", g=NG)
        BLK = PROJ[:, :, 0:CMP_BLOCK * 64].rearrange("p v (l n) -> p v l n", l=CMP_BLOCK)
        TMP = PROJ[:, 0, COL_VSB:COL_VSB + 1024]
        ROWB = MIX[0:NH, 0, 0:BIAS_W]
        TABLE = MIX[0:N_BUCKETS, 0, 1024:1024 + NH]
        ONEHOT = MIX[0:N_BUCKETS, 1, 0:BIAS_W]

        Q = big[:, A_PROJ:A_PROJ + TT * D].rearrange("p (t d) -> p t d", t=TT)
        A_R = 16384
        SK = part(2048, A_R).rearrange("p (w n) -> p w n", w=HP)
        SKT = part(2048).rearrange("p (w n) -> p w n", w=HP)
        PQT = part(4096).rearrange("p (w n) -> p w n", w=HP)
        S = part(4096).rearrange("p (t w n) -> p t w n", t=TT, w=HP)
        CAND = part(4096).rearrange("p (t h n) -> p t h n", t=TT, h=NH)
        EQ = big[:, A_R:A_R + 2048].rearrange("p (h k a) -> p h k a", h=NH, k=TOPK)
        A_TOP = A_R + 4096
        TOPS = part(512, A_TOP).rearrange("p (t w k) -> p t w k", t=TT, w=HP)
        TOPI = part(512).bitcast(U32).rearrange("p (t w k) -> p t w k", t=TT, w=HP)
        TOPF = part(512).rearrange("p (t w k) -> p t w k", t=TT, w=HP)
        BEST = part(256).rearrange("p (t h k) -> p t h k", t=TT, h=NH)
        POS = part(256).bitcast(U32).rearrange("p (t h k) -> p t h k", t=TT, h=NH)
        POSAB = part(512).bitcast(U32).rearrange("p (s n) -> p s n", s=2)
        POSF = part(512).rearrange("p (s t h k) -> p s t h k", s=2, t=TT, h=NH)
        PICK = part(768).rearrange("p (s t h k) -> p s t h k", s=3, t=TT, h=NH)
        GSUM = part(16).rearrange("p (t h) -> p t h", t=TT)

        WACT = big[:, :].rearrange("p (i c) -> p i c", c=T)
        WACT_C = big[:, :].rearrange("p (i c) -> p c i", c=T)
        ONE_I = raw[:, 2, :].rearrange("p (s n) -> p s n", s=2)
        ONE_J = raw[:, 3, :].rearrange("p (s n) -> p s n", s=2)
        X1 = big[:, 0:TT * D].rearrange("p (t d) -> p t d", t=TT)

        x_rows = x.rearrange("b (t p) d -> p (b t) d", p=P)
        x1_rows = x1_dram.rearrange("(t p) d -> p t d", p=P)
        out_rows = out.rearrange("b (t p) d -> p (b t) d", p=P)
        win_k = w_in[0].rearrange("(k p) n -> p k n", p=P)
        wout_k = w_out[0].rearrange("(k p) n -> p k n", p=P)
        wq_k = peer_w_query[0].rearrange("(k p) n -> p k n", p=P)
        u_rows = peer_expert_u[0].rearrange("(i p) (f d) -> i f p d", p=P, f=2)
        v_rows = peer_expert_v[0].rearrange("(i p) (f d) -> i f p d", p=P, f=2)

        raw_loaded = [sem(f"raw_loaded{i}") for i in range(RAW)]
        hi_done, split_done, split_free = sem("hi_done"), sem("split_done"), sem("split_free")
        acc_free = sem("acc_free")
        u_turned = sem("u_turned")
        cmp_used = sem("cmp_used")
        x1_stored, out_stored = sem("x1_stored"), sem("out_stored")

        def loaded(eng, slot, g):
            eng.wait_ge(raw_loaded[slot], 16 * (g // RAW + 1))

        block = ctx.enter_context(nc.Block())

        @block.sync
        def _(sp):
            def load(slot, src, shape=None):
                dst = raw[:, slot, :]
                if shape:
                    dst = dst[:, 0:shape[0] * shape[1]].rearrange("p (a b) -> p a b", a=shape[0])
                sp.dma_start(dst, src).then_inc(raw_loaded[slot], 16)

            def chunk(src_k, c, signal, first):
                for s in range(STEPS_PER_CHUNK):
                    if first is not None or s >= RAW:
                        sp.wait_ge(signal, (0 if first is None else first) + s - (RAW if first is None else 0) + 1)
                    load(s % RAW, src_k[:, 2 * s:2 * s + 2, bass.ds(c * CHUNK, CHUNK)], (2, CHUNK))

            sp.dma_start(X, x_rows).then_inc(sem("x_loaded"), 16)
            for src, row, n in ((norm1_g[0], G_NORM1, 16), (norm2_g[0], G_NORM2, 16), (sb_out_g[0], G_MIX, 8),
                                (nsa_out_g[0], G_MIX + 8, 8), (q_norm_g[0], G_Q, 1), (k_norm_g[0], G_K, 1)):
                sp.dma_start(gain_rows[row:row + n, :], src.rearrange("(a n) -> a n", n=P)).then_inc(sem("gains_loaded"), 16)
            sp.dma_start(gain_rows[G_PE:G_ALL, :], cmp_pe[0]).then_inc(sem("gains_loaded"), 16)
            sp.dma_start(TABLE, rel_bias_table).then_inc(sem("table_loaded"), 16)
            sp.dma_start(ONEHOT, onehot).then_inc(sem("table_loaded"), 16)
            for v, w2 in enumerate((cmp_k_w2, cmp_v_w2)):
                sp.dma_start(W2S[:, 2 * v:2 * v + 2, :], w2[0].rearrange("(f p) n -> p f n", p=P)).then_inc(sem("w2_loaded"), 16)
            chunk(win_k, 0, split_done, None)
            with sp.Fori(1, W_IN_CHUNKS) as c:
                chunk(win_k, c, split_done, c * STEPS_PER_CHUNK - RAW)
            for s in range(TAIL_STEPS):
                sp.wait_ge(split_done, SP_TAIL + s - RAW + 1)
                load(s, win_k[:, TAIL_K * s:TAIL_K * (s + 1), COL_GATE:IN_COLS], (TAIL_K, N_GATES))
            for s in range(CMP_STEPS):
                if s < RAW:
                    sp.wait_ge(split_done, SP_TAIL + s + 1)
                else:
                    sp.wait_ge(cmp_used, s - RAW + 1)
                w1 = (cmp_k_w1, cmp_v_w1)[s * 2 // CMP_STEPS][0].rearrange("(l p) n -> p l n", p=P)
                l = CMP_L * (s % (CMP_STEPS // 2))
                load(s % RAW, w1[:, l:l + CMP_L, :], (CMP_L, CMP_HIDDEN))
            for s in range(RAW):
                sp.wait_ge(cmp_used, CMP_STEPS - RAW + s + 1)
                load(s, wout_k[:, 2 * s:2 * s + 2, 0:CHUNK], (2, CHUNK))
            for s in range(RAW, STEPS_PER_CHUNK):
                sp.wait_ge(split_done, SP_OUT + s - RAW + 1)
                load(s % RAW, wout_k[:, 2 * s:2 * s + 2, 0:CHUNK], (2, CHUNK))
            with sp.Fori(1, W_CHUNKS) as c:
                chunk(wout_k, c, split_done, c * STEPS_PER_CHUNK + SP_OUT - RAW)
            sp.wait_ge(sem("x1_ready"), W_CHUNKS)
            sp.dma_start(x1_rows, X).then_inc(x1_stored, 16)
            sp.dma_start(SK, peer_sub_keys[0].rearrange("h s n d -> n (h s) d")).then_inc(sem("keys_loaded"), 16)
            with sp.Fori(0, W_CHUNKS) as c:
                chunk(wq_k, c, split_done, c * STEPS_PER_CHUNK + SP_QUERY - RAW)
            for s in range(RAW):
                sp.wait_ge(split_done, SP_U + s - RAW + 1)
                load(s, u_rows[s // 2, s % 2])
            with sp.Fori(1, NE_T // 2) as pair:
                i = pair * 2
                for s in range(RAW):
                    sp.wait_ge(u_turned, i * 2 + s - RAW + 1)
                    load(s, u_rows[bass.ds(i + s // 2, 1), s % 2].rearrange("a p d -> (a p) d"))
            for s in range(2):
                sp.wait_ge(u_turned, E_STEPS - RAW + s + 1)
                load(s, v_rows[0, s])
            sp.wait_ge(sem("gates_built"), BUILD_STEPS)
            for s in range(2):
                load(2 + s, v_rows[1, s])
            with sp.Fori(1, NE_T // 2) as pair:
                i = pair * 2
                for s in range(RAW):
                    sp.wait_ge(split_done, i * 2 + s - RAW + SP_V + 1)
                    load(s, v_rows[bass.ds(i + s // 2, 1), s % 2].rearrange("a p d -> (a p) d"))
            sp.wait_ge(x1_stored, 16)
            sp.wait_ge(sem("w_lo_done"), 16)
            sp.dma_start(X1, x1_rows).then_inc(sem("x1_loaded"), 16)
            for t in range(TT):
                sp.wait_ge(sem("out_ready"), t + 1)
                sp.dma_start(out_rows[:, t, :], X1[:, t, :]).then_inc(out_stored, 16)
            sp.wait_ge(out_stored, 16 * TT)

        @block.gpsimd
        def _(pool):
            made = sem("constants")
            pool.memset(ident[:], 0.0).then_inc(made, 1)
            pool.memset(neg_tri[:], -1.0).then_inc(made, 1)
            pool.memset(before[:], 1.0).then_inc(made, 1)
            pool.memset(neg_ones[:], -1.0).then_inc(made, 1)
            pool.memset(has_block, 1.0).then_inc(made, 1)
            pool.iota(iota[:], pattern=[[1, P]], base=0, channel_multiplier=0, allow_small_or_imprecise_dtypes=True).then_inc(made, 1)
            pool.memset(minus_half, -0.5).then_inc(made, 1)
            pool.wait_ge(made, 7)
            pool.affine_select(out=ident[:], in_=ident[:], compare_op=ALU.not_equal, fill=1.0, base=0,
                               pattern=[[-1, P]], channel_multiplier=1).then_inc(made, 1)
            pool.affine_select(out=neg_tri[:], in_=neg_tri[:], compare_op=ALU.is_ge, fill=0.0, base=0,
                               pattern=[[-1, P]], channel_multiplier=1).then_inc(made, 1)
            pool.affine_select(out=before[:], in_=before[:], compare_op=ALU.is_gt, fill=0.0, base=0,
                               pattern=[[1, P]], channel_multiplier=-1).then_inc(made, 1)
            pool.affine_select(out=has_block, in_=has_block, compare_op=ALU.is_ge, fill=0.0, base=1 - CMP_BLOCK,
                               pattern=[[0, 1]], channel_multiplier=1).then_inc(made, 1)
            def power(n, v):
                pool.wait_ge(sem("mean_square"), n)
                pool.tensor_tensor(v, v, minus_half[0:v.shape[0], 0:v.shape[1]], ALU.pow).then_inc(sem("inverse_rms"), 1)

            power(1, rstd[:, 0:TT])
            pool.wait_ge(sem("bias_rows"), 1)
            pool.dma_start(bias_dram[:, :, 0:BIAS_W], ROWB.unsqueeze(1).broadcast_to([NH, P, BIAS_W])).then_inc(sem("bias_stored"), 16)
            pool.wait_ge(sem("bias_stored"), 16)
            pool.dma_start(BIAS, bass.AP(tensor=bias_dram.tensor, offset=P, ap=[[BIAS_W, P], [P * (BIAS_W + 1), NH], [1, 384]])).then_inc(sem("bias_loaded"), 16)
            power(2, nrstd)
            pool.wait_ge(sem("sb_out"), 2)
            for v in range(2):
                pool.memset(PROJ[:, v, 0:CMP_BLOCK * 64], 0.0).then_inc(sem("blocks_cleared"), 1)
            power(3, krstd[0:NC])
            power(4, rstd[:, 0:2 * TT])
            power(5, rstd[:, 0:TT])

        @block.scalar
        def _(act):
            act_step = sem("act_step")
            steps = [0]

            def link(ins):
                steps[0] += 1
                ins.then_inc(act_step, 1)
                act.wait_ge(act_step, steps[0])

            def hi(slot, g, n, width):
                loaded(act, slot, g)
                act.wait_ge(split_free, n + 1)
                act.activation(split_hi[:, slot % SPLIT, 0:width], raw[:, slot, 0:width], ACT.Copy).then_inc(hi_done, 1)

            def loaded_at(slot, uses):
                act.wait_ge(raw_loaded[slot], 16 * uses)

            def hi_chunk(uses0, n0):
                for s in range(STEPS_PER_CHUNK):
                    loaded_at(s % RAW, uses0 + (s // RAW + 1))
                    act.wait_ge(split_free, n0 + s + 1)
                    act.activation(split_hi[:, s % SPLIT, :], raw[:, s % RAW, :], ACT.Copy).then_inc(hi_done, 1)

            def turned_hi(use, gain0):
                for k in range(KC):
                    if k % 2 == 0:
                        act.wait_ge(sem("rows_turned"), (KC // 2) * use + k // 2 + 1)
                    act.activation(ht[:, k, 0:T], psf[:, k * T:(k + 1) * T], ACT.Copy,
                                   scale=gain_cols[:, gain0 + k:gain0 + k + 1]).then_inc(sem("ht_hi"), 1)

            act.wait_ge(sem("gains_turned"), 1)
            link(act.activation(gain_cols[:], psf[:, 0:G_ALL], ACT.Copy))
            act.sem_inc(sem("gains_ready"), 1)
            turned_hi(0, G_NORM1)
            with act.Fori(0, W_IN_CHUNKS) as c:
                hi_chunk(c * 2 + RAW_IN // RAW, c * STEPS_PER_CHUNK + SP_IN)
            for s in range(TAIL_STEPS):
                hi(s, RAW_TAIL + s, SP_TAIL + s, TAIL_K * N_GATES)

            act.wait_ge(acc_free, 2 + CH_TAIL + 1)
            act.activation(gates.rearrange("p (t n) -> p t n", t=TT), PROJ[:, :, COL_GATE:IN_COLS], ACT.Exp, scale=-1.0).then_inc(sem("gate_exp"), 1)

            for b in range(2):
                act.wait_ge(sem("sb_turned"), b + 1)
                act.activation(QKT[:, :, 0:T], ps[:, 4:8, 0:T], ACT.Copy, scale=SCALE).then_inc(sem("sb_q"), 1)
                act.wait_ge(sem("sb_z"), b + 1)
                link(act.activation(T1, ps[:, 0:4, 0:384], ACT.Abs))
                link(act.activation(T1f, T1f, ACT.Exp, scale=-1.0))
                act.activation(T1f, T1f, ACT.Ln, bias=1.0).then_inc(sem("sb_ln"), 1)
                act.wait_ge(sem("sb_cumsum"), b + 1)
                act.activation(T1, ps[:, 0:4, 0:384], ACT.Exp).then_inc(sem("sb_exp"), 1)

            act.wait_ge(sem("q_turned"), 1)
            act.activation(QT.rearrange("p h n -> p (h n)"), psf[:, 0:2048], ACT.Copy, scale=gain_cols[:, G_Q:G_Q + 1]).then_inc(sem("q_ready"), 1)
            act.wait_ge(cmp_used, CMP_STEPS)
            act.activation(HG[0:64], ps[0:64, 0:2, 0:CMP_HIDDEN], ACT.Gelu_apprx_tanh).then_inc(sem("hidden"), 1)
            act.wait_ge(sem("hidden_turned"), 1)
            act.activation(HGT.rearrange("p w n -> p (w n)"), psf[:, 2 * 512:2 * 512 + 256], ACT.Copy).then_inc(sem("hidden_t"), 1)
            act.wait_ge(sem("cmp_shifted"), 1)
            act.activation(cmp_p, cmp_p, ACT.Exp).then_inc(sem("cmp_exp"), 1)
            act.wait_ge(sem("cmp_p_turned"), 1)
            act.activation(PCT[0:NC].rearrange("p b n -> p (b n)"), psf[0:NC, 0:2048], ACT.Copy).then_inc(sem("cmp_pt"), 1)
            for r in range(4):
                act.wait_ge(sem("ns_shifted"), r + 1)
                act.activation(T1f, T1f, ACT.Exp).then_inc(sem("ns_exp"), 1)
                act.wait_ge(sem("ns_p_turned"), r + 1)
                act.activation(T2f, psf[:, 4 * 512:7 * 512], ACT.Copy).then_inc(sem("ns_pt"), 1)

            turned_hi(1, G_MIX)
            with act.Fori(0, W_CHUNKS) as c:
                hi_chunk(c * 2 + RAW_OUT // RAW, c * STEPS_PER_CHUNK + SP_OUT)
            turned_hi(2, G_NORM2)
            with act.Fori(0, W_CHUNKS) as c:
                hi_chunk(c * 2 + RAW_QUERY // RAW, c * STEPS_PER_CHUNK + SP_QUERY)

            for b in range(2):
                act.wait_ge(sem("pq_turned"), b + 1)
                act.activation(PQT.rearrange("p w n -> p (w n)")[:, b * 2048:(b + 1) * 2048],
                               psf[:, b * 2048:(b + 1) * 2048], ACT.Copy).then_inc(sem("pq_ready"), 1)
            act.wait_ge(sem("keys_turned"), 1)
            act.activation(SKT.rearrange("p w n -> p (w n)"), psf[:, 0:2048], ACT.Copy).then_inc(sem("keys_ready"), 1)
            act.wait_ge(sem("best_shifted"), 1)
            act.activation(PICK[:, 2], PICK[:, 2], ACT.Exp).then_inc(sem("best_exp"), 1)

            with act.Fori(0, NE_T // 2) as pair:
                i = pair * 2
                for j in range(2):
                    for f in range(2):
                        act.wait_ge(u_turned, i * 2 + 2 * j + f + 1)
                        act.wait_ge(split_free, i * 2 + 2 * j + f + SP_U + 1)
                        act.activation(split_hi[:, f, :], psf[:, f * 1024:(f + 1) * 1024], ACT.Copy).then_inc(hi_done, 1)
                    act.wait_ge(sem("s_summed"), i + j + 3)
                    act.activation(WACT[:, bass.ds(i + j, 1), :].rearrange("p a c -> p (a c)"), s_sum[:, j, :],
                                   ACT.Gelu_apprx_tanh).then_inc(sem("acted"), 1)

            def v_tile(i, j):
                act.wait_ge(split_free, i * 2 + 2 * j + SP_V)
                if j == 0:
                    act.wait_ge(sem("gates_built"), BUILD_STEPS)
                act.activation(w_hi[:, j, :], WACT[:, bass.ds(i + j, 1), :].rearrange("p a c -> p (a c)"), ACT.Copy).then_inc(sem("w_hi_done"), 1)
                for f in range(2):
                    slot = 2 * j + f
                    act.wait_ge(raw_loaded[slot], i * 8 + 16 * (RAW_V // RAW + 1))
                    act.wait_ge(split_free, i * 2 + 2 * j + f + SP_V + 1)
                    act.activation(split_hi[:, f, :], raw[:, slot, :], ACT.Copy).then_inc(hi_done, 1)

            with act.Fori(0, NE_T // 2) as pair:
                i = pair * 2
                for j in range(2):
                    v_tile(i, j)

        @block.vector
        def _(dve):
            dve_step = sem("dve_step")
            steps = [0]

            def link(ins):
                steps[0] += 1
                ins.then_inc(dve_step, 1)
                dve.wait_ge(dve_step, steps[0])

            def flag(name, n=1):
                dve.sem_inc(sem(name), n)

            def lo(slot, n, width=STEP):
                dve.wait_ge(hi_done, n + 1)
                dve.tensor_tensor(split_lo[:, slot % SPLIT, 0:width], raw[:, slot, 0:width],
                                  split_hi[:, slot % SPLIT, 0:width].bitcast(F32), ALU.subtract).then_inc(split_done, 1)

            norms = [0]

            def inverse_rms(dst, sums, n):
                norms[0] += 1
                dve.tensor_scalar(dst, sums, 1.0 / n, EPS, ALU.mult, ALU.add).then_inc(sem("mean_square"), 1)
                dve.wait_ge(sem("inverse_rms"), norms[0])

            def normed_rows(src, parts):
                w = D // parts
                for t in range(TT):
                    for h in range(parts):
                        ins = dve.tensor_tensor_reduce(XN[:, t, h * w:(h + 1) * w], src[:, t, h * w:(h + 1) * w],
                                                       src[:, t, h * w:(h + 1) * w], 1.0, 0.0, ALU.mult, ALU.add,
                                                       ssq[:, t * parts + h:t * parts + h + 1])
                link(ins)
                inverse_rms(rstd[:, 0:TT * parts], ssq[:, 0:TT * parts], w)
                for t in range(TT):
                    for h in range(parts):
                        ins = dve.tensor_scalar(XN[:, t, h * w:(h + 1) * w], src[:, t, h * w:(h + 1) * w],
                                                rstd[:, t * parts + h:t * parts + h + 1], None, ALU.mult)
                ins.then_inc(sem("rows_normed"), 1)

            def turned_lo(use, gain0):
                for k in range(KC):
                    if k % 2 == 0:
                        dve.wait_ge(sem("ht_hi"), KC * use + k + 2)
                    dve.scalar_tensor_tensor(out=ht[:, k, T:2 * T], in0=psf[:, k * T:(k + 1) * T],
                                             scalar=gain_cols[:, gain0 + k:gain0 + k + 1],
                                             in1=ht[:, k, 0:T].bitcast(F32), op0=ALU.mult,
                                             op1=ALU.subtract).then_inc(sem("ht_lo"), 1)

            def bank_pair(parity, width):
                return ps[:, 2 * parity:2 * parity + 2, 0:width]

            def to_proj(c, parity, n_end):
                dve.wait_ge(split_free, n_end + 2)
                dve.tensor_copy(PROJ[:, :, bass.ds(c * CHUNK, CHUNK)], bank_pair(parity, CHUNK)).then_inc(acc_free, 1)

            dve.wait_ge(sem("x_loaded"), 16)
            normed_rows(X, 1)
            dve.memset(s_sum[:], 0.0).then_inc(acc_free, 2)
            dve.wait_ge(sem("bias_mm"), 1)
            link(dve.tensor_copy(ROWB[:, 0:T + 1], ps[0:NH, 7, 0:T + 1]))
            dve.memset(ROWB[:, T + 1:BIAS_W], NEG).then_inc(sem("bias_rows"), 1)
            turned_lo(0, G_NORM1)

            def in_chunk(c, parity, prev):
                for s in range(STEPS_PER_CHUNK):
                    lo(s % RAW, c * STEPS_PER_CHUNK + s + SP_IN)
                    if s == 1 and prev:
                        to_proj(c - 1, 1 - parity, c * STEPS_PER_CHUNK + SP_IN)

            in_chunk(0, 0, False)
            with dve.Fori(0, W_IN_CHUNKS // 2) as pair:
                c = pair * 2 + 1
                in_chunk(c, 1, True)
                in_chunk(c + 1, 0, True)
            for s in range(TAIL_STEPS):
                lo(s, SP_TAIL + s, TAIL_K * N_GATES)
                if s == 1:
                    to_proj(W_IN_CHUNKS - 1, (W_IN_CHUNKS - 1) % 2, SP_TAIL)
            dve.wait_ge(split_free, SP_OUT + 2)
            dve.tensor_copy(PROJ[:, :, COL_GATE:IN_COLS], bank_pair(CH_TAIL % 2, N_GATES)).then_inc(acc_free, 1)
            dve.wait_ge(acc_free, 2 + CH_TAIL + 1)

            q_rows = PROJ[:, :, COL_Q:COL_Q + NH * HD]
            for t in range(TT):
                dve.tensor_tensor(SQ[:, t * 1024:(t + 1) * 1024], q_rows[:, t, :], q_rows[:, t, :], ALU.mult)
            for b, col in enumerate((COL_KSLC, COL_KWIN)):
                k_rows = PROJ[:, :, col:col + NG * HD]
                ins = dve.tensor_tensor(SQK[:, b * 512:(b + 1) * 512].rearrange("p (t n) -> p t n", t=TT), k_rows, k_rows, ALU.mult)
            link(ins)
            link(dve.tensor_reduce(nssq, big[:, A_QT:A_QT + 3072].rearrange("p (h d) -> p h d", d=HD), AX_X, ALU.add))
            inverse_rms(nrstd, nssq, HD)
            for t in range(TT):
                v = q_rows[:, t, :].rearrange("p (h d) -> p h d", d=HD)
                dve.tensor_tensor(v, v, nrstd[:, t * NH:(t + 1) * NH].unsqueeze(2).broadcast_to([P, NH, HD]), ALU.mult)
            for b, col in enumerate((COL_KSLC, COL_KWIN)):
                for t in range(TT):
                    v = PROJ[:, t, col:col + NG * HD].rearrange("p (g d) -> p g d", d=HD)
                    o = 16 + b * 4 + t * NG
                    ins = dve.tensor_tensor(v, v, nrstd[:, o:o + NG].unsqueeze(2).broadcast_to([P, NG, HD]), ALU.mult)
            ins.then_inc(sem("nsa_normed"), 1)
            dve.wait_ge(sem("gate_exp"), 1)
            link(dve.tensor_scalar(gates, gates, 1.0, None, ALU.add))
            link(dve.reciprocal(gates, gates))
            gate = gates.rearrange("p (t h r) -> p t h r", t=TT, r=3)

            dve.wait_ge(sem("constants"), 11)

            def diagonal(v):
                f = v.rearrange("p h (b n) -> p h b n", n=P)
                return [f[:, :, b, :] for b in (0, 2)]

            mask4 = before[:, :].unsqueeze(1).broadcast_to([P, 4, P])
            for b in range(2):
                dve.wait_ge(sem("sb_q"), b + 1)
                dve.tensor_copy(QKT[:, :, T:2 * T], ps[:, 4:8, T:2 * T]).then_inc(sem("sb_k"), 1)
                dve.wait_ge(sem("sb_ln"), b + 1)
                link(dve.scalar_tensor_tensor(out=T2, in0=ps[:, 0:4, 0:384], scalar=0.0, in1=T1, op0=ALU.max, op1=ALU.add))
                for v in diagonal(T2):
                    dve.tensor_tensor(v, v, mask4, ALU.mult).then_inc(sem("sb_softplus"), 1)
                dve.wait_ge(sem("sb_exp"), b + 1)
                for v in diagonal(T1):
                    dve.scalar_tensor_tensor(out=v, in0=v, scalar=1.0, in1=mask4, op0=ALU.min, op1=ALU.mult).then_inc(sem("sb_a"), 1)
                dve.wait_ge(sem("sb_pv"), b + 1)
                dve.tensor_copy(MIX[:, :, b * 512:(b + 1) * 512].rearrange("p t (h d) -> p h t d", h=4),
                                ps[:, 4:6, :].rearrange("p b (h t d) -> p (b h) t d", h=2, t=TT)).then_inc(sem("sb_out"), 1)

            dve.wait_ge(sem("k_turned"), 1)
            dve.tensor_scalar(KT.rearrange("p b g n -> p (b g n)"), psf[:, 4 * 512:6 * 512], gain_cols[:, G_K:G_K + 1], SCALE, ALU.mult, ALU.mult).then_inc(sem("k_ready"), 1)
            link(dve.tensor_copy(KVC.rearrange("p b g n -> p (b g n)"), psf[:, 6 * 512:8 * 512]))
            dve.wait_ge(sem("blocks_cleared"), 2)
            pe = gain_cols[:, G_PE:G_ALL].unsqueeze(2).broadcast_to([P, CMP_BLOCK, NC])
            for v in range(2):
                for g in range(NG):
                    src = KVC[:, v, g, :]
                    windows = bass.AP(tensor=src.tensor, offset=src.offset, ap=[list(src.ap[0]), [1, CMP_BLOCK], [CMP_STRIDE, NC]])
                    dve.tensor_tensor(BLK[:, v, :, 32 * g:32 * g + NC], windows, pe, ALU.add).then_inc(sem("blocks_ready"), 1)
            dve.wait_ge(sem("cmp_kv"), 1)
            link(dve.tensor_copy(KCV[0:NC].rearrange("p v g n -> p (v g n)"), ps[0:NC, 3, :]))
            link(dve.tensor_tensor(KSQ[0:NC], KCV[0:NC, 0], KCV[0:NC, 0], ALU.mult))
            link(dve.tensor_reduce(kssq[0:NC], KSQ[0:NC], AX_X, ALU.add))
            inverse_rms(krstd[0:NC], kssq[0:NC], HD)
            dve.tensor_tensor(KCV[0:NC, 0], KCV[0:NC, 0], krstd[0:NC].unsqueeze(2).broadcast_to([NC, NG, HD]), ALU.mult).then_inc(sem("kc_ready"), 1)
            dve.wait_ge(sem("kc_turned"), 1)
            dve.tensor_scalar(KCT.rearrange("p g n -> p (g n)"), ps[:, 2, 256:288], gain_cols[:, G_K:G_K + 1], SCALE, ALU.mult, ALU.mult).then_inc(sem("kct_ready"), 1)

            dve.wait_ge(sem("cmp_s"), 1)
            dve.wait_ge(sem("bias_loaded"), 16)
            cp = cmp_p.rearrange("p (h t c) -> p h t c", h=NH, t=TT)
            sc = ps[:, 4, 0:256].rearrange("p (h t c) -> p h t c", h=NH, t=TT)
            for t in range(TT):
                start = CMP_BLOCK - 1 + P * (TT - 1 - t)
                ins = dve.tensor_tensor(cp[:, :, t, :], sc[:, :, t, 0:NC],
                                        BIAS[:, :, start:start + CMP_STRIDE * (NC - 1) + 1:CMP_STRIDE], ALU.add)
            link(ins)
            cpr = cmp_p.rearrange("p (b c) -> p b c", c=NC)
            link(dve.tensor_reduce(row_max, cpr, AX_X, ALU.max))
            dve.tensor_tensor(cpr, cpr, row_max.unsqueeze(2).broadcast_to([P, 16, NC]), ALU.subtract).then_inc(sem("cmp_shifted"), 1)
            dve.wait_ge(sem("cmp_exp"), 1)
            link(dve.tensor_reduce(row_sum, cpr, AX_X, ALU.add))
            link(dve.reciprocal(row_sum, row_sum))
            rs = row_sum.rearrange("p (h t) -> p h t", t=TT)
            cf = coef.rearrange("p (h t) -> p h t", t=TT)
            link(dve.tensor_tensor(cf, rs, gate[:, :, :, 0].rearrange("p t h -> p h t"), ALU.mult))
            link(dve.tensor_scalar(cf[:, :, 0], cf[:, :, 0], has_block, None, ALU.mult))
            dve.wait_ge(sem("cmp_pv"), 1)
            nsa = MIX[:, :, 1024:2048]
            link(dve.tensor_tensor(nsa.rearrange("p t (h d) -> p h t d", h=NH),
                                   psf[:, 2048:4096].rearrange("p (h t d) -> p h t d", h=NH, t=TT),
                                   cf.unsqueeze(3).broadcast_to([P, NH, TT, HD]), ALU.mult))
            flag("cmp_out")

            for r in range(4):
                branch, b = divmod(r, 2)
                dve.wait_ge(sem("ns_s"), r + 1)
                dve.tensor_tensor(T1[:, :, 0:P], ps[:, 0:4, 0:P], BIAS[:, 4 * b:4 * b + 4, P:2 * P], ALU.add)
                link(dve.tensor_tensor(T1[:, :, P:3 * P], ps[:, 0:4, P:3 * P], BIAS[:, 4 * b:4 * b + 4, 0:2 * P], ALU.add))
                m = row_max[:, 0:8].rearrange("p (t h) -> p t h", t=TT)
                s4 = row_sum[:, 0:8].rearrange("p (t h) -> p t h", t=TT)
                dve.tensor_reduce(m[:, 0, :], T1[:, :, 0:P], AX_X, ALU.max)
                link(dve.tensor_reduce(m[:, 1, :], T1[:, :, P:3 * P], AX_X, ALU.max))
                dve.tensor_tensor(T1[:, :, 0:P], T1[:, :, 0:P], m[:, 0, :].unsqueeze(2).broadcast_to([P, 4, P]), ALU.subtract)
                dve.tensor_tensor(T1[:, :, P:3 * P], T1[:, :, P:3 * P], m[:, 1, :].unsqueeze(2).broadcast_to([P, 4, 2 * P]), ALU.subtract).then_inc(sem("ns_shifted"), 1)
                dve.wait_ge(sem("ns_exp"), r + 1)
                dve.tensor_reduce(s4[:, 0, :], T1[:, :, 0:P], AX_X, ALU.add)
                link(dve.tensor_reduce(s4[:, 1, :], T1[:, :, P:3 * P], AX_X, ALU.add))
                link(dve.reciprocal(row_sum[:, 0:8], row_sum[:, 0:8]))
                cf4 = coef[:, 0:8].rearrange("p (t h) -> p t h", t=TT)
                link(dve.tensor_tensor(cf4, s4, gate[:, :, 4 * b:4 * b + 4, 1 + branch], ALU.mult))
                dve.wait_ge(sem("ns_pv"), r + 1)
                link(dve.tensor_tensor(TMP.rearrange("p (h t d) -> p h t d", h=4, t=TT),
                                       psf[:, 3072:4096].rearrange("p (h t d) -> p h t d", h=4, t=TT),
                                       cf4.rearrange("p t h -> p h t").unsqueeze(3).broadcast_to([P, 4, TT, HD]), ALU.mult))
                flag("ns_out")
                v = nsa[:, :, b * 512:(b + 1) * 512].rearrange("p t (h d) -> p h t d", h=4)
                link(dve.tensor_tensor(v, v, TMP.rearrange("p (h t d) -> p h t d", h=4, t=TT), ALU.add))

            normed_rows(MIX, 2)
            turned_lo(1, G_MIX)

            def to_x1(c):
                dve.wait_ge(split_free, SP_OUT + (c + 1) * STEPS_PER_CHUNK + 2)
                v = X[:, :, c * CHUNK:(c + 1) * CHUNK]
                dve.tensor_tensor(v, v, bank_pair((CH_OUT + c) % 2, CHUNK), ALU.add).then_inc(sem("x1_ready"), 1)
                dve.sem_inc(acc_free, 1)

            for c in range(W_CHUNKS):
                for s in range(STEPS_PER_CHUNK):
                    lo(s % RAW, SP_OUT + c * STEPS_PER_CHUNK + s)
                    if s == 1 and c:
                        to_x1(c - 1)
            to_x1(W_CHUNKS - 1)
            dve.wait_ge(sem("x1_ready"), W_CHUNKS)
            normed_rows(X, 1)
            turned_lo(2, G_NORM2)

            def to_q(c):
                dve.wait_ge(split_free, SP_QUERY + (c + 1) * STEPS_PER_CHUNK + 2)
                dve.tensor_copy(Q[:, :, c * CHUNK:(c + 1) * CHUNK], bank_pair((CH_QUERY + c) % 2, CHUNK)).then_inc(acc_free, 1)

            for c in range(W_CHUNKS):
                for s in range(STEPS_PER_CHUNK):
                    lo(s % RAW, SP_QUERY + c * STEPS_PER_CHUNK + s)
                    if s == 1 and c:
                        to_q(c - 1)
            to_q(W_CHUNKS - 1)

            dve.wait_ge(sem("scores"), 1)
            link(dve.tensor_copy(S.rearrange("p t w n -> p (t w n)"), psf[:, :]))
            flag("scores_read")
            pairs = [(t, w) for t in range(TT) for w in range(HP)]
            for r in range(2):
                k = slice(8 * r, 8 * r + 8)
                for t, w in pairs:
                    ins = dve.max(TOPS[:, t, w, k], S[:, t, w, :])
                link(ins)
                for t, w in pairs:
                    ins = dve.max_index(TOPI[:, t, w, k], TOPS[:, t, w, k], S[:, t, w, :])
                link(ins)
                if r == 0:
                    for t, w in pairs:
                        ins = dve.match_replace(S[:, t, w, :], TOPS[:, t, w, k], S[:, t, w, :], -3.0e38)
                    link(ins)
            link(dve.tensor_copy(TOPF.rearrange("p t w k -> p (t w k)"), TOPI.rearrange("p t w k -> p (t w k)")))
            for t in range(TT):
                tops = TOPS[:, t].rearrange("p (h s) k -> p h s k", s=2)
                ins = dve.tensor_tensor(CAND[:, t].rearrange("p h (a b) -> p h a b", a=TOPK),
                                        tops[:, :, 0, :].unsqueeze(3).broadcast_to([P, NH, TOPK, TOPK]),
                                        tops[:, :, 1, :].unsqueeze(2).broadcast_to([P, NH, TOPK, TOPK]), ALU.add)
            link(ins)
            pairs = [(t, h) for t in range(TT) for h in range(NH)]
            for r in range(2):
                k = slice(8 * r, 8 * r + 8)
                for t, h in pairs:
                    ins = dve.max(BEST[:, t, h, k], CAND[:, t, h, :])
                link(ins)
                for t, h in pairs:
                    ins = dve.max_index(POS[:, t, h, k], BEST[:, t, h, k], CAND[:, t, h, :])
                link(ins)
                if r == 0:
                    for t, h in pairs:
                        ins = dve.match_replace(CAND[:, t, h, :], BEST[:, t, h, k], CAND[:, t, h, :], -3.0e38)
                    link(ins)
            best = BEST.rearrange("p t h k -> p (t h) k")
            pick_g = PICK[:, 2].rearrange("p t h k -> p (t h) k")
            dve.tensor_tensor(pick_g, best, best[:, :, 0:1].broadcast_to([P, 16, TOPK]), ALU.subtract).then_inc(sem("best_shifted"), 1)
            pos = POS.rearrange("p t h k -> p (t h k)")
            dve.tensor_scalar(POSAB[:, 0, :], pos, 4, None, ALU.logical_shift_right)
            link(dve.tensor_scalar(POSAB[:, 1, :], pos, 15, None, ALU.bitwise_and))
            link(dve.tensor_copy(POSF.rearrange("p s t h k -> p (s t h k)"), POSAB.rearrange("p s n -> p (s n)")))
            for t in range(TT):
                topf = TOPF[:, t].rearrange("p (h s) k -> p h s k", s=2)
                for s in range(2):
                    link(dve.tensor_tensor(EQ, POSF[:, s, t].unsqueeze(3).broadcast_to([P, NH, TOPK, TOPK]),
                                           iota[:, 0:TOPK].unsqueeze(1).unsqueeze(1).broadcast_to([P, NH, TOPK, TOPK]), ALU.is_equal))
                    link(dve.tensor_tensor(EQ, EQ, topf[:, :, s, :].unsqueeze(2).broadcast_to([P, NH, TOPK, TOPK]), ALU.mult))
                    link(dve.tensor_reduce(PICK[:, s, t], EQ, AX_X, ALU.add))
            dve.wait_ge(sem("best_exp"), 1)
            gsum = GSUM.rearrange("p t h -> p (t h)")
            link(dve.tensor_reduce(gsum, pick_g, AX_X, ALU.add))
            link(dve.reciprocal(gsum, gsum))
            link(dve.tensor_tensor(pick_g, pick_g, gsum.unsqueeze(2).broadcast_to([P, 16, TOPK]), ALU.mult))
            flag("picks")
            dve.wait_ge(sem("picks_turned"), 1)
            for s in range(3):
                dve.tensor_copy(picked[:, s, :], ps[:, 4 + s, 0:T]).then_inc(sem("picked_ready"), 1)

            with dve.Fori(0, NE_T // 2) as pair:
                i = pair * 2
                for j in range(2):
                    for f in range(2):
                        dve.wait_ge(hi_done, i * 2 + 2 * j + f + SP_U + 1)
                        dve.tensor_tensor(split_lo[:, f, :], psf[:, f * 1024:(f + 1) * 1024],
                                          split_hi[:, f, :].bitcast(F32), ALU.subtract).then_inc(split_done, 1)
                    dve.wait_ge(split_free, i * 2 + 2 * j + 2 + SP_U + 2)
                    dve.wait_ge(sem("acted"), i + j + 1)
                    dve.tensor_copy(s_sum[:, j, :], ps[:, 4 + j, 0:T]).then_inc(sem("s_copied"), 1)
                    dve.wait_ge(sem("s_copied"), i + j + 1)
                    dve.tensor_tensor(s_sum[:, j, :], s_sum[:, j, :], ps[:, 4 + j, T:2 * T], ALU.add).then_inc(sem("s_summed"), 1)

            def one_i(s, j):
                dve.wait_ge(sem("onehot_free"), s + j + 1)
                for c in range(TOKENS_PER_BANK):
                    col = (s + j) * TOKENS_PER_BANK + c
                    ins = dve.tensor_scalar(ONE_I[:, j, c * P:(c + 1) * P], iota[:, :], picked[:, 0, bass.ds(col, 1)],
                                            picked[:, 2, bass.ds(col, 1)], ALU.is_equal, ALU.mult)
                ins.then_inc(sem("onehot_i"), 1)
                cols = picked[:, 1, bass.ds((s + j) * TOKENS_PER_BANK, TOKENS_PER_BANK)]
                dve.tensor_tensor(ONE_J[:, j, :].rearrange("p (c n) -> p c n", c=TOKENS_PER_BANK),
                                  iota[:, :].unsqueeze(1).broadcast_to([P, TOKENS_PER_BANK, P]),
                                  cols.unsqueeze(2).broadcast_to([P, TOKENS_PER_BANK, P]),
                                  ALU.is_equal).then_inc(sem("onehot_j"), 1)

            def apply_gates(s, j):
                dve.wait_ge(sem("gates_mm"), s + j + 1)
                v = WACT_C[:, bass.ds((s + j) * TOKENS_PER_BANK, TOKENS_PER_BANK), :]
                dve.tensor_tensor(v, v, ps[:, 6 + j, :].rearrange("p (c i) -> p c i", c=TOKENS_PER_BANK), ALU.mult).then_inc(sem("gates_built"), 1)

            dve.wait_ge(sem("acted"), NE_T + 2)
            with dve.Fori(0, BUILD_STEPS // 2) as pair:
                s = pair * 2
                one_i(s, 0)
                one_i(s, 1)
                apply_gates(s, 0)
                apply_gates(s, 1)

            with dve.Fori(0, NE_T // 2) as pair:
                i = pair * 2
                for j in range(2):
                    dve.wait_ge(sem("w_hi_done"), i + j + 1)
                    dve.tensor_tensor(w_lo[:, j, :], WACT[:, bass.ds(i + j, 1), :].rearrange("p a c -> p (a c)"),
                                      w_hi[:, j, :].bitcast(F32), ALU.subtract).then_inc(sem("w_lo_done"), 1)
                    for f in range(2):
                        dve.wait_ge(hi_done, i * 2 + 2 * j + f + SP_V + 1)
                        dve.tensor_tensor(split_lo[:, f, :], raw[:, 2 * j + f, :],
                                          split_hi[:, f, :].bitcast(F32), ALU.subtract).then_inc(split_done, 1)
            dve.wait_ge(sem("x1_loaded"), 16)
            dve.wait_ge(split_free, SP_V + E_STEPS + 2)
            for t in range(TT):
                dve.tensor_tensor(X1[:, t, :], X1[:, t, :], psf[:, t * D:(t + 1) * D], ALU.add).then_inc(sem("out_ready"), 1)

        @block.tensor
        def _(pe):
            def turn_rows(use):
                pe.wait_ge(sem("rows_normed"), use + 1)
                for k in range(KC):
                    for t in range(TT):
                        ins = pe.transpose(psf[:, k * T + t * P:k * T + (t + 1) * P], XN[:, t, k * P:(k + 1) * P], ident[:, :])
                    if k % 2:
                        ins.then_inc(sem("rows_turned"), 1)

            def gemm_step(acc, slot, ks, width, n, last):
                pe.wait_ge(split_done, n + 1)
                for j, k in enumerate(ks):
                    w_h = split_hi[:, slot, j * width:(j + 1) * width]
                    w_l = split_lo[:, slot, j * width:(j + 1) * width]
                    for t in range(TT):
                        h_h = ht[:, k, t * P:(t + 1) * P]
                        h_l = ht[:, k, T + t * P:T + (t + 1) * P]
                        pe.matmul(acc[t], h_h, w_h, start=k == 0, stop=False)
                        pe.matmul(acc[t], h_h, w_l, start=False, stop=False)
                        ins = pe.matmul(acc[t], h_l, w_h, start=False, stop=k == KC - 1)
                ins.then_inc(split_free, 1)

            def gemm_chunk(ch, parity, n0):
                pe.wait_ge(acc_free, ch + 1)
                acc = [ps[:, 2 * parity + t, :] for t in range(TT)]
                for s in range(STEPS_PER_CHUNK):
                    gemm_step(acc, s % SPLIT, (2 * s, 2 * s + 1), CHUNK, n0 + s, s == STEPS_PER_CHUNK - 1)

            pe.sem_inc(split_free, 2)
            pe.wait_ge(sem("constants"), 11)
            pe.wait_ge(sem("gains_loaded"), 16 * 7)
            pe.transpose(psf[:, 0:G_ALL], gain_rows[0:G_ALL, :], ident[0:G_ALL, 0:G_ALL]).then_inc(sem("gains_turned"), 1)
            pe.wait_ge(sem("table_loaded"), 32)
            pe.matmul(ps[0:NH, 7, :], TABLE, ONEHOT, start=True, stop=True).then_inc(sem("bias_mm"), 1)
            pe.wait_ge(sem("gains_ready"), 1)
            pe.wait_ge(sem("bias_rows"), 1)
            turn_rows(0)
            pe.wait_ge(sem("ht_lo"), KC)
            with pe.Fori(0, W_IN_CHUNKS // 2) as pair:
                c = pair * 2
                gemm_chunk(c, 0, c * STEPS_PER_CHUNK + SP_IN)
                gemm_chunk(c + 1, 1, c * STEPS_PER_CHUNK + STEPS_PER_CHUNK + SP_IN)
            gemm_chunk(W_IN_CHUNKS - 1, 0, SP_TAIL - STEPS_PER_CHUNK)
            pe.wait_ge(acc_free, CH_TAIL + 1)
            for s in range(TAIL_STEPS):
                gemm_step([ps[:, 2 + t, 0:N_GATES] for t in range(TT)], s % SPLIT,
                          range(TAIL_K * s, TAIL_K * (s + 1)), N_GATES, SP_TAIL + s, s == TAIL_STEPS - 1)

            pe.wait_ge(acc_free, 2 + CH_TAIL + 1)
            for b in range(2):
                if b:
                    pe.wait_ge(sem("sb_out"), b)
                for h in range(4):
                    for s, col in enumerate((COL_QSB, COL_KSB)):
                        for t in range(TT):
                            c = col + (4 * b + h) * HD
                            ins = pe.transpose(ps[:, 4 + h, s * T + t * P:s * T + (t + 1) * P], PROJ[:, t, c:c + HD], ident[:, :])
                ins.then_inc(sem("sb_turned"), 1)
                pe.wait_ge(sem("sb_q"), b + 1)
                pe.wait_ge(sem("sb_k"), b + 1)
                for h in range(4):
                    pe.matmul(ps[:, h, 0:T], QKT[:, h, T:T + P], QKT[:, h, 0:T], start=True, stop=False, skip_group_check=True)
                    ins = pe.matmul(ps[:, h, T:T + P], QKT[:, h, T + P:2 * T], QKT[:, h, P:T], start=False, stop=False, skip_group_check=True)
                ins.then_inc(sem("sb_z"), 1)
                pe.wait_ge(sem("sb_softplus"), 2 * b + 2)
                for h in range(4):
                    pe.matmul(ps[:, h, 0:T], neg_tri[:, :], T2[:, h, 0:T], start=False, stop=False, skip_group_check=True)
                    pe.matmul(ps[:, h, P:T], neg_ones[:, :], T2[:, h, T:T + P], start=False, stop=False, skip_group_check=True)
                    ins = pe.matmul(ps[:, h, T:T + P], neg_tri[:, :], T2[:, h, T:T + P], start=False, stop=True, skip_group_check=True)
                ins.then_inc(sem("sb_cumsum"), 1)
                pe.wait_ge(sem("sb_a"), 2 * b + 2)
                for h in range(4):
                    c = COL_VSB + (4 * b + h) * HD
                    o = ps[:, 4 + h // 2, (h % 2) * T:(h % 2 + 1) * T]
                    pe.matmul(o[:, 0:P], T1[:, h, 0:P], PROJ[:, 0, c:c + HD], start=True, stop=True)
                    pe.matmul(o[:, P:T], T1[:, h, P:T], PROJ[:, 0, c:c + HD], start=True, stop=False)
                    ins = pe.matmul(o[:, P:T], T1[:, h, T:T + P], PROJ[:, 1, c:c + HD], start=False, stop=True)
                ins.then_inc(sem("sb_pv"), 1)

            pe.wait_ge(sem("nsa_normed"), 1)
            pe.wait_ge(sem("sb_out"), 2)
            for h in range(NH):
                for t in range(TT):
                    c = COL_Q + h * HD
                    ins = pe.transpose(psf[:, h * T + t * P:h * T + (t + 1) * P], PROJ[:, t, c:c + HD], ident[:, :])
            ins.then_inc(sem("q_turned"), 1)
            for b, col in enumerate((COL_KSLC, COL_KWIN, COL_KCMP, COL_VCMP)):
                for g in range(NG):
                    for t in range(TT):
                        c = col + g * HD
                        ins = pe.transpose(ps[:, 4 + b, g * T + t * P:g * T + (t + 1) * P], PROJ[:, t, c:c + HD], ident[:, :])
            ins.then_inc(sem("k_turned"), 1)
            pe.wait_ge(sem("q_ready"), 1)
            pe.wait_ge(sem("blocks_ready"), 4)
            for s in range(CMP_STEPS):
                v = 2 * s // CMP_STEPS
                loaded(pe, s % RAW, RAW_CMP + s)
                for j in range(CMP_L):
                    l = CMP_L * (s % (CMP_STEPS // 2)) + j
                    ins = pe.matmul(ps[0:64, v, 0:CMP_HIDDEN], BLK[:, v, l, :], raw[:, s % RAW, j * CMP_HIDDEN:(j + 1) * CMP_HIDDEN],
                                    start=l == 0, stop=l == CMP_BLOCK - 1)
                ins.then_inc(cmp_used, 1)
            pe.wait_ge(sem("hidden"), 1)
            for v in range(2):
                for f in range(2):
                    ins = pe.transpose(ps[:, 2, (2 * v + f) * 64:(2 * v + f + 1) * 64], HG[0:64, v, f * P:(f + 1) * P], ident[0:64, 0:64])
            ins.then_inc(sem("hidden_turned"), 1)
            pe.wait_ge(sem("hidden_t"), 1)
            pe.wait_ge(sem("w2_loaded"), 32)
            for v in range(2):
                for g in range(NG):
                    for f in range(2):
                        ins = pe.matmul(ps[0:NC, 3, (v * NG + g) * HD:(v * NG + g + 1) * HD], HGT[:, 2 * v + f, 32 * g:32 * g + NC],
                                        W2S[:, 2 * v + f, :], start=f == 0, stop=f == 1)
            ins.then_inc(sem("cmp_kv"), 1)
            pe.wait_ge(sem("kc_ready"), 1)
            for g in range(NG):
                ins = pe.transpose(ps[:, 2, 256 + 16 * g:256 + 16 * g + NC], KCV[0:NC, 0, g, :], ident[0:NC, 0:NC])
            ins.then_inc(sem("kc_turned"), 1)
            pe.wait_ge(sem("kct_ready"), 1)
            for h in range(NH):
                for t in range(TT):
                    o = (h * TT + t) * 16
                    ins = pe.matmul(ps[:, 4, o:o + NC], QT[:, h, t * P:(t + 1) * P], KCT[:, h // GROUP, 0:NC], start=True, stop=True)
            ins.then_inc(sem("cmp_s"), 1)
            pe.wait_ge(sem("cmp_exp"), 1)
            for b in range(16):
                ins = pe.transpose(psf[0:NC, b * P:(b + 1) * P], cmp_p[:, b * NC:(b + 1) * NC], ident[:, :])
            ins.then_inc(sem("cmp_p_turned"), 1)
            pe.wait_ge(sem("cmp_pt"), 1)
            for b in range(16):
                ins = pe.matmul(psf[:, 2048 + b * P:2048 + (b + 1) * P], PCT[0:NC, b, :], KCV[0:NC, 1, b // TT // GROUP, :], start=True, stop=True)
            ins.then_inc(sem("cmp_pv"), 1)

            pe.wait_ge(sem("cmp_out"), 1)
            pe.wait_ge(sem("k_ready"), 1)
            for r in range(4):
                branch, b = divmod(r, 2)
                v_col = (COL_VSLC, COL_VWIN)[branch] + b * HD
                for h in range(4):
                    pe.matmul(ps[:, h, 0:P], QT[:, 4 * b + h, 0:P], KT[:, branch, b, 0:P], start=True, stop=True)
                    ins = pe.matmul(ps[:, h, P:3 * P], QT[:, 4 * b + h, P:T], KT[:, branch, b, :], start=True, stop=True)
                ins.then_inc(sem("ns_s"), 1)
                pe.wait_ge(sem("ns_exp"), r + 1)
                if r:
                    pe.wait_ge(sem("ns_out"), r)
                for j in range(12):
                    ins = pe.transpose(ps[:, 4 + j // 4, (j % 4) * P:(j % 4 + 1) * P], T1[:, j // 3, (j % 3) * P:(j % 3 + 1) * P], ident[:, :])
                ins.then_inc(sem("ns_p_turned"), 1)
                pe.wait_ge(sem("ns_pt"), r + 1)
                for h in range(4):
                    o = 3072 + h * T
                    pe.matmul(psf[:, o:o + P], T2b[:, 3 * h, :], PROJ[:, 0, v_col:v_col + HD], start=True, stop=True)
                    pe.matmul(psf[:, o + P:o + T], T2b[:, 3 * h + 1, :], PROJ[:, 0, v_col:v_col + HD], start=True, stop=False)
                    ins = pe.matmul(psf[:, o + P:o + T], T2b[:, 3 * h + 2, :], PROJ[:, 1, v_col:v_col + HD], start=False, stop=True)
                ins.then_inc(sem("ns_pv"), 1)

            turn_rows(1)
            pe.wait_ge(sem("ht_lo"), 2 * KC)
            with pe.Fori(0, W_CHUNKS // 2) as pair:
                c = pair * 2
                gemm_chunk(c + CH_OUT, CH_OUT % 2, c * STEPS_PER_CHUNK + SP_OUT)
                gemm_chunk(c + CH_OUT + 1, 1 - CH_OUT % 2, c * STEPS_PER_CHUNK + STEPS_PER_CHUNK + SP_OUT)
            turn_rows(2)
            pe.wait_ge(sem("ht_lo"), 3 * KC)
            with pe.Fori(0, W_CHUNKS // 2) as pair:
                c = pair * 2
                gemm_chunk(c + CH_QUERY, CH_QUERY % 2, c * STEPS_PER_CHUNK + SP_QUERY)
                gemm_chunk(c + CH_QUERY + 1, 1 - CH_QUERY % 2, c * STEPS_PER_CHUNK + STEPS_PER_CHUNK + SP_QUERY)

            pe.wait_ge(acc_free, 2 + CH_QUERY + W_CHUNKS)
            for w in range(HP):
                for t in range(TT):
                    ins = pe.transpose(psf[:, w * T + t * P:w * T + (t + 1) * P], Q[:, t, w * P:(w + 1) * P], ident[:, :])
                if w % 8 == 7:
                    ins.then_inc(sem("pq_turned"), 1)
            pe.wait_ge(sem("keys_loaded"), 16)
            pe.wait_ge(sem("pq_ready"), 1)
            for w in range(HP):
                ins = pe.transpose(psf[:, w * P:(w + 1) * P], SK[:, w, :], ident[:, :])
            ins.then_inc(sem("keys_turned"), 1)
            pe.wait_ge(sem("keys_ready"), 1)
            pe.wait_ge(sem("pq_ready"), 2)
            for t in range(TT):
                for w in range(HP):
                    o = (t * HP + w) * P
                    ins = pe.matmul(psf[:, o:o + P], PQT[:, w, t * P:(t + 1) * P], SKT[:, w, :], start=True, stop=True)
            ins.then_inc(sem("scores"), 1)
            pe.wait_ge(sem("scores_read"), 1)
            pe.wait_ge(sem("picks"), 1)
            for s in range(3):
                for t in range(TT):
                    ins = pe.transpose(ps[:, 4 + s, t * P:(t + 1) * P], PICK[:, s, t].rearrange("p h k -> p (h k)"), ident[:, :])
            ins.then_inc(sem("picks_turned"), 1)
            pe.wait_ge(sem("picked_ready"), 3)

            pe.sem_inc(sem("s_summed"), 2)
            pe.sem_inc(sem("acted"), 2)

            def turn_u(slot, f, uses, n):
                pe.wait_ge(raw_loaded[slot], uses)
                pe.wait_ge(split_done, n - 1)
                for k in range(8):
                    ins = pe.transpose(psf[:, f * 1024 + k * P:f * 1024 + (k + 1) * P], raw[:, slot, k * P:(k + 1) * P], ident[:, :])
                ins.then_inc(u_turned, 1)

            def u_product(j, f, n):
                pe.wait_ge(split_done, n + 1)
                for k in range(8):
                    kk = 8 * f + k
                    pe.matmul(ps[:, 4 + j, :], split_hi[:, f, k * P:(k + 1) * P], ht[:, kk, :], start=kk == 0, stop=False, skip_group_check=True)
                    ins = pe.matmul(ps[:, 4 + j, T:2 * T], split_lo[:, f, k * P:(k + 1) * P], ht[:, kk, 0:T], start=False, stop=kk == KC - 1, skip_group_check=True)
                ins.then_inc(split_free, 1)

            turn_u(0, 0, 16 * (RAW_U // RAW + 1), SP_U)

            def u_tile(i, j, more):
                turn_u(2 * j + 1, 1, i * 8 + 16 * (RAW_U // RAW + 1), i * 2 + 2 * j + 1 + SP_U)
                pe.wait_ge(sem("s_summed"), i + j + 1)
                u_product(j, 0, i * 2 + 2 * j + SP_U)
                if more:
                    turn_u(2 - 2 * j, 0, i * 8 + 16 * (RAW_U // RAW + 1 + j), i * 2 + 2 * j + 2 + SP_U)
                u_product(j, 1, i * 2 + 2 * j + 1 + SP_U)

            with pe.Fori(0, NE_T // 2 - 1) as pair:
                i = pair * 2
                u_tile(i, 0, True)
                u_tile(i, 1, True)
            u_tile(NE_T - 2, 0, True)
            u_tile(NE_T - 2, 1, False)

            pe.sem_inc(sem("onehot_free"), 2)
            with pe.Fori(0, BUILD_STEPS // 2) as pair:
                s = pair * 2
                for j in range(2):
                    pe.wait_ge(sem("onehot_i"), s + j + 1)
                    pe.wait_ge(sem("onehot_j"), s + j + 1)
                    for c in range(TOKENS_PER_BANK):
                        ins = pe.matmul(ps[:, 6 + j, c * P:(c + 1) * P], ONE_J[:, j, c * P:(c + 1) * P], ONE_I[:, j, c * P:(c + 1) * P], start=True, stop=True)
                    ins.then_inc(sem("gates_mm"), 1)
                    pe.sem_inc(sem("onehot_free"), 1)

            pe.wait_ge(sem("gates_built"), BUILD_STEPS)

            def v_tile(i, j, first, last):
                pe.wait_ge(sem("w_lo_done"), i + j + 1)
                for f in range(2):
                    pe.wait_ge(split_done, i * 2 + 2 * j + f + SP_V + 1)
                    for t in range(TT):
                        g_h = w_hi[:, j, t * P:(t + 1) * P]
                        g_l = w_lo[:, j, t * P:(t + 1) * P]
                        for c in range(2):
                            acc = ps[:, 4 * t + 2 * f + c, :]
                            v_h = split_hi[:, f, c * 512:(c + 1) * 512]
                            v_l = split_lo[:, f, c * 512:(c + 1) * 512]
                            pe.matmul(acc, g_h, v_h, start=first, stop=False)
                            pe.matmul(acc, g_h, v_l, start=False, stop=False)
                            ins = pe.matmul(acc, g_l, v_h, start=False, stop=last)
                    ins.then_inc(split_free, 1)

            v_tile(0, 0, True, False)
            v_tile(0, 1, False, False)
            with pe.Fori(1, NE_T // 2 - 1) as pair:
                i = pair * 2
                v_tile(i, 0, False, False)
                v_tile(i, 1, False, False)
            v_tile(NE_T - 2, 0, False, False)
            v_tile(NE_T - 2, 1, False, True)


_INS = ['x', 'norm1_g', 'w_in', 'cmp_pe', 'cmp_k_w1', 'cmp_k_w2', 'cmp_v_w1', 'cmp_v_w2', 'q_norm_g', 'k_norm_g',
        'rel_bias_table', 'sb_out_g', 'nsa_out_g', 'w_out', 'norm2_g', 'peer_w_query', 'peer_sub_keys',
        'peer_expert_u', 'peer_expert_v']


def kernel(**inputs):
    import numpy as _np
    import concourse.bacc as _bacc
    from concourse import mybir as _mybir
    from concourse.bass_utils import run_bass_kernel_spmd as _run

    nc = _bacc.Bacc("TRN2", target_bir_lowering=False, num_devices=1)
    arrays, args = {}, []
    for name in _INS:
        a = _np.ascontiguousarray(inputs[name])
        arrays[f"in_{name}"] = a
        args.append(nc.dram_tensor(f"in_{name}", a.shape, _mybir.dt.from_np(a.dtype), kind="ExternalInput").ap())
    a = bucket_onehot()
    arrays["bucket_onehot"] = a
    args.append(nc.dram_tensor("bucket_onehot", a.shape, _mybir.dt.from_np(a.dtype), kind="ExternalInput").ap())
    args.append(nc.dram_tensor("out_0", (1, T, D), _mybir.dt.float32, kind="ExternalOutput").ap())
    layer(nc, *args)
    r = _run(nc, [arrays], core_ids=[0])
    return r.results[0]["out_0"]
```

```python
from contextlib import ExitStack

import numpy as np

import concourse.bass as bass
from concourse import mybir

ALU = mybir.AluOpType
ACT = mybir.ActivationFunctionType
F32 = mybir.dt.float32
F32R = mybir.dt.float32r
U32 = mybir.dt.uint32
AX_X = mybir.AxisListType.X

P = 128
T = 256
D = 2048
TT = T // P
KC = D // P
HD = 128
NH = 8
NG = 2
GROUP = NH // NG
IN_COLS = 5656
EPS = 1e-6
NEG = -1e30
SCALE = HD ** -0.5
CMP_BLOCK, CMP_STRIDE, CMP_HIDDEN = 32, 16, 256
NC = (T - CMP_BLOCK) // CMP_STRIDE + 1
N_BUCKETS, MAX_DISTANCE = 32, 128
NKEYS = 128
TOPK = 16
HP = 2 * NH
NE = NKEYS * NKEYS

COL_QSB, COL_KSB, COL_VSB, COL_Q = 0, 1024, 2048, 3072
COL_KCMP, COL_VCMP, COL_KSLC, COL_VSLC, COL_KWIN, COL_VWIN, COL_GATE = 4096, 4352, 4608, 4864, 5120, 5376, 5632
N_GATES = IN_COLS - COL_GATE

G_NORM1, G_NORM2, G_MIX, G_Q, G_K, G_PE = 0, 16, 32, 48, 49, 50
G_ALL = G_PE + CMP_BLOCK

RAW = 4
SPLIT = 2
STEP = 1024
CHUNK = 512
W_IN_CHUNKS = COL_GATE // CHUNK
STEPS_PER_CHUNK = D * CHUNK // P // STEP
TAIL_STEPS = 4
TAIL_K = KC // TAIL_STEPS
W_CHUNKS = D // CHUNK
CMP_STEPS = 2 * CMP_BLOCK * HD * CMP_HIDDEN // P // STEP
CMP_L = STEP // CMP_HIDDEN
E_STEPS = 2 * NE // P
UNIT = 512
UNITS = D // UNIT
UNIT_K = UNIT // P
U_UNITS = UNITS * NE // P

RAW_IN = 0
RAW_TAIL = RAW_IN + W_IN_CHUNKS * STEPS_PER_CHUNK
RAW_CMP = RAW_TAIL + TAIL_STEPS
RAW_OUT = RAW_CMP + CMP_STEPS
RAW_QUERY = RAW_OUT + W_CHUNKS * STEPS_PER_CHUNK
RAW_U = RAW_QUERY + W_CHUNKS * STEPS_PER_CHUNK
RAW_V = RAW_U + E_STEPS

SP_IN = 0
SP_TAIL = SP_IN + W_IN_CHUNKS * STEPS_PER_CHUNK
SP_OUT = SP_TAIL + TAIL_STEPS
SP_QUERY = SP_OUT + W_CHUNKS * STEPS_PER_CHUNK
SP_U = SP_QUERY + W_CHUNKS * STEPS_PER_CHUNK
SP_V = SP_U + U_UNITS

CH_IN, CH_TAIL, CH_OUT = 0, W_IN_CHUNKS, W_IN_CHUNKS + 1
CH_QUERY = CH_OUT + W_CHUNKS

BIAS_W = 512
NE_T = NE // P
TOKENS_PER_BANK = 4
BUILD_STEPS = T // TOKENS_PER_BANK
HEADS = TT * NH
TILES_PER_HEAD = 4
ROUTE_TILES = HEADS * TILES_PER_HEAD
assert NE_T - ROUTE_TILES == BUILD_STEPS
HEAD_OPS = 28


def bucket_onehot():
    dist = np.maximum(T - np.arange(BIAS_W), 0)
    exact = N_BUCKETS // 2
    ratio = np.log(np.maximum(dist, 1).astype(np.float32) / np.float32(exact)) / np.float32(np.log(MAX_DISTANCE / exact))
    large = np.minimum(exact + (ratio * (N_BUCKETS - exact)).astype(np.int32), N_BUCKETS - 1)
    bucket = np.where(dist < exact, dist, large)
    return (np.arange(N_BUCKETS)[:, None] == bucket[None, :]).astype(np.float32)


def layer(nc, x, norm1_g, w_in, cmp_pe, cmp_k_w1, cmp_k_w2, cmp_v_w1, cmp_v_w2, q_norm_g, k_norm_g,
          rel_bias_table, sb_out_g, nsa_out_g, w_out, norm2_g, peer_w_query, peer_sub_keys,
          peer_expert_u, peer_expert_v, onehot, out):
    with ExitStack() as ctx:
        def sb(name, shape, dt=F32):
            return ctx.enter_context(nc.sbuf_tensor(name, shape, dt))

        sems = {}

        def sem(name):
            if name not in sems:
                sems[name] = ctx.enter_context(nc.semaphore(name))
            return sems[name]

        x1_dram = nc.dram_tensor("x1_dram", [T, D], F32, kind="Internal").ap()
        bias_dram = nc.dram_tensor("bias_dram", [NH, P, BIAS_W + 1], F32, kind="Internal").ap()

        big = sb("big", [P, NE_T * T])
        raw = sb("raw", [P, RAW, STEP])
        split_hi = sb("split_hi", [P, SPLIT, STEP], F32R)
        split_lo = sb("split_lo", [P, SPLIT, STEP], F32R)
        ht = sb("ht", [P, KC, 2 * T], F32R)
        ident = sb("ident", [P, P])
        iota = sb("iota", [P, P])
        gain_cols = sb("gain_cols", [P, G_ALL])
        picked = sb("picked", [P, 3, T])
        s_sum = sb("s_sum", [P, 2, T])
        w_hi = sb("w_hi", [P, 2, T], F32R)
        w_lo = sb("w_lo", [P, 2, T], F32R)
        one_i = sb("one_i", [P, 2, TOKENS_PER_BANK * P])
        small = sb("small", [P, 280])
        ps = ctx.enter_context(nc.psum_tensor("ps", [P, 8, 512], F32))
        psf = ps[:, :, :].rearrange("p b n -> p (b n)")

        at = [0]

        def tiny(n):
            at[0] += n
            assert at[0] <= 280
            return small[:, at[0] - n:at[0]]

        ssq = tiny(8)
        rstd = tiny(8)
        gates = tiny(TT * N_GATES)
        nssq = tiny(24)
        nrstd = tiny(24)
        row_max = tiny(16)
        row_sum = tiny(16)
        coef = tiny(16)
        has_block = tiny(1)
        kssq = tiny(2)
        krstd = tiny(2)
        minus_half = tiny(24)

        at_big = [0]

        def part(n, at=None):
            a = at_big[0] if at is None else at
            at_big[0] = a + n
            assert a + n <= NE_T * T
            return big[:, a:a + n]

        X = part(TT * D).rearrange("p (t d) -> p t d", t=TT)
        A_PROJ = TT * D
        PROJ = part(TT * IN_COLS).rearrange("p (t n) -> p t n", t=TT)
        MIX = part(TT * D).rearrange("p (t d) -> p t d", t=TT)
        A_XN = A_PROJ + TT * IN_COLS + TT * D
        XN = part(TT * D).rearrange("p (t d) -> p t d", t=TT)
        QKT = part(4 * 512, A_XN).rearrange("p (h n) -> p h n", h=4)
        T1f = part(4 * 384)
        T2f = part(4 * 384)
        T1 = T1f.rearrange("p (h n) -> p h n", h=4)
        T2 = T2f.rearrange("p (h n) -> p h n", h=4)
        T2b = T2f.rearrange("p (b n) -> p b n", b=12)
        A_T1 = A_XN + 2048
        PCT = big[:, A_T1:A_T1 + 2048].rearrange("p (b n) -> p b n", b=16)
        BIAS = part(NH * 384).rearrange("p (h n) -> p h n", h=NH)
        A_QT = at_big[0]
        QT = part(NH * T).rearrange("p (h n) -> p h n", h=NH)
        KT = part(2 * NG * T).rearrange("p (b g n) -> p b g n", b=2, g=NG)
        KVC = part(2 * NG * T).rearrange("p (b g n) -> p b g n", b=2, g=NG)
        W2S = part(512).rearrange("p (w n) -> p w n", w=4)
        neg_tri, neg_ones, before = part(P), part(P), part(P)
        cmp_p = T1f[:, 0:16 * NC]
        SQ = big[:, A_QT:A_QT + 2048]
        SQK = big[:, A_QT + 2048:A_QT + 3072]
        gain_rows = MIX[:, 0, 1536:1536 + P]
        HG = big[:, A_XN:A_XN + 512].rearrange("p (v n) -> p v n", v=2)
        HGT = big[:, A_XN + 512:A_XN + 768].rearrange("p (w n) -> p w n", w=4)
        KCV = big[:, A_XN + 768:A_XN + 1280].rearrange("p (v g n) -> p v g n", v=2, g=NG)
        KCT = big[:, A_XN + 1280:A_XN + 1312].rearrange("p (g n) -> p g n", g=NG)
        KSQ = big[:, A_XN + 1312:A_XN + 1568].rearrange("p (g n) -> p g n", g=NG)
        BLK = PROJ[:, :, 0:CMP_BLOCK * 64].rearrange("p v (l n) -> p v l n", l=CMP_BLOCK)
        TMP = PROJ[:, 0, COL_VSB:COL_VSB + 1024]
        ROWB = MIX[0:NH, 0, 0:BIAS_W]
        TABLE = MIX[0:N_BUCKETS, 0, 1024:1024 + NH]
        ONEHOT = MIX[0:N_BUCKETS, 1, 0:BIAS_W]

        Q = big[:, A_PROJ:A_PROJ + TT * D].rearrange("p (t d) -> p t d", t=TT)
        A_R = 16384
        SK = part(2048, A_R).rearrange("p (w n) -> p w n", w=HP)
        SKT = part(2048).rearrange("p (w n) -> p w n", w=HP)
        PQT = part(4096).rearrange("p (w n) -> p w n", w=HP)
        S = part(4096).rearrange("p (t w n) -> p t w n", t=TT, w=HP)
        PICK = part(768).rearrange("p (s t h k) -> p s t h k", s=3, t=TT, h=NH)
        GSUM = part(16).rearrange("p (t h) -> p t h", t=TT)
        head_s = part(2 * NKEYS).rearrange("p (s n) -> p s n", s=2)
        head_top = part(2 * TOPK).rearrange("p (s k) -> p s k", s=2)
        head_topi = part(2 * TOPK).bitcast(U32).rearrange("p (s k) -> p s k", s=2)
        head_topf = part(2 * TOPK).rearrange("p (s k) -> p s k", s=2)
        head_sums = part(TOPK * TOPK)
        head_best = part(TOPK)
        head_pos = part(TOPK).bitcast(U32)
        head_ab = part(2 * TOPK).bitcast(U32).rearrange("p (s k) -> p s k", s=2)
        head_abf = part(2 * TOPK).rearrange("p (s k) -> p s k", s=2)
        head_eq = part(2 * TOPK * TOPK).rearrange("p (s k a) -> p s k a", s=2, k=TOPK)

        WACT = big[:, :].rearrange("p (i c) -> p i c", c=T)
        WACT_C = big[:, :].rearrange("p (i c) -> p c i", c=T)
        one_j = [w[:, :, :].rearrange("p a b -> p (a b)") for w in (w_hi, w_lo)]
        unit_hi = split_hi[:, :, :].rearrange("p s n -> p (s n)")
        unit_lo = split_lo[:, :, :].rearrange("p s n -> p (s n)")
        X1 = big[:, 0:TT * D].rearrange("p (t d) -> p t d", t=TT)

        x_rows = x.rearrange("b (t p) d -> p (b t) d", p=P)
        x1_rows = x1_dram.rearrange("(t p) d -> p t d", p=P)
        out_rows = out.rearrange("b (t p) d -> p (b t) d", p=P)
        win_k = w_in[0].rearrange("(k p) n -> p k n", p=P)
        wout_k = w_out[0].rearrange("(k p) n -> p k n", p=P)
        wq_k = peer_w_query[0].rearrange("(k p) n -> p k n", p=P)
        u_rows = peer_expert_u[0].rearrange("(i p) (f d) -> i f p d", p=P, f=2)
        v_rows = peer_expert_v[0].rearrange("(i p) (f d) -> i f p d", p=P, f=2)

        raw_loaded = [sem(f"raw_loaded{i}") for i in range(RAW)]
        hi_done, split_done, split_free = sem("hi_done"), sem("split_done"), sem("split_free")
        acc_free = sem("acc_free")
        u_turned = sem("u_turned")
        cmp_used = sem("cmp_used")
        x1_stored, out_stored = sem("x1_stored"), sem("out_stored")

        def loaded(eng, slot, g):
            eng.wait_ge(raw_loaded[slot], 16 * (g // RAW + 1))

        block = ctx.enter_context(nc.Block())

        @block.sync
        def _(sp):
            def load(slot, src, shape=None):
                dst = raw[:, slot, :]
                if shape:
                    dst = dst[:, 0:shape[0] * shape[1]].rearrange("p (a b) -> p a b", a=shape[0])
                sp.dma_start(dst, src).then_inc(raw_loaded[slot], 16)

            def chunk(src_k, c, signal, first):
                for s in range(STEPS_PER_CHUNK):
                    if first is not None or s >= RAW:
                        sp.wait_ge(signal, (0 if first is None else first) + s - (RAW if first is None else 0) + 1)
                    load(s % RAW, src_k[:, 2 * s:2 * s + 2, bass.ds(c * CHUNK, CHUNK)], (2, CHUNK))

            sp.dma_start(X, x_rows).then_inc(sem("x_loaded"), 16)
            for src, row, n in ((norm1_g[0], G_NORM1, 16), (norm2_g[0], G_NORM2, 16), (sb_out_g[0], G_MIX, 8),
                                (nsa_out_g[0], G_MIX + 8, 8), (q_norm_g[0], G_Q, 1), (k_norm_g[0], G_K, 1)):
                sp.dma_start(gain_rows[row:row + n, :], src.rearrange("(a n) -> a n", n=P)).then_inc(sem("gains_loaded"), 16)
            sp.dma_start(gain_rows[G_PE:G_ALL, :], cmp_pe[0]).then_inc(sem("gains_loaded"), 16)
            sp.dma_start(TABLE, rel_bias_table).then_inc(sem("table_loaded"), 16)
            sp.dma_start(ONEHOT, onehot).then_inc(sem("table_loaded"), 16)
            for v, w2 in enumerate((cmp_k_w2, cmp_v_w2)):
                sp.dma_start(W2S[:, 2 * v:2 * v + 2, :], w2[0].rearrange("(f p) n -> p f n", p=P)).then_inc(sem("w2_loaded"), 16)
            chunk(win_k, 0, split_done, None)
            with sp.Fori(1, W_IN_CHUNKS) as c:
                chunk(win_k, c, split_done, c * STEPS_PER_CHUNK - RAW)
            for s in range(TAIL_STEPS):
                sp.wait_ge(split_done, SP_TAIL + s - RAW + 1)
                load(s, win_k[:, TAIL_K * s:TAIL_K * (s + 1), COL_GATE:IN_COLS], (TAIL_K, N_GATES))
            for s in range(CMP_STEPS):
                if s < RAW:
                    sp.wait_ge(split_done, SP_TAIL + s + 1)
                else:
                    sp.wait_ge(cmp_used, s - RAW + 1)
                w1 = (cmp_k_w1, cmp_v_w1)[s * 2 // CMP_STEPS][0].rearrange("(l p) n -> p l n", p=P)
                l = CMP_L * (s % (CMP_STEPS // 2))
                load(s % RAW, w1[:, l:l + CMP_L, :], (CMP_L, CMP_HIDDEN))
            for s in range(RAW):
                sp.wait_ge(cmp_used, CMP_STEPS - RAW + s + 1)
                load(s, wout_k[:, 2 * s:2 * s + 2, 0:CHUNK], (2, CHUNK))
            for s in range(RAW, STEPS_PER_CHUNK):
                sp.wait_ge(split_done, SP_OUT + s - RAW + 1)
                load(s % RAW, wout_k[:, 2 * s:2 * s + 2, 0:CHUNK], (2, CHUNK))
            with sp.Fori(1, W_CHUNKS) as c:
                chunk(wout_k, c, split_done, c * STEPS_PER_CHUNK + SP_OUT - RAW)
            sp.wait_ge(sem("x1_ready"), W_CHUNKS)
            sp.dma_start(x1_rows, X).then_inc(x1_stored, 16)
            sp.dma_start(SK, peer_sub_keys[0].rearrange("h s n d -> n (h s) d")).then_inc(sem("keys_loaded"), 16)
            with sp.Fori(0, W_CHUNKS) as c:
                chunk(wq_k, c, split_done, c * STEPS_PER_CHUNK + SP_QUERY - RAW)
            for s in range(RAW):
                sp.wait_ge(split_done, SP_U + s - RAW + 1)
                load(s, u_rows[s // 2, s % 2])
            with sp.Fori(1, NE_T // 2) as pair:
                i = pair * 2
                for s in range(RAW):
                    sp.wait_ge(u_turned, i * 4 + 2 * (s - RAW + 1))
                    load(s, u_rows[bass.ds(i + s // 2, 1), s % 2].rearrange("a p d -> (a p) d"))
            for s in range(RAW):
                sp.wait_ge(u_turned, U_UNITS - 2 * (RAW - s - 1))
                load(s, v_rows[s // 2, s % 2])
            with sp.Fori(1, NE_T // 2) as pair:
                i = pair * 2
                for s in range(RAW):
                    sp.wait_ge(split_done, i * 2 + s - RAW + SP_V + 1)
                    load(s, v_rows[bass.ds(i + s // 2, 1), s % 2].rearrange("a p d -> (a p) d"))
            sp.wait_ge(x1_stored, 16)
            sp.wait_ge(sem("w_lo_done"), 16)
            sp.dma_start(X1, x1_rows).then_inc(sem("x1_loaded"), 16)
            for t in range(TT):
                sp.wait_ge(sem("out_ready"), t + 1)
                sp.dma_start(out_rows[:, t, :], X1[:, t, :]).then_inc(out_stored, 16)
            sp.wait_ge(out_stored, 16 * TT)

        @block.gpsimd
        def _(pool):
            made = sem("constants")
            pool.memset(ident[:], 0.0).then_inc(made, 1)
            pool.memset(neg_tri, -1.0).then_inc(made, 1)
            pool.memset(before, 1.0).then_inc(made, 1)
            pool.memset(neg_ones, -1.0).then_inc(made, 1)
            pool.memset(has_block, 1.0).then_inc(made, 1)
            pool.iota(iota[:], pattern=[[1, P]], base=0, channel_multiplier=0, allow_small_or_imprecise_dtypes=True).then_inc(made, 1)
            pool.memset(minus_half, -0.5).then_inc(made, 1)
            pool.wait_ge(made, 7)
            pool.affine_select(out=ident[:], in_=ident[:], compare_op=ALU.not_equal, fill=1.0, base=0,
                               pattern=[[-1, P]], channel_multiplier=1).then_inc(made, 1)
            pool.affine_select(out=neg_tri, in_=neg_tri, compare_op=ALU.is_ge, fill=0.0, base=0,
                               pattern=[[-1, P]], channel_multiplier=1).then_inc(made, 1)
            pool.affine_select(out=before, in_=before, compare_op=ALU.is_gt, fill=0.0, base=0,
                               pattern=[[1, P]], channel_multiplier=-1).then_inc(made, 1)
            pool.affine_select(out=has_block, in_=has_block, compare_op=ALU.is_ge, fill=0.0, base=1 - CMP_BLOCK,
                               pattern=[[0, 1]], channel_multiplier=1).then_inc(made, 1)
            def power(n, v):
                pool.wait_ge(sem("mean_square"), n)
                pool.tensor_tensor(v, v, minus_half[0:v.shape[0], 0:v.shape[1]], ALU.pow).then_inc(sem("inverse_rms"), 1)

            power(1, rstd[:, 0:TT])
            pool.wait_ge(sem("bias_rows"), 1)
            pool.dma_start(bias_dram[:, :, 0:BIAS_W], ROWB.unsqueeze(1).broadcast_to([NH, P, BIAS_W])).then_inc(sem("bias_stored"), 16)
            pool.wait_ge(sem("bias_stored"), 16)
            pool.dma_start(BIAS, bass.AP(tensor=bias_dram.tensor, offset=P, ap=[[BIAS_W, P], [P * (BIAS_W + 1), NH], [1, 384]])).then_inc(sem("bias_loaded"), 16)
            power(2, nrstd)
            pool.wait_ge(sem("sb_out"), 2)
            for v in range(2):
                pool.memset(PROJ[:, v, 0:CMP_BLOCK * 64], 0.0).then_inc(sem("blocks_cleared"), 1)
            power(3, krstd[0:NC])
            power(4, rstd[:, 0:2 * TT])
            power(5, rstd[:, 0:TT])
            pool.wait_ge(sem("picks_turned"), 1)
            pool.memset(WACT[:, ROUTE_TILES:NE_T, :], 1.0).then_inc(sem("gates_cleared"), 1)

        @block.scalar
        def _(act):
            act_step = sem("act_step")
            steps = [0]

            def link(ins):
                steps[0] += 1
                ins.then_inc(act_step, 1)
                act.wait_ge(act_step, steps[0])

            def hi(slot, g, n, width):
                loaded(act, slot, g)
                act.wait_ge(split_free, n + 1)
                act.activation(split_hi[:, slot % SPLIT, 0:width], raw[:, slot, 0:width], ACT.Copy).then_inc(hi_done, 1)

            def loaded_at(slot, uses):
                act.wait_ge(raw_loaded[slot], 16 * uses)

            def hi_chunk(uses0, n0):
                for s in range(STEPS_PER_CHUNK):
                    loaded_at(s % RAW, uses0 + (s // RAW + 1))
                    act.wait_ge(split_free, n0 + s + 1)
                    act.activation(split_hi[:, s % SPLIT, :], raw[:, s % RAW, :], ACT.Copy).then_inc(hi_done, 1)

            def turned_hi(use, gain0):
                for k in range(KC):
                    if k % 2 == 0:
                        act.wait_ge(sem("rows_turned"), (KC // 2) * use + k // 2 + 1)
                    act.activation(ht[:, k, 0:T], psf[:, k * T:(k + 1) * T], ACT.Copy,
                                   scale=gain_cols[:, gain0 + k:gain0 + k + 1]).then_inc(sem("ht_hi"), 1)

            act.wait_ge(sem("gains_turned"), 1)
            link(act.activation(gain_cols[:], psf[:, 0:G_ALL], ACT.Copy))
            act.sem_inc(sem("gains_ready"), 1)
            turned_hi(0, G_NORM1)
            with act.Fori(0, W_IN_CHUNKS) as c:
                hi_chunk(c * 2 + RAW_IN // RAW, c * STEPS_PER_CHUNK + SP_IN)
            for s in range(TAIL_STEPS):
                hi(s, RAW_TAIL + s, SP_TAIL + s, TAIL_K * N_GATES)

            act.wait_ge(acc_free, 2 + CH_TAIL + 1)
            act.activation(gates.rearrange("p (t n) -> p t n", t=TT), PROJ[:, :, COL_GATE:IN_COLS], ACT.Exp, scale=-1.0).then_inc(sem("gate_exp"), 1)

            act.preload_act_table_set("natural_log_exp_and_others")
            for b in range(2):
                act.wait_ge(sem("sb_turned"), b + 1)
                act.activation(QKT[:, :, 0:T], ps[:, 4:8, 0:T], ACT.Copy, scale=SCALE).then_inc(sem("sb_q"), 1)
                act.wait_ge(sem("sb_z"), b + 1)
                link(act.activation(T1, ps[:, 0:4, 0:384], ACT.Abs))
                link(act.activation(T1f, T1f, ACT.Exp, scale=-1.0))
                act.activation(T1f, T1f, ACT.Ln, bias=1.0).then_inc(sem("sb_ln"), 1)
                act.wait_ge(sem("sb_cumsum"), b + 1)
                act.activation(T1, ps[:, 0:4, 0:384], ACT.Exp).then_inc(sem("sb_exp"), 1)

            act.wait_ge(sem("q_turned"), 1)
            act.activation(QT.rearrange("p h n -> p (h n)"), psf[:, 0:2048], ACT.Copy, scale=gain_cols[:, G_Q:G_Q + 1]).then_inc(sem("q_ready"), 1)
            act.wait_ge(cmp_used, CMP_STEPS)
            act.activation(HG[0:64], ps[0:64, 0:2, 0:CMP_HIDDEN], ACT.Gelu_apprx_tanh).then_inc(sem("hidden"), 1)
            act.wait_ge(sem("hidden_turned"), 1)
            act.activation(HGT.rearrange("p w n -> p (w n)"), psf[:, 2 * 512:2 * 512 + 256], ACT.Copy).then_inc(sem("hidden_t"), 1)
            act.wait_ge(sem("cmp_shifted"), 1)
            act.activation(cmp_p, cmp_p, ACT.Exp).then_inc(sem("cmp_exp"), 1)
            act.wait_ge(sem("cmp_p_turned"), 1)
            act.wait_ge(sem("cmp_summed"), 1)
            act.activation(PCT[0:NC].rearrange("p b n -> p (b n)"), psf[0:NC, 0:2048], ACT.Copy).then_inc(sem("cmp_pt"), 1)
            for r in range(4):
                act.wait_ge(sem("ns_shifted"), r + 1)
                act.activation(T1f, T1f, ACT.Exp).then_inc(sem("ns_exp"), 1)
                act.wait_ge(sem("ns_p_turned"), r + 1)
                act.activation(T2f, psf[:, 4 * 512:7 * 512], ACT.Copy).then_inc(sem("ns_pt"), 1)

            turned_hi(1, G_MIX)
            with act.Fori(0, W_CHUNKS) as c:
                hi_chunk(c * 2 + RAW_OUT // RAW, c * STEPS_PER_CHUNK + SP_OUT)
            turned_hi(2, G_NORM2)
            with act.Fori(0, W_CHUNKS) as c:
                hi_chunk(c * 2 + RAW_QUERY // RAW, c * STEPS_PER_CHUNK + SP_QUERY)

            for b in range(2):
                act.wait_ge(sem("pq_turned"), b + 1)
                act.activation(PQT.rearrange("p w n -> p (w n)")[:, b * 2048:(b + 1) * 2048],
                               psf[:, b * 2048:(b + 1) * 2048], ACT.Copy).then_inc(sem("pq_ready"), 1)
            act.wait_ge(sem("keys_turned"), 1)
            act.activation(SKT.rearrange("p w n -> p (w n)"), psf[:, 0:2048], ACT.Copy).then_inc(sem("keys_ready"), 1)

            def unit_part(i, j, u):
                n = i * UNITS + j * UNITS + u
                act.wait_ge(u_turned, n + 1)
                act.wait_ge(split_free, n + SP_U - 1)
                act.activation(unit_hi[:, u * UNIT:(u + 1) * UNIT], ps[:, u, :], ACT.Copy).then_inc(hi_done, 1)

            def gelu(i, j):
                act.wait_ge(sem("s_summed"), i + j + 3)
                act.activation(WACT[:, bass.ds(i + j, 1), :].rearrange("p a c -> p (a c)"),
                               s_sum[:, j % 2, :], ACT.Gelu_apprx_tanh).then_inc(sem("acted"), 1)

            def route_tiles(i, first):
                for j in range(TILES_PER_HEAD):
                    for u in range(UNITS):
                        unit_part(i, j, u)
                        if u == 1 and j:
                            gelu(i, j - 1)
                        if u == 1 and not j and not first:
                            gelu_before(i)

            def gelu_before(i):
                act.wait_ge(sem("s_summed"), i + 2)
                act.activation(WACT[:, bass.ds(i - 1, 1), :].rearrange("p a c -> p (a c)"),
                               s_sum[:, 1, :], ACT.Gelu_apprx_tanh).then_inc(sem("acted"), 1)

            act.preload_act_table(ACT.Gelu_apprx_tanh)
            route_tiles(0, True)
            with act.Fori(1, HEADS) as head:
                route_tiles(head * TILES_PER_HEAD, False)
            act.wait_ge(sem("s_summed"), ROUTE_TILES + 2)
            act.activation(WACT[:, ROUTE_TILES - 1, :], s_sum[:, 1, :], ACT.Gelu_apprx_tanh).then_inc(sem("acted"), 1)
            act.wait_ge(sem("best_shifted"), 1)
            act.activation(PICK[:, 2], PICK[:, 2], ACT.Exp).then_inc(sem("best_exp"), 1)
            act.preload_act_table(ACT.Gelu_apprx_tanh)

            def build_tile(s, j, first):
                i = s + ROUTE_TILES
                unit_part(i, j, 0)
                act.wait_ge(sem("gates_mm"), s + j + 1)
                if first and not j:
                    act.wait_ge(sem("picked_ready"), 3)
                for c in range(TOKENS_PER_BANK):
                    col = s * TOKENS_PER_BANK + j * TOKENS_PER_BANK + c
                    ins = act.activation(one_j[j][:, c * P:(c + 1) * P], iota[:, :], ACT.Abs, scale=-1.0,
                                         bias=picked[:, 1, bass.ds(col, 1)])
                    if c == 1:
                        unit_part(i, j, 1)
                ins.then_inc(sem("onehot_abs"), 1)
                if not (first and not j):
                    act.wait_ge(sem("s_summed"), s + j + ROUTE_TILES + 2)
                    act.activation(s_sum[:, 1 - j, :], s_sum[:, 1 - j, :], ACT.Gelu_apprx_tanh).then_inc(sem("acted"), 1)
                unit_part(i, j, 2)
                act.wait_ge(sem("onehot_abs"), s + j + 1)
                act.activation(one_j[j], one_j[j].bitcast(F32), ACT.Relu, scale=-1.0, bias=1.0).then_inc(sem("onehot_j"), 1)
                unit_part(i, j, 3)

            for j in range(2):
                build_tile(0, j, True)
            with act.Fori(1, BUILD_STEPS // 2) as pair:
                for j in range(2):
                    build_tile(pair * 2, j, False)
            act.wait_ge(sem("s_summed"), NE_T + 2)
            act.activation(s_sum[:, 1, :], s_sum[:, 1, :], ACT.Gelu_apprx_tanh).then_inc(sem("acted"), 1)

            def v_tile(i, j):
                act.wait_ge(split_free, i * 2 + 2 * j + SP_V)
                if j == 0:
                    act.wait_ge(sem("gates_built"), BUILD_STEPS + 2)
                act.activation(w_hi[:, j, :], WACT[:, bass.ds(i + j, 1), :].rearrange("p a c -> p (a c)"), ACT.Copy).then_inc(sem("w_hi_done"), 1)
                for f in range(2):
                    slot = 2 * j + f
                    act.wait_ge(raw_loaded[slot], i * 8 + 16 * (RAW_V // RAW + 1))
                    act.wait_ge(split_free, i * 2 + 2 * j + f + SP_V + 1)
                    act.activation(split_hi[:, f, :], raw[:, slot, :], ACT.Copy).then_inc(hi_done, 1)

            with act.Fori(0, NE_T // 2) as pair:
                i = pair * 2
                for j in range(2):
                    v_tile(i, j)

        @block.vector
        def _(dve):
            dve_step = sem("dve_step")
            steps = [0]

            def link(ins):
                steps[0] += 1
                ins.then_inc(dve_step, 1)
                dve.wait_ge(dve_step, steps[0])

            def flag(name, n=1):
                dve.sem_inc(sem(name), n)

            def lo(slot, n, width=STEP):
                dve.wait_ge(hi_done, n + 1)
                dve.tensor_tensor(split_lo[:, slot % SPLIT, 0:width], raw[:, slot, 0:width],
                                  split_hi[:, slot % SPLIT, 0:width].bitcast(F32), ALU.subtract).then_inc(split_done, 1)

            norms = [0]

            def inverse_rms(dst, sums, n):
                norms[0] += 1
                dve.tensor_scalar(dst, sums, 1.0 / n, EPS, ALU.mult, ALU.add).then_inc(sem("mean_square"), 1)
                dve.wait_ge(sem("inverse_rms"), norms[0])

            def normed_rows(src, parts):
                w = D // parts
                for t in range(TT):
                    for h in range(parts):
                        ins = dve.tensor_tensor_reduce(XN[:, t, h * w:(h + 1) * w], src[:, t, h * w:(h + 1) * w],
                                                       src[:, t, h * w:(h + 1) * w], 1.0, 0.0, ALU.mult, ALU.add,
                                                       ssq[:, t * parts + h:t * parts + h + 1])
                link(ins)
                inverse_rms(rstd[:, 0:TT * parts], ssq[:, 0:TT * parts], w)
                for t in range(TT):
                    for h in range(parts):
                        ins = dve.tensor_scalar(XN[:, t, h * w:(h + 1) * w], src[:, t, h * w:(h + 1) * w],
                                                rstd[:, t * parts + h:t * parts + h + 1], None, ALU.mult)
                ins.then_inc(sem("rows_normed"), 1)

            def turned_lo(use, gain0):
                for k in range(KC):
                    if k % 2 == 0:
                        dve.wait_ge(sem("ht_hi"), KC * use + k + 2)
                    dve.scalar_tensor_tensor(out=ht[:, k, T:2 * T], in0=psf[:, k * T:(k + 1) * T],
                                             scalar=gain_cols[:, gain0 + k:gain0 + k + 1],
                                             in1=ht[:, k, 0:T].bitcast(F32), op0=ALU.mult,
                                             op1=ALU.subtract).then_inc(sem("ht_lo"), 1)

            def bank_pair(parity, width):
                return ps[:, 2 * parity:2 * parity + 2, 0:width]

            def to_proj(c, parity, n_end):
                dve.wait_ge(split_free, n_end + 2)
                dve.tensor_copy(PROJ[:, :, bass.ds(c * CHUNK, CHUNK)], bank_pair(parity, CHUNK)).then_inc(acc_free, 1)

            dve.wait_ge(sem("x_loaded"), 16)
            normed_rows(X, 1)
            dve.memset(s_sum[:], 0.0).then_inc(acc_free, 2)
            dve.wait_ge(sem("bias_mm"), 1)
            link(dve.tensor_copy(ROWB[:, 0:T + 1], ps[0:NH, 7, 0:T + 1]))
            dve.memset(ROWB[:, T + 1:BIAS_W], NEG).then_inc(sem("bias_rows"), 1)
            turned_lo(0, G_NORM1)

            def in_chunk(c, parity, prev):
                for s in range(STEPS_PER_CHUNK):
                    lo(s % RAW, c * STEPS_PER_CHUNK + s + SP_IN)
                    if s == 1 and prev:
                        to_proj(c - 1, 1 - parity, c * STEPS_PER_CHUNK + SP_IN)

            in_chunk(0, 0, False)
            with dve.Fori(0, W_IN_CHUNKS // 2) as pair:
                c = pair * 2 + 1
                in_chunk(c, 1, True)
                in_chunk(c + 1, 0, True)
            for s in range(TAIL_STEPS):
                lo(s, SP_TAIL + s, TAIL_K * N_GATES)
                if s == 1:
                    to_proj(W_IN_CHUNKS - 1, (W_IN_CHUNKS - 1) % 2, SP_TAIL)
            dve.wait_ge(split_free, SP_OUT + 2)
            dve.tensor_copy(PROJ[:, :, COL_GATE:IN_COLS], bank_pair(CH_TAIL % 2, N_GATES)).then_inc(acc_free, 1)
            dve.wait_ge(acc_free, 2 + CH_TAIL + 1)

            q_rows = PROJ[:, :, COL_Q:COL_Q + NH * HD]
            for t in range(TT):
                dve.tensor_tensor(SQ[:, t * 1024:(t + 1) * 1024], q_rows[:, t, :], q_rows[:, t, :], ALU.mult)
            for b, col in enumerate((COL_KSLC, COL_KWIN)):
                k_rows = PROJ[:, :, col:col + NG * HD]
                ins = dve.tensor_tensor(SQK[:, b * 512:(b + 1) * 512].rearrange("p (t n) -> p t n", t=TT), k_rows, k_rows, ALU.mult)
            link(ins)
            link(dve.tensor_reduce(nssq, big[:, A_QT:A_QT + 3072].rearrange("p (h d) -> p h d", d=HD), AX_X, ALU.add))
            inverse_rms(nrstd, nssq, HD)
            for t in range(TT):
                v = q_rows[:, t, :].rearrange("p (h d) -> p h d", d=HD)
                dve.tensor_tensor(v, v, nrstd[:, t * NH:(t + 1) * NH].unsqueeze(2).broadcast_to([P, NH, HD]), ALU.mult)
            for b, col in enumerate((COL_KSLC, COL_KWIN)):
                for t in range(TT):
                    v = PROJ[:, t, col:col + NG * HD].rearrange("p (g d) -> p g d", d=HD)
                    o = 16 + b * 4 + t * NG
                    ins = dve.tensor_tensor(v, v, nrstd[:, o:o + NG].unsqueeze(2).broadcast_to([P, NG, HD]), ALU.mult)
            ins.then_inc(sem("nsa_normed"), 1)
            dve.wait_ge(sem("gate_exp"), 1)
            link(dve.tensor_scalar(gates, gates, 1.0, None, ALU.add))
            link(dve.reciprocal(gates, gates))
            gate = gates.rearrange("p (t h r) -> p t h r", t=TT, r=3)

            dve.wait_ge(sem("constants"), 11)

            def diagonal(v):
                f = v.rearrange("p h (b n) -> p h b n", n=P)
                return [f[:, :, b, :] for b in (0, 2)]

            mask4 = before[:, :].unsqueeze(1).broadcast_to([P, 4, P])
            for b in range(2):
                dve.wait_ge(sem("sb_q"), b + 1)
                dve.tensor_copy(QKT[:, :, T:2 * T], ps[:, 4:8, T:2 * T]).then_inc(sem("sb_k"), 1)
                dve.wait_ge(sem("sb_ln"), b + 1)
                link(dve.scalar_tensor_tensor(out=T2, in0=ps[:, 0:4, 0:384], scalar=0.0, in1=T1, op0=ALU.max, op1=ALU.add))
                for v in diagonal(T2):
                    dve.tensor_tensor(v, v, mask4, ALU.mult).then_inc(sem("sb_softplus"), 1)
                dve.wait_ge(sem("sb_exp"), b + 1)
                for v in diagonal(T1):
                    dve.scalar_tensor_tensor(out=v, in0=v, scalar=1.0, in1=mask4, op0=ALU.min, op1=ALU.mult).then_inc(sem("sb_a"), 1)
                dve.wait_ge(sem("sb_pv"), b + 1)
                dve.tensor_copy(MIX[:, :, b * 512:(b + 1) * 512].rearrange("p t (h d) -> p h t d", h=4),
                                ps[:, 4:6, :].rearrange("p b (h t d) -> p (b h) t d", h=2, t=TT)).then_inc(sem("sb_out"), 1)

            dve.wait_ge(sem("k_turned"), 1)
            dve.tensor_scalar(KT.rearrange("p b g n -> p (b g n)"), psf[:, 4 * 512:6 * 512], gain_cols[:, G_K:G_K + 1], SCALE, ALU.mult, ALU.mult).then_inc(sem("k_ready"), 1)
            link(dve.tensor_copy(KVC.rearrange("p b g n -> p (b g n)"), psf[:, 6 * 512:8 * 512]))
            dve.wait_ge(sem("blocks_cleared"), 2)
            pe = gain_cols[:, G_PE:G_ALL].unsqueeze(2).broadcast_to([P, CMP_BLOCK, NC])
            for v in range(2):
                for g in range(NG):
                    src = KVC[:, v, g, :]
                    windows = bass.AP(tensor=src.tensor, offset=src.offset, ap=[list(src.ap[0]), [1, CMP_BLOCK], [CMP_STRIDE, NC]])
                    dve.tensor_tensor(BLK[:, v, :, 32 * g:32 * g + NC], windows, pe, ALU.add).then_inc(sem("blocks_ready"), 1)
            dve.wait_ge(sem("cmp_kv"), 1)
            link(dve.tensor_copy(KCV[0:NC].rearrange("p v g n -> p (v g n)"), ps[0:NC, 3, :]))
            link(dve.tensor_tensor(KSQ[0:NC], KCV[0:NC, 0], KCV[0:NC, 0], ALU.mult))
            link(dve.tensor_reduce(kssq[0:NC], KSQ[0:NC], AX_X, ALU.add))
            inverse_rms(krstd[0:NC], kssq[0:NC], HD)
            dve.tensor_tensor(KCV[0:NC, 0], KCV[0:NC, 0], krstd[0:NC].unsqueeze(2).broadcast_to([NC, NG, HD]), ALU.mult).then_inc(sem("kc_ready"), 1)
            dve.wait_ge(sem("kc_turned"), 1)
            dve.tensor_scalar(KCT.rearrange("p g n -> p (g n)"), ps[:, 2, 256:288], gain_cols[:, G_K:G_K + 1], SCALE, ALU.mult, ALU.mult).then_inc(sem("kct_ready"), 1)

            dve.wait_ge(sem("cmp_s"), 1)
            dve.wait_ge(sem("bias_loaded"), 16)
            cp = cmp_p.rearrange("p (h t c) -> p h t c", h=NH, t=TT)
            sc = ps[:, 4, 0:256].rearrange("p (h t c) -> p h t c", h=NH, t=TT)
            for t in range(TT):
                start = CMP_BLOCK - 1 + P * (TT - 1 - t)
                ins = dve.tensor_tensor(cp[:, :, t, :], sc[:, :, t, 0:NC],
                                        BIAS[:, :, start:start + CMP_STRIDE * (NC - 1) + 1:CMP_STRIDE], ALU.add)
            link(ins)
            cpr = cmp_p.rearrange("p (b c) -> p b c", c=NC)
            link(dve.tensor_reduce(row_max, cpr, AX_X, ALU.max))
            dve.tensor_tensor(cpr, cpr, row_max.unsqueeze(2).broadcast_to([P, 16, NC]), ALU.subtract).then_inc(sem("cmp_shifted"), 1)
            dve.wait_ge(sem("cmp_exp"), 1)
            link(dve.tensor_reduce(row_sum, cpr, AX_X, ALU.add))
            flag("cmp_summed")
            link(dve.reciprocal(row_sum, row_sum))
            rs = row_sum.rearrange("p (h t) -> p h t", t=TT)
            cf = coef.rearrange("p (h t) -> p h t", t=TT)
            link(dve.tensor_tensor(cf, rs, gate[:, :, :, 0].rearrange("p t h -> p h t"), ALU.mult))
            link(dve.tensor_scalar(cf[:, :, 0], cf[:, :, 0], has_block, None, ALU.mult))
            dve.wait_ge(sem("cmp_pv"), 1)
            nsa = MIX[:, :, 1024:2048]
            link(dve.tensor_tensor(nsa.rearrange("p t (h d) -> p h t d", h=NH),
                                   psf[:, 2048:4096].rearrange("p (h t d) -> p h t d", h=NH, t=TT),
                                   cf.unsqueeze(3).broadcast_to([P, NH, TT, HD]), ALU.mult))
            flag("cmp_out")

            for r in range(4):
                branch, b = divmod(r, 2)
                dve.wait_ge(sem("ns_s"), r + 1)
                dve.tensor_tensor(T1[:, :, 0:P], ps[:, 0:4, 0:P], BIAS[:, 4 * b:4 * b + 4, P:2 * P], ALU.add)
                link(dve.tensor_tensor(T1[:, :, P:3 * P], ps[:, 0:4, P:3 * P], BIAS[:, 4 * b:4 * b + 4, 0:2 * P], ALU.add))
                m = row_max[:, 0:8].rearrange("p (t h) -> p t h", t=TT)
                s4 = row_sum[:, 0:8].rearrange("p (t h) -> p t h", t=TT)
                dve.tensor_reduce(m[:, 0, :], T1[:, :, 0:P], AX_X, ALU.max)
                link(dve.tensor_reduce(m[:, 1, :], T1[:, :, P:3 * P], AX_X, ALU.max))
                dve.tensor_tensor(T1[:, :, 0:P], T1[:, :, 0:P], m[:, 0, :].unsqueeze(2).broadcast_to([P, 4, P]), ALU.subtract)
                dve.tensor_tensor(T1[:, :, P:3 * P], T1[:, :, P:3 * P], m[:, 1, :].unsqueeze(2).broadcast_to([P, 4, 2 * P]), ALU.subtract).then_inc(sem("ns_shifted"), 1)
                dve.wait_ge(sem("ns_exp"), r + 1)
                dve.tensor_reduce(s4[:, 0, :], T1[:, :, 0:P], AX_X, ALU.add)
                link(dve.tensor_reduce(s4[:, 1, :], T1[:, :, P:3 * P], AX_X, ALU.add))
                link(dve.reciprocal(row_sum[:, 0:8], row_sum[:, 0:8]))
                cf4 = coef[:, 0:8].rearrange("p (t h) -> p t h", t=TT)
                link(dve.tensor_tensor(cf4, s4, gate[:, :, 4 * b:4 * b + 4, 1 + branch], ALU.mult))
                dve.wait_ge(sem("ns_pv"), r + 1)
                link(dve.tensor_tensor(TMP.rearrange("p (h t d) -> p h t d", h=4, t=TT),
                                       psf[:, 3072:4096].rearrange("p (h t d) -> p h t d", h=4, t=TT),
                                       cf4.rearrange("p t h -> p h t").unsqueeze(3).broadcast_to([P, 4, TT, HD]), ALU.mult))
                flag("ns_out")
                v = nsa[:, :, b * 512:(b + 1) * 512].rearrange("p t (h d) -> p h t d", h=4)
                link(dve.tensor_tensor(v, v, TMP.rearrange("p (h t d) -> p h t d", h=4, t=TT), ALU.add))

            normed_rows(MIX, 2)
            turned_lo(1, G_MIX)

            def to_x1(c):
                dve.wait_ge(split_free, SP_OUT + (c + 1) * STEPS_PER_CHUNK + 2)
                v = X[:, :, c * CHUNK:(c + 1) * CHUNK]
                dve.tensor_tensor(v, v, bank_pair((CH_OUT + c) % 2, CHUNK), ALU.add).then_inc(sem("x1_ready"), 1)
                dve.sem_inc(acc_free, 1)

            for c in range(W_CHUNKS):
                for s in range(STEPS_PER_CHUNK):
                    lo(s % RAW, SP_OUT + c * STEPS_PER_CHUNK + s)
                    if s == 1 and c:
                        to_x1(c - 1)
            to_x1(W_CHUNKS - 1)
            dve.wait_ge(sem("x1_ready"), W_CHUNKS)
            normed_rows(X, 1)
            turned_lo(2, G_NORM2)

            def to_q(c):
                dve.wait_ge(split_free, SP_QUERY + (c + 1) * STEPS_PER_CHUNK + 2)
                dve.tensor_copy(Q[:, :, c * CHUNK:(c + 1) * CHUNK], bank_pair((CH_QUERY + c) % 2, CHUNK)).then_inc(acc_free, 1)

            for c in range(W_CHUNKS):
                for s in range(STEPS_PER_CHUNK):
                    lo(s % RAW, SP_QUERY + c * STEPS_PER_CHUNK + s)
                    if s == 1 and c:
                        to_q(c - 1)
            to_q(W_CHUNKS - 1)

            dve.wait_ge(sem("scores"), 1)
            link(dve.tensor_copy(S.rearrange("p t w n -> p (t w n)"), psf[:, :]))
            flag("scores_read")

            def unit_part(i, j, u):
                dve.wait_ge(hi_done, i * UNITS + j * UNITS + u + SP_U + 1)
                dve.tensor_tensor(unit_lo[:, u * UNIT:(u + 1) * UNIT], ps[:, u, :],
                                  unit_hi[:, u * UNIT:(u + 1) * UNIT].bitcast(F32), ALU.subtract).then_inc(split_done, 1)

            def s_sum_of(i, j):
                dve.wait_ge(split_free, i * UNITS + (j + 1) * UNITS + SP_U + 2)
                dve.wait_ge(sem("acted"), i + j + 1)
                dve.tensor_copy(s_sum[:, j % 2, :], ps[:, 4 + j % 2, 0:T]).then_inc(sem("s_copied"), 1)
                dve.wait_ge(sem("s_copied"), i + j + 1)
                dve.tensor_tensor(s_sum[:, j % 2, :], s_sum[:, j % 2, :], ps[:, 4 + j % 2, T:2 * T], ALU.add).then_inc(sem("s_summed"), 1)

            def head_part(head, part):
                def done(ins):
                    ins.then_inc(sem("head_step"), 1)

                def after(k):
                    dve.wait_ge(sem("head_step"), head * HEAD_OPS + k)

                def after_apart(k):
                    after(k)
                    dve.sem_inc(sem("head_waits"), 1)

                picks = [PICK[:, s].rearrange("p t h k -> p (t h k)")[:, bass.ds(head * TOPK, TOPK)] for s in range(3)]
                lo8, hi8 = slice(0, 8), slice(8, 16)
                if part == 0:
                    done(dve.tensor_copy(head_s.rearrange("p s n -> p (s n)"),
                                         S.rearrange("p t w n -> p (t w n)")[:, bass.ds(head * (2 * NKEYS), 2 * NKEYS)]))
                    after_apart(1)
                    for s in range(2):
                        done(dve.max(head_top[:, s, lo8], head_s[:, s, :]))
                elif part == 1:
                    after_apart(3)
                    for s in range(2):
                        done(dve.max_index(head_topi[:, s, lo8], head_top[:, s, lo8], head_s[:, s, :]))
                    after_apart(5)
                    for s in range(2):
                        done(dve.match_replace(head_s[:, s, :], head_top[:, s, lo8], head_s[:, s, :], -3.0e38))
                elif part == 2:
                    after_apart(7)
                    for s in range(2):
                        done(dve.max(head_top[:, s, hi8], head_s[:, s, :]))
                    after_apart(9)
                    for s in range(2):
                        done(dve.max_index(head_topi[:, s, hi8], head_top[:, s, hi8], head_s[:, s, :]))
                elif part == 3:
                    after(11)
                    done(dve.tensor_copy(head_topf, head_topi))
                    done(dve.tensor_tensor(head_sums.rearrange("p (a b) -> p a b", a=TOPK),
                                           head_top[:, 0, :].unsqueeze(2).broadcast_to([P, TOPK, TOPK]),
                                           head_top[:, 1, :].unsqueeze(1).broadcast_to([P, TOPK, TOPK]), ALU.add))
                elif part == 4:
                    after_apart(13)
                    done(dve.max(head_best[:, lo8], head_sums))
                    after_apart(14)
                    done(dve.max_index(head_pos[:, lo8], head_best[:, lo8], head_sums))
                    after_apart(15)
                    done(dve.match_replace(head_sums, head_best[:, lo8], head_sums, -3.0e38))
                elif part == 5:
                    after_apart(16)
                    done(dve.max(head_best[:, hi8], head_sums))
                    after_apart(17)
                    done(dve.max_index(head_pos[:, hi8], head_best[:, hi8], head_sums))
                elif part == 6:
                    after(18)
                    done(dve.tensor_scalar(head_ab[:, 0, :], head_pos, 4, None, ALU.logical_shift_right))
                    done(dve.tensor_scalar(head_ab[:, 1, :], head_pos, 15, None, ALU.bitwise_and))
                    done(dve.tensor_tensor(picks[2], head_best, head_best[:, 0:1].broadcast_to([P, TOPK]), ALU.subtract))
                    after(20)
                    done(dve.tensor_copy(head_abf, head_ab))
                else:
                    after(22)
                    for s in range(2):
                        done(dve.tensor_tensor(head_eq[:, s], head_abf[:, s, :].unsqueeze(2).broadcast_to([P, TOPK, TOPK]),
                                               iota[:, 0:TOPK].unsqueeze(1).broadcast_to([P, TOPK, TOPK]), ALU.is_equal))
                    after(24)
                    for s in range(2):
                        done(dve.tensor_tensor(head_eq[:, s], head_eq[:, s], head_topf[:, s, :].unsqueeze(1).broadcast_to([P, TOPK, TOPK]), ALU.mult))
                    after(26)
                    for s in range(2):
                        done(dve.tensor_reduce(picks[s], head_eq[:, s], AX_X, ALU.add))

            def route_tiles(head, first):
                i = head * TILES_PER_HEAD
                for j in range(TILES_PER_HEAD):
                    for u in range(UNITS):
                        unit_part(i, j, u)
                        if u == 1:
                            if not (first and not j):
                                s_sum_before(i, j)
                            head_part(head, 2 * j)
                        if u == 3:
                            head_part(head, 2 * j + 1)

            def s_sum_before(i, j):
                dve.wait_ge(split_free, i * UNITS + j * UNITS + SP_U + 2)
                dve.wait_ge(sem("acted"), i + j)
                k = (j + 1) % 2
                dve.tensor_copy(s_sum[:, k, :], ps[:, 4 + k, 0:T]).then_inc(sem("s_copied"), 1)
                dve.wait_ge(sem("s_copied"), i + j)
                dve.tensor_tensor(s_sum[:, k, :], s_sum[:, k, :], ps[:, 4 + k, T:2 * T], ALU.add).then_inc(sem("s_summed"), 1)

            route_tiles(0, True)
            with dve.Fori(1, HEADS) as head:
                route_tiles(head, False)
            s_sum_before(ROUTE_TILES, 0)
            dve.wait_ge(sem("head_step"), HEADS * HEAD_OPS)
            dve.sem_inc(sem("best_shifted"), 1)
            dve.wait_ge(sem("best_exp"), 1)
            pick_g = PICK[:, 2].rearrange("p t h k -> p (t h) k")
            gsum = GSUM.rearrange("p t h -> p (t h)")
            link(dve.tensor_reduce(gsum, pick_g, AX_X, ALU.add))
            link(dve.reciprocal(gsum, gsum))
            link(dve.tensor_tensor(pick_g, pick_g, gsum.unsqueeze(2).broadcast_to([P, HEADS, TOPK]), ALU.mult))
            flag("picks")
            dve.wait_ge(sem("picks_turned"), 1)
            dve.tensor_copy(picked[:, 0, :], ps[:, 6, 0:T]).then_inc(sem("picked_ready"), 1)
            dve.tensor_copy(picked[:, 2, :], ps[:, 6, T:2 * T]).then_inc(sem("picked_ready"), 1)
            dve.tensor_copy(picked[:, 1, :], ps[:, 7, 0:T]).then_inc(sem("picked_ready"), 1)
            dve.wait_ge(sem("picked_ready"), 3)

            def first_onehot(s, j):
                dve.wait_ge(sem("gates_mm"), s + j + 1)
                for c in range(TOKENS_PER_BANK):
                    col = s * TOKENS_PER_BANK + j * TOKENS_PER_BANK + c
                    ins = dve.tensor_scalar(one_i[:, j, c * P:(c + 1) * P], iota[:, :], picked[:, 0, bass.ds(col, 1)],
                                            picked[:, 2, bass.ds(col, 1)], ALU.is_equal, ALU.mult)
                ins.then_inc(sem("onehot_i"), 1)

            def apply_gates(s, j):
                dve.wait_ge(sem("gates_mm"), s + j + 2)
                v = WACT_C[:, bass.ds(s * TOKENS_PER_BANK + (j - 1) * TOKENS_PER_BANK, TOKENS_PER_BANK), :]
                dve.tensor_tensor(v, v, ps[:, 6 + (j + 1) % 2, :].rearrange("p (c i) -> p c i", c=TOKENS_PER_BANK), ALU.mult).then_inc(sem("gates_built"), 1)

            def apply_act(s, j):
                dve.wait_ge(sem("acted"), s + j + ROUTE_TILES + 2)
                v = WACT[:, bass.ds(s + j + (ROUTE_TILES - 1), 1), :].rearrange("p a c -> p (a c)")
                dve.wait_ge(sem("gates_built"), s + j + 2)
                dve.tensor_tensor(v, v, s_sum[:, (j + 1) % 2, :], ALU.mult).then_inc(sem("act_applied"), 1)

            def build_tile(s, j, first):
                i = s + ROUTE_TILES
                unit_part(i, j, 0)
                first_onehot(s, j)
                unit_part(i, j, 1)
                if not (first and not j):
                    s_sum_before(i, j)
                    unit_part(i, j, 2)
                    if first:
                        dve.wait_ge(sem("gates_cleared"), 1)
                    else:
                        dve.wait_ge(sem("act_applied"), s + j - 1)
                    apply_gates(s, j)
                    unit_part(i, j, 3)
                    apply_act(s, j)
                else:
                    unit_part(i, j, 2)
                    unit_part(i, j, 3)

            for j in range(2):
                build_tile(0, j, True)
            with dve.Fori(1, BUILD_STEPS // 2) as pair:
                for j in range(2):
                    build_tile(pair * 2, j, False)
            s_sum_before(NE_T, 0)
            dve.wait_ge(sem("act_applied"), BUILD_STEPS - 1)
            apply_gates(BUILD_STEPS, 0)
            apply_act(BUILD_STEPS, 0)

            with dve.Fori(0, NE_T // 2) as pair:
                i = pair * 2
                for j in range(2):
                    dve.wait_ge(sem("w_hi_done"), i + j + 1)
                    dve.tensor_tensor(w_lo[:, j, :], WACT[:, bass.ds(i + j, 1), :].rearrange("p a c -> p (a c)"),
                                      w_hi[:, j, :].bitcast(F32), ALU.subtract).then_inc(sem("w_lo_done"), 1)
                    for f in range(2):
                        dve.wait_ge(hi_done, i * 2 + 2 * j + f + SP_V + 1)
                        dve.tensor_tensor(split_lo[:, f, :], raw[:, 2 * j + f, :],
                                          split_hi[:, f, :].bitcast(F32), ALU.subtract).then_inc(split_done, 1)
            dve.wait_ge(sem("x1_loaded"), 16)
            dve.wait_ge(split_free, SP_V + E_STEPS + 2)
            for t in range(TT):
                dve.tensor_tensor(X1[:, t, :], X1[:, t, :], psf[:, t * D:(t + 1) * D], ALU.add).then_inc(sem("out_ready"), 1)

        @block.tensor
        def _(pe):
            def turn_rows(use):
                pe.wait_ge(sem("rows_normed"), use + 1)
                for k in range(KC):
                    for t in range(TT):
                        ins = pe.transpose(psf[:, k * T + t * P:k * T + (t + 1) * P], XN[:, t, k * P:(k + 1) * P], ident[:, :])
                    if k % 2:
                        ins.then_inc(sem("rows_turned"), 1)

            def gemm_step(acc, slot, ks, width, n, last):
                pe.wait_ge(split_done, n + 1)
                for j, k in enumerate(ks):
                    w_h = split_hi[:, slot, j * width:(j + 1) * width]
                    w_l = split_lo[:, slot, j * width:(j + 1) * width]
                    for t in range(TT):
                        h_h = ht[:, k, t * P:(t + 1) * P]
                        h_l = ht[:, k, T + t * P:T + (t + 1) * P]
                        pe.matmul(acc[t], h_h, w_h, start=k == 0, stop=False)
                        pe.matmul(acc[t], h_h, w_l, start=False, stop=False)
                        ins = pe.matmul(acc[t], h_l, w_h, start=False, stop=k == KC - 1)
                ins.then_inc(split_free, 1)

            def gemm_chunk(ch, parity, n0):
                pe.wait_ge(acc_free, ch + 1)
                acc = [ps[:, 2 * parity + t, :] for t in range(TT)]
                for s in range(STEPS_PER_CHUNK):
                    gemm_step(acc, s % SPLIT, (2 * s, 2 * s + 1), CHUNK, n0 + s, s == STEPS_PER_CHUNK - 1)

            pe.sem_inc(split_free, 2)
            pe.wait_ge(sem("constants"), 11)
            pe.wait_ge(sem("gains_loaded"), 16 * 7)
            pe.transpose(psf[:, 0:G_ALL], gain_rows[0:G_ALL, :], ident[0:G_ALL, 0:G_ALL]).then_inc(sem("gains_turned"), 1)
            pe.wait_ge(sem("table_loaded"), 32)
            pe.matmul(ps[0:NH, 7, :], TABLE, ONEHOT, start=True, stop=True).then_inc(sem("bias_mm"), 1)
            pe.wait_ge(sem("gains_ready"), 1)
            pe.wait_ge(sem("bias_rows"), 1)
            turn_rows(0)
            pe.wait_ge(sem("ht_lo"), KC)
            with pe.Fori(0, W_IN_CHUNKS // 2) as pair:
                c = pair * 2
                gemm_chunk(c, 0, c * STEPS_PER_CHUNK + SP_IN)
                gemm_chunk(c + 1, 1, c * STEPS_PER_CHUNK + STEPS_PER_CHUNK + SP_IN)
            gemm_chunk(W_IN_CHUNKS - 1, 0, SP_TAIL - STEPS_PER_CHUNK)
            pe.wait_ge(acc_free, CH_TAIL + 1)
            for s in range(TAIL_STEPS):
                gemm_step([ps[:, 2 + t, 0:N_GATES] for t in range(TT)], s % SPLIT,
                          range(TAIL_K * s, TAIL_K * (s + 1)), N_GATES, SP_TAIL + s, s == TAIL_STEPS - 1)

            pe.wait_ge(acc_free, 2 + CH_TAIL + 1)
            for b in range(2):
                if b:
                    pe.wait_ge(sem("sb_out"), b)
                for h in range(4):
                    for s, col in enumerate((COL_QSB, COL_KSB)):
                        for t in range(TT):
                            c = col + (4 * b + h) * HD
                            ins = pe.transpose(ps[:, 4 + h, s * T + t * P:s * T + (t + 1) * P], PROJ[:, t, c:c + HD], ident[:, :])
                ins.then_inc(sem("sb_turned"), 1)
                pe.wait_ge(sem("sb_q"), b + 1)
                pe.wait_ge(sem("sb_k"), b + 1)
                for h in range(4):
                    pe.matmul(ps[:, h, 0:T], QKT[:, h, T:T + P], QKT[:, h, 0:T], start=True, stop=False, skip_group_check=True)
                    ins = pe.matmul(ps[:, h, T:T + P], QKT[:, h, T + P:2 * T], QKT[:, h, P:T], start=False, stop=False, skip_group_check=True)
                ins.then_inc(sem("sb_z"), 1)
                pe.wait_ge(sem("sb_softplus"), 2 * b + 2)
                for h in range(4):
                    pe.matmul(ps[:, h, 0:T], neg_tri[:, :], T2[:, h, 0:T], start=False, stop=False, skip_group_check=True)
                    pe.matmul(ps[:, h, P:T], neg_ones[:, :], T2[:, h, T:T + P], start=False, stop=False, skip_group_check=True)
                    ins = pe.matmul(ps[:, h, T:T + P], neg_tri[:, :], T2[:, h, T:T + P], start=False, stop=True, skip_group_check=True)
                ins.then_inc(sem("sb_cumsum"), 1)
                pe.wait_ge(sem("sb_a"), 2 * b + 2)
                for h in range(4):
                    c = COL_VSB + (4 * b + h) * HD
                    o = ps[:, 4 + h // 2, (h % 2) * T:(h % 2 + 1) * T]
                    pe.matmul(o[:, 0:P], T1[:, h, 0:P], PROJ[:, 0, c:c + HD], start=True, stop=True)
                    pe.matmul(o[:, P:T], T1[:, h, P:T], PROJ[:, 0, c:c + HD], start=True, stop=False)
                    ins = pe.matmul(o[:, P:T], T1[:, h, T:T + P], PROJ[:, 1, c:c + HD], start=False, stop=True)
                ins.then_inc(sem("sb_pv"), 1)

            pe.wait_ge(sem("nsa_normed"), 1)
            pe.wait_ge(sem("sb_out"), 2)
            for h in range(NH):
                for t in range(TT):
                    c = COL_Q + h * HD
                    ins = pe.transpose(psf[:, h * T + t * P:h * T + (t + 1) * P], PROJ[:, t, c:c + HD], ident[:, :])
            ins.then_inc(sem("q_turned"), 1)
            for b, col in enumerate((COL_KSLC, COL_KWIN, COL_KCMP, COL_VCMP)):
                for g in range(NG):
                    for t in range(TT):
                        c = col + g * HD
                        ins = pe.transpose(ps[:, 4 + b, g * T + t * P:g * T + (t + 1) * P], PROJ[:, t, c:c + HD], ident[:, :])
            ins.then_inc(sem("k_turned"), 1)
            pe.wait_ge(sem("q_ready"), 1)
            pe.wait_ge(sem("blocks_ready"), 4)
            for s in range(CMP_STEPS):
                v = 2 * s // CMP_STEPS
                loaded(pe, s % RAW, RAW_CMP + s)
                for j in range(CMP_L):
                    l = CMP_L * (s % (CMP_STEPS // 2)) + j
                    ins = pe.matmul(ps[0:64, v, 0:CMP_HIDDEN], BLK[:, v, l, :], raw[:, s % RAW, j * CMP_HIDDEN:(j + 1) * CMP_HIDDEN],
                                    start=l == 0, stop=l == CMP_BLOCK - 1)
                ins.then_inc(cmp_used, 1)
            pe.wait_ge(sem("hidden"), 1)
            for v in range(2):
                for f in range(2):
                    ins = pe.transpose(ps[:, 2, (2 * v + f) * 64:(2 * v + f + 1) * 64], HG[0:64, v, f * P:(f + 1) * P], ident[0:64, 0:64])
            ins.then_inc(sem("hidden_turned"), 1)
            pe.wait_ge(sem("hidden_t"), 1)
            pe.wait_ge(sem("w2_loaded"), 32)
            for v in range(2):
                for g in range(NG):
                    for f in range(2):
                        ins = pe.matmul(ps[0:NC, 3, (v * NG + g) * HD:(v * NG + g + 1) * HD], HGT[:, 2 * v + f, 32 * g:32 * g + NC],
                                        W2S[:, 2 * v + f, :], start=f == 0, stop=f == 1)
            ins.then_inc(sem("cmp_kv"), 1)
            pe.wait_ge(sem("kc_ready"), 1)
            for g in range(NG):
                ins = pe.transpose(ps[:, 2, 256 + 16 * g:256 + 16 * g + NC], KCV[0:NC, 0, g, :], ident[0:NC, 0:NC])
            ins.then_inc(sem("kc_turned"), 1)
            pe.wait_ge(sem("kct_ready"), 1)
            for h in range(NH):
                for t in range(TT):
                    o = (h * TT + t) * 16
                    ins = pe.matmul(ps[:, 4, o:o + NC], QT[:, h, t * P:(t + 1) * P], KCT[:, h // GROUP, 0:NC], start=True, stop=True)
            ins.then_inc(sem("cmp_s"), 1)
            pe.wait_ge(sem("cmp_exp"), 1)
            for b in range(16):
                ins = pe.transpose(psf[0:NC, b * P:(b + 1) * P], cmp_p[:, b * NC:(b + 1) * NC], ident[:, :])
            ins.then_inc(sem("cmp_p_turned"), 1)
            pe.wait_ge(sem("cmp_pt"), 1)
            for b in range(16):
                ins = pe.matmul(psf[:, 2048 + b * P:2048 + (b + 1) * P], PCT[0:NC, b, :], KCV[0:NC, 1, b // TT // GROUP, :], start=True, stop=True)
            ins.then_inc(sem("cmp_pv"), 1)

            pe.wait_ge(sem("cmp_out"), 1)
            pe.wait_ge(sem("k_ready"), 1)
            for r in range(4):
                branch, b = divmod(r, 2)
                v_col = (COL_VSLC, COL_VWIN)[branch] + b * HD
                for h in range(4):
                    pe.matmul(ps[:, h, 0:P], QT[:, 4 * b + h, 0:P], KT[:, branch, b, 0:P], start=True, stop=True)
                    ins = pe.matmul(ps[:, h, P:3 * P], QT[:, 4 * b + h, P:T], KT[:, branch, b, :], start=True, stop=True)
                ins.then_inc(sem("ns_s"), 1)
                pe.wait_ge(sem("ns_exp"), r + 1)
                if r:
                    pe.wait_ge(sem("ns_out"), r)
                for j in range(12):
                    ins = pe.transpose(ps[:, 4 + j // 4, (j % 4) * P:(j % 4 + 1) * P], T1[:, j // 3, (j % 3) * P:(j % 3 + 1) * P], ident[:, :])
                ins.then_inc(sem("ns_p_turned"), 1)
                pe.wait_ge(sem("ns_pt"), r + 1)
                for h in range(4):
                    o = 3072 + h * T
                    pe.matmul(psf[:, o:o + P], T2b[:, 3 * h, :], PROJ[:, 0, v_col:v_col + HD], start=True, stop=True)
                    pe.matmul(psf[:, o + P:o + T], T2b[:, 3 * h + 1, :], PROJ[:, 0, v_col:v_col + HD], start=True, stop=False)
                    ins = pe.matmul(psf[:, o + P:o + T], T2b[:, 3 * h + 2, :], PROJ[:, 1, v_col:v_col + HD], start=False, stop=True)
                ins.then_inc(sem("ns_pv"), 1)

            turn_rows(1)
            pe.wait_ge(sem("ht_lo"), 2 * KC)
            with pe.Fori(0, W_CHUNKS // 2) as pair:
                c = pair * 2
                gemm_chunk(c + CH_OUT, CH_OUT % 2, c * STEPS_PER_CHUNK + SP_OUT)
                gemm_chunk(c + CH_OUT + 1, 1 - CH_OUT % 2, c * STEPS_PER_CHUNK + STEPS_PER_CHUNK + SP_OUT)
            turn_rows(2)
            pe.wait_ge(sem("ht_lo"), 3 * KC)
            with pe.Fori(0, W_CHUNKS // 2) as pair:
                c = pair * 2
                gemm_chunk(c + CH_QUERY, CH_QUERY % 2, c * STEPS_PER_CHUNK + SP_QUERY)
                gemm_chunk(c + CH_QUERY + 1, 1 - CH_QUERY % 2, c * STEPS_PER_CHUNK + STEPS_PER_CHUNK + SP_QUERY)

            pe.wait_ge(acc_free, 2 + CH_QUERY + W_CHUNKS)
            for w in range(HP):
                for t in range(TT):
                    ins = pe.transpose(psf[:, w * T + t * P:w * T + (t + 1) * P], Q[:, t, w * P:(w + 1) * P], ident[:, :])
                if w % 8 == 7:
                    ins.then_inc(sem("pq_turned"), 1)
            pe.wait_ge(sem("keys_loaded"), 16)
            pe.wait_ge(sem("pq_ready"), 1)
            for w in range(HP):
                ins = pe.transpose(psf[:, w * P:(w + 1) * P], SK[:, w, :], ident[:, :])
            ins.then_inc(sem("keys_turned"), 1)
            pe.wait_ge(sem("keys_ready"), 1)
            pe.wait_ge(sem("pq_ready"), 2)
            for t in range(TT):
                for w in range(HP):
                    o = (t * HP + w) * P
                    ins = pe.matmul(psf[:, o:o + P], PQT[:, w, t * P:(t + 1) * P], SKT[:, w, :], start=True, stop=True)
            ins.then_inc(sem("scores"), 1)
            pe.wait_ge(sem("scores_read"), 1)

            pe.sem_inc(sem("s_summed"), 2)
            pe.sem_inc(sem("acted"), 2)

            def turn_unit(i, j, u):
                slot = 2 * (j % 2) + u // 2
                if u % 2 == 0:
                    pe.wait_ge(raw_loaded[slot], i * 8 + 16 * (j // 2 + RAW_U // RAW + 1))
                pe.wait_ge(split_done, i * UNITS + j * UNITS + u + SP_U - 3)
                for k in range(UNIT_K):
                    c = (u % 2) * UNIT + k * P
                    ins = pe.transpose(ps[:, u, k * P:(k + 1) * P], raw[:, slot, c:c + P], ident[:, :])
                ins.then_inc(u_turned, 1)

            def u_tile(i, j, last=False):
                for u in range(UNITS):
                    if not (last and u >= 2):
                        turn_unit(i, j + (u + 2) // UNITS, (u + 2) % UNITS)
                    if u == 0:
                        pe.wait_ge(sem("s_summed"), i + j + 1)
                    pe.wait_ge(split_done, i * UNITS + j * UNITS + u + SP_U + 1)
                    acc = ps[:, 4 + j % 2, :]
                    for k in range(UNIT_K):
                        kk = UNIT_K * u + k
                        c = u * UNIT + k * P
                        pe.matmul(acc, unit_hi[:, c:c + P], ht[:, kk, :], start=kk == 0, stop=False, skip_group_check=True)
                        ins = pe.matmul(acc[:, T:2 * T], unit_lo[:, c:c + P], ht[:, kk, 0:T], start=False, stop=kk == KC - 1, skip_group_check=True)
                    ins.then_inc(split_free, 1)

            turn_unit(0, 0, 0)
            turn_unit(0, 0, 1)
            with pe.Fori(0, HEADS) as head:
                for j in range(TILES_PER_HEAD):
                    u_tile(head * TILES_PER_HEAD, j)
            pe.wait_ge(sem("picks"), 1)
            for s, (bank, o) in enumerate(((6, 0), (7, 0), (6, T))):
                for t in range(TT):
                    ins = pe.transpose(ps[:, bank, o + t * P:o + (t + 1) * P], PICK[:, s, t].rearrange("p h k -> p (h k)"), ident[:, :])
            ins.then_inc(sem("picks_turned"), 1)
            pe.wait_ge(sem("picked_ready"), 3)

            pe.sem_inc(sem("gates_mm"), 2)
            pe.sem_inc(sem("gates_built"), 2)

            def build_step(s, j):
                pe.wait_ge(sem("onehot_i"), s + j + 1)
                pe.wait_ge(sem("onehot_j"), s + j + 1)
                pe.wait_ge(sem("gates_built"), s + j + 1)
                for c in range(TOKENS_PER_BANK):
                    ins = pe.matmul(ps[:, 6 + j, c * P:(c + 1) * P], one_j[j][:, c * P:(c + 1) * P].bitcast(F32),
                                    one_i[:, j, c * P:(c + 1) * P], start=True, stop=True)
                ins.then_inc(sem("gates_mm"), 1)

            with pe.Fori(0, BUILD_STEPS // 2 - 1) as pair:
                for j in range(2):
                    u_tile(pair * 2 + ROUTE_TILES, j)
                    build_step(pair * 2, j)
            for j in range(2):
                u_tile(NE_T - 2, j, last=j == 1)
                build_step(BUILD_STEPS - 2, j)
            pe.wait_ge(sem("gates_built"), BUILD_STEPS + 2)

            def v_tile(i, j, first, last):
                pe.wait_ge(sem("w_lo_done"), i + j + 1)
                for f in range(2):
                    pe.wait_ge(split_done, i * 2 + 2 * j + f + SP_V + 1)
                    for t in range(TT):
                        g_h = w_hi[:, j, t * P:(t + 1) * P]
                        g_l = w_lo[:, j, t * P:(t + 1) * P]
                        for c in range(2):
                            acc = ps[:, 4 * t + 2 * f + c, :]
                            v_h = split_hi[:, f, c * 512:(c + 1) * 512]
                            v_l = split_lo[:, f, c * 512:(c + 1) * 512]
                            pe.matmul(acc, g_h, v_h, start=first, stop=False)
                            pe.matmul(acc, g_h, v_l, start=False, stop=False)
                            ins = pe.matmul(acc, g_l, v_h, start=False, stop=last)
                    ins.then_inc(split_free, 1)

            v_tile(0, 0, True, False)
            v_tile(0, 1, False, False)
            with pe.Fori(1, NE_T // 2 - 1) as pair:
                i = pair * 2
                v_tile(i, 0, False, False)
                v_tile(i, 1, False, False)
            v_tile(NE_T - 2, 0, False, False)
            v_tile(NE_T - 2, 1, False, True)


_INS = ['x', 'norm1_g', 'w_in', 'cmp_pe', 'cmp_k_w1', 'cmp_k_w2', 'cmp_v_w1', 'cmp_v_w2', 'q_norm_g', 'k_norm_g',
        'rel_bias_table', 'sb_out_g', 'nsa_out_g', 'w_out', 'norm2_g', 'peer_w_query', 'peer_sub_keys',
        'peer_expert_u', 'peer_expert_v']


def kernel(**inputs):
    import numpy as _np
    import concourse.bacc as _bacc
    from concourse import mybir as _mybir
    from concourse.bass_utils import run_bass_kernel_spmd as _run

    nc = _bacc.Bacc("TRN2", target_bir_lowering=False, num_devices=1)
    arrays, args = {}, []
    for name in _INS:
        a = _np.ascontiguousarray(inputs[name])
        arrays[f"in_{name}"] = a
        args.append(nc.dram_tensor(f"in_{name}", a.shape, _mybir.dt.from_np(a.dtype), kind="ExternalInput").ap())
    a = bucket_onehot()
    arrays["bucket_onehot"] = a
    args.append(nc.dram_tensor("bucket_onehot", a.shape, _mybir.dt.from_np(a.dtype), kind="ExternalInput").ap())
    args.append(nc.dram_tensor("out_0", (1, T, D), _mybir.dt.float32, kind="ExternalOutput").ap())
    layer(nc, *args)
    r = _run(nc, [arrays], core_ids=[0])
    return r.results[0]["out_0"]
```

```python
from contextlib import ExitStack

import numpy as np

import concourse.bass as bass
from concourse import mybir

ALU = mybir.AluOpType
ACT = mybir.ActivationFunctionType
F32 = mybir.dt.float32
F32R = mybir.dt.float32r
U32 = mybir.dt.uint32
AX_X = mybir.AxisListType.X

P = 128
T = 256
D = 2048
TT = T // P
KC = D // P
HD = 128
NH = 8
NG = 2
GROUP = NH // NG
IN_COLS = 5656
EPS = 1e-6
NEG = -1e30
SCALE = HD ** -0.5
CMP_BLOCK, CMP_STRIDE, CMP_HIDDEN = 32, 16, 256
NC = (T - CMP_BLOCK) // CMP_STRIDE + 1
N_BUCKETS, MAX_DISTANCE = 32, 128
NKEYS = 128
TOPK = 16
HP = 2 * NH
NE = NKEYS * NKEYS

COL_QSB, COL_KSB, COL_VSB, COL_Q = 0, 1024, 2048, 3072
COL_KCMP, COL_VCMP, COL_KSLC, COL_VSLC, COL_KWIN, COL_VWIN, COL_GATE = 4096, 4352, 4608, 4864, 5120, 5376, 5632
N_GATES = IN_COLS - COL_GATE

G_NORM1, G_NORM2, G_MIX, G_Q, G_K, G_PE = 0, 16, 32, 48, 49, 50
G_ALL = G_PE + CMP_BLOCK

RAW = 4
SPLIT = 2
STEP = 1024
CHUNK = 512
W_IN_CHUNKS = COL_GATE // CHUNK
STEPS_PER_CHUNK = D * CHUNK // P // STEP
TAIL_STEPS = 2
TAIL_K = KC // TAIL_STEPS
W_CHUNKS = D // CHUNK
CMP_STEPS = 2 * CMP_BLOCK * HD * CMP_HIDDEN // P // STEP
CMP_L = STEP // CMP_HIDDEN
E_STEPS = 2 * NE // P
UNIT = 512
UNITS = D // UNIT
UNIT_K = UNIT // P
U_UNITS = UNITS * NE // P

RAW_IN = 0
RAW_CMP = RAW_IN + W_IN_CHUNKS * STEPS_PER_CHUNK
RAW_OUT = RAW_CMP + CMP_STEPS
RAW_QUERY = RAW_OUT + W_CHUNKS * STEPS_PER_CHUNK
RAW_U = RAW_QUERY + W_CHUNKS * STEPS_PER_CHUNK
RAW_V = RAW_U + E_STEPS

SP_IN = 0
SP_TAIL = SP_IN + W_IN_CHUNKS * STEPS_PER_CHUNK
SP_OUT = SP_TAIL + TAIL_STEPS
SP_QUERY = SP_OUT + W_CHUNKS * STEPS_PER_CHUNK
SP_U = SP_QUERY + W_CHUNKS * STEPS_PER_CHUNK
SP_V = SP_U + U_UNITS

CH_IN, CH_TAIL, CH_OUT = 0, W_IN_CHUNKS, W_IN_CHUNKS + 1
CH_QUERY = CH_OUT + W_CHUNKS

BIAS_W = 512
BESIDE = 3
BESIDE_STEPS = BESIDE * STEPS_PER_CHUNK
FIRST_BESIDE = W_IN_CHUNKS - BESIDE
ROUNDS = 2 * NH // 2
NE_T = NE // P
TOKENS_PER_BANK = 4
BUILD_STEPS = T // TOKENS_PER_BANK
HEADS = TT * NH
TILES_PER_HEAD = 4
ROUTE_TILES = HEADS * TILES_PER_HEAD
assert NE_T - ROUTE_TILES == BUILD_STEPS
HEAD_OPS = 28


def bucket_onehot():
    dist = np.maximum(T - np.arange(BIAS_W), 0)
    exact = N_BUCKETS // 2
    ratio = np.log(np.maximum(dist, 1).astype(np.float32) / np.float32(exact)) / np.float32(np.log(MAX_DISTANCE / exact))
    large = np.minimum(exact + (ratio * (N_BUCKETS - exact)).astype(np.int32), N_BUCKETS - 1)
    bucket = np.where(dist < exact, dist, large)
    return (np.arange(N_BUCKETS)[:, None] == bucket[None, :]).astype(np.float32)


def layer(nc, x, norm1_g, w_in, cmp_pe, cmp_k_w1, cmp_k_w2, cmp_v_w1, cmp_v_w2, q_norm_g, k_norm_g,
          rel_bias_table, sb_out_g, nsa_out_g, w_out, norm2_g, peer_w_query, peer_sub_keys,
          peer_expert_u, peer_expert_v, onehot, out):
    with ExitStack() as ctx:
        def sb(name, shape, dt=F32):
            return ctx.enter_context(nc.sbuf_tensor(name, shape, dt))

        sems = {}

        def sem(name):
            if name not in sems:
                sems[name] = ctx.enter_context(nc.semaphore(name))
            return sems[name]

        x1_dram = nc.dram_tensor("x1_dram", [T, D], F32, kind="Internal").ap()
        bias_dram = nc.dram_tensor("bias_dram", [NH, P, BIAS_W + 1], F32, kind="Internal").ap()

        big = sb("big", [P, NE_T * T])
        raw = sb("raw", [P, RAW, STEP])
        split_hi = sb("split_hi", [P, SPLIT, STEP], F32R)
        split_lo = sb("split_lo", [P, SPLIT, STEP], F32R)
        ht = sb("ht", [P, KC, 2 * T], F32R)
        ident = sb("ident", [P, P])
        iota = sb("iota", [P, P])
        gain_cols = sb("gain_cols", [P, G_ALL])
        picked = sb("picked", [P, 3, T])
        s_sum = sb("s_sum", [P, 2, T])
        w_hi = sb("w_hi", [P, 2, T], F32R)
        w_lo = sb("w_lo", [P, 2, T], F32R)
        one_i = sb("one_i", [P, 2, TOKENS_PER_BANK * P])
        small = sb("small", [P, 320])
        ps = ctx.enter_context(nc.psum_tensor("ps", [P, 8, 512], F32))
        psf = ps[:, :, :].rearrange("p b n -> p (b n)")

        at = [0]

        def tiny(n):
            at[0] += n
            assert at[0] <= 320
            return small[:, at[0] - n:at[0]]

        ssq = tiny(8)
        x1_ssq = tiny(TT * W_CHUNKS)
        rstd = tiny(8)
        gates = tiny(TT * N_GATES)
        nssq = tiny(24)
        nrstd = tiny(24)
        row_max = tiny(16)
        row_sum = tiny(16)
        coef = tiny(16)
        round_max = tiny(8).rearrange("p (r n) -> p r n", r=2)
        round_neg = tiny(8).rearrange("p (r n) -> p r n", r=2)
        round_sum = tiny(16).rearrange("p (r n) -> p r n", r=4)
        round_coef = tiny(8).rearrange("p (r n) -> p r n", r=2)
        has_block = tiny(1)
        kssq = tiny(2)
        krstd = tiny(2)
        minus_half = tiny(24)

        at_big = [0]

        def part(n, at=None):
            a = at_big[0] if at is None else at
            at_big[0] = a + n
            assert a + n <= NE_T * T
            return big[:, a:a + n]

        X = part(TT * D).rearrange("p (t d) -> p t d", t=TT)
        A_PROJ = TT * D
        PROJ = part(TT * IN_COLS).rearrange("p (t n) -> p t n", t=TT)
        MIX = part(TT * D).rearrange("p (t d) -> p t d", t=TT)
        A_XN = A_PROJ + TT * IN_COLS + TT * D
        XN = part(TT * D).rearrange("p (t d) -> p t d", t=TT)
        QKT = part(4 * 512, A_XN).rearrange("p (h n) -> p h n", h=4)
        T1f = part(4 * 384)
        T2f = part(4 * 384)
        T1 = T1f.rearrange("p (h n) -> p h n", h=4)
        T2 = T2f.rearrange("p (h n) -> p h n", h=4)
        T1r = T1f.rearrange("p (r h n) -> p r h n", r=2, h=2)
        T2r = T2f.rearrange("p (r b n) -> p r b n", r=2, b=6)
        BIAS = part(NH * 384).rearrange("p (h n) -> p h n", h=NH)
        A_QT = at_big[0]
        QT = part(NH * T).rearrange("p (h n) -> p h n", h=NH)
        KT = part(2 * NG * T).rearrange("p (b g n) -> p b g n", b=2, g=NG)
        KVC = part(2 * NG * T).rearrange("p (b g n) -> p b g n", b=2, g=NG)
        W2S = part(512).rearrange("p (w n) -> p w n", w=4)
        neg_tri, neg_ones, before = part(P), part(P), part(P)
        cmp_p = KVC.rearrange("p b g n -> p (b g n)")[:, 0:16 * NC]
        SQ = big[:, A_QT:A_QT + 2048]
        SQK = big[:, A_QT + 2048:A_QT + 3072]
        gain_rows = MIX[:, 0, 1536:1536 + P]
        HG = big[:, A_XN:A_XN + 512].rearrange("p (v n) -> p v n", v=2)
        HGT = big[:, A_XN + 512:A_XN + 768].rearrange("p (w n) -> p w n", w=4)
        KCV = big[:, A_XN + 768:A_XN + 1280].rearrange("p (v g n) -> p v g n", v=2, g=NG)
        KCT = big[:, A_XN + 1280:A_XN + 1312].rearrange("p (g n) -> p g n", g=NG)
        KSQ = big[:, A_XN + 1312:A_XN + 1568].rearrange("p (g n) -> p g n", g=NG)
        GATES_T = big[0:N_GATES, A_XN + 1312:A_XN + 1568]
        BLK = PROJ[:, :, 0:CMP_BLOCK * 64].rearrange("p v (l n) -> p v l n", l=CMP_BLOCK)
        PCT = PROJ[:, 0, 0:2048].rearrange("p (b n) -> p b n", b=16)
        W_TAIL = MIX[:, 1, BIAS_W:BIAS_W + KC * N_GATES].rearrange("p (k n) -> p k n", k=KC)
        tail_raw = MIX[:, 1, BIAS_W:BIAS_W + KC * N_GATES]
        ROWB = MIX[0:NH, 0, 0:BIAS_W]
        TABLE = MIX[0:N_BUCKETS, 0, 1024:1024 + NH]
        ONEHOT = MIX[0:N_BUCKETS, 1, 0:BIAS_W]

        Q = big[:, A_PROJ:A_PROJ + TT * D].rearrange("p (t d) -> p t d", t=TT)
        A_R = ROUTE_TILES * T
        SK = part(2048, A_R).rearrange("p (w n) -> p w n", w=HP)
        SKT = part(2048).rearrange("p (w n) -> p w n", w=HP)
        PQT = part(4096).rearrange("p (w n) -> p w n", w=HP)
        A_S = at_big[0]
        S = part(4096).rearrange("p (t w n) -> p t w n", t=TT, w=HP)
        A_PICK = at_big[0]
        PICK = part(768).rearrange("p (s t h k) -> p s t h k", s=3, t=TT, h=NH)
        GSUM = part(16).rearrange("p (t h) -> p t h", t=TT)
        A_HEAD = at_big[0]
        head_s = part(2 * NKEYS).rearrange("p (s n) -> p s n", s=2)
        head_top = part(2 * TOPK).rearrange("p (s k) -> p s k", s=2)
        head_topi = part(2 * TOPK).bitcast(U32).rearrange("p (s k) -> p s k", s=2)
        head_topf = part(2 * TOPK).rearrange("p (s k) -> p s k", s=2)
        head_sums = part(TOPK * TOPK)
        head_best = part(TOPK)
        head_pos = part(TOPK).bitcast(U32)
        head_ab = part(2 * TOPK).bitcast(U32).rearrange("p (s k) -> p s k", s=2)
        head_abf = part(2 * TOPK).rearrange("p (s k) -> p s k", s=2)
        head_eq = part(2 * TOPK * TOPK).rearrange("p (s k a) -> p s k a", s=2, k=TOPK)
        A_ROUTED = at_big[0]

        WACT = big[:, :].rearrange("p (i c) -> p i c", c=T)
        WACT_C = big[:, :].rearrange("p (i c) -> p c i", c=T)
        one_j = [w[:, :, :].rearrange("p a b -> p (a b)") for w in (w_hi, w_lo)]
        unit_hi = split_hi[:, :, :].rearrange("p s n -> p (s n)")
        unit_lo = split_lo[:, :, :].rearrange("p s n -> p (s n)")
        X1 = big[:, 0:TT * D].rearrange("p (t d) -> p t d", t=TT)

        x_rows = x.rearrange("b (t p) d -> p (b t) d", p=P)
        x1_rows = x1_dram.rearrange("(t p) d -> p t d", p=P)
        out_rows = out.rearrange("b (t p) d -> p (b t) d", p=P)
        win_k = w_in[0].rearrange("(k p) n -> p k n", p=P)
        wout_k = w_out[0].rearrange("(k p) n -> p k n", p=P)
        wq_k = peer_w_query[0].rearrange("(k p) n -> p k n", p=P)
        u_rows = peer_expert_u[0].rearrange("(i p) (f d) -> i f p d", p=P, f=2)
        v_rows = peer_expert_v[0].rearrange("(i p) (f d) -> i f p d", p=P, f=2)

        raw_loaded = [sem(f"raw_loaded{i}") for i in range(RAW)]
        hi_done, split_done, split_free = sem("hi_done"), sem("split_done"), sem("split_free")
        acc_free = sem("acc_free")
        u_turned = sem("u_turned")
        cmp_used = sem("cmp_used")
        x1_stored, out_stored = sem("x1_stored"), sem("out_stored")

        def turned_at(use, k):
            return (2 * KC // 4 + k % 4) * T if use == 1 and k < KC // 2 else k * T

        def loaded(eng, slot, g):
            eng.wait_ge(raw_loaded[slot], 16 * (g // RAW + 1))

        block = ctx.enter_context(nc.Block())

        @block.sync
        def _(sp):
            def load(slot, src, shape=None):
                dst = raw[:, slot, :]
                if shape:
                    dst = dst[:, 0:shape[0] * shape[1]].rearrange("p (a b) -> p a b", a=shape[0])
                sp.dma_start(dst, src).then_inc(raw_loaded[slot], 16)

            def chunk(src_k, c, signal, first):
                for s in range(STEPS_PER_CHUNK):
                    if first is not None or s >= RAW:
                        sp.wait_ge(signal, (0 if first is None else first) + s - (RAW if first is None else 0) + 1)
                    load(s % RAW, src_k[:, 2 * s:2 * s + 2, bass.ds(c * CHUNK, CHUNK)], (2, CHUNK))

            for t in range(TT):
                sp.dma_start(X[:, t, :], x_rows[:, t, :]).then_inc(sem(f"x_loaded{t}"), 16)
            for src, row, n in ((norm1_g[0], G_NORM1, 16), (norm2_g[0], G_NORM2, 16), (sb_out_g[0], G_MIX, 8),
                                (nsa_out_g[0], G_MIX + 8, 8), (q_norm_g[0], G_Q, 1), (k_norm_g[0], G_K, 1)):
                sp.dma_start(gain_rows[row:row + n, :], src.rearrange("(a n) -> a n", n=P)).then_inc(sem("gains_loaded"), 16)
            sp.dma_start(gain_rows[G_PE:G_ALL, :], cmp_pe[0]).then_inc(sem("gains_loaded"), 16)
            sp.dma_start(TABLE, rel_bias_table).then_inc(sem("table_loaded"), 16)
            sp.dma_start(ONEHOT, onehot).then_inc(sem("table_loaded"), 16)
            sp.dma_start(W_TAIL, win_k[:, :, COL_GATE:IN_COLS]).then_inc(sem("tail_loaded"), 16)
            for v, w2 in enumerate((cmp_k_w2, cmp_v_w2)):
                sp.dma_start(W2S[:, 2 * v:2 * v + 2, :], w2[0].rearrange("(f p) n -> p f n", p=P)).then_inc(sem("w2_loaded"), 16)
            chunk(win_k, 0, split_done, None)
            with sp.Fori(1, W_IN_CHUNKS) as c:
                chunk(win_k, c, split_done, c * STEPS_PER_CHUNK - RAW)
            for s in range(CMP_STEPS):
                if s < RAW:
                    sp.wait_ge(split_done, SP_TAIL - RAW + s + 1)
                else:
                    sp.wait_ge(cmp_used, s - RAW + 1)
                w1 = (cmp_k_w1, cmp_v_w1)[s * 2 // CMP_STEPS][0].rearrange("(l p) n -> p l n", p=P)
                l = CMP_L * (s % (CMP_STEPS // 2))
                load(s % RAW, w1[:, l:l + CMP_L, :], (CMP_L, CMP_HIDDEN))
            for s in range(RAW):
                sp.wait_ge(cmp_used, CMP_STEPS - RAW + s + 1)
                load(s, wout_k[:, 2 * s:2 * s + 2, 0:CHUNK], (2, CHUNK))
            for s in range(RAW, STEPS_PER_CHUNK):
                sp.wait_ge(split_done, SP_OUT + s - RAW + 1)
                load(s % RAW, wout_k[:, 2 * s:2 * s + 2, 0:CHUNK], (2, CHUNK))
            with sp.Fori(1, W_CHUNKS) as c:
                chunk(wout_k, c, split_done, c * STEPS_PER_CHUNK + SP_OUT - RAW)
            def query_steps(a, b):
                for s in range(a, b):
                    sp.wait_ge(split_done, SP_QUERY + s - RAW + 1)
                    load(s % RAW, wq_k[:, 2 * s:2 * s + 2, 0:CHUNK], (2, CHUNK))

            query_steps(0, RAW)
            sp.wait_ge(sem("x1_ready"), W_CHUNKS)
            sp.dma_start(SK, peer_sub_keys[0].rearrange("h s n d -> n (h s) d")).then_inc(sem("keys_loaded"), 16)
            sp.dma_start(x1_rows, X).then_inc(x1_stored, 16)
            query_steps(RAW, STEPS_PER_CHUNK)
            with sp.Fori(1, W_CHUNKS) as c:
                chunk(wq_k, c, split_done, c * STEPS_PER_CHUNK + SP_QUERY - RAW)
            for s in range(RAW):
                sp.wait_ge(split_done, SP_U + s - RAW + 1)
                load(s, u_rows[s // 2, s % 2])
            with sp.Fori(1, NE_T // 2) as pair:
                i = pair * 2
                for s in range(RAW):
                    sp.wait_ge(u_turned, i * 4 + 2 * (s - RAW + 1))
                    load(s, u_rows[bass.ds(i + s // 2, 1), s % 2].rearrange("a p d -> (a p) d"))
            for s in range(RAW):
                sp.wait_ge(u_turned, U_UNITS - 2 * (RAW - s - 1))
                load(s, v_rows[s // 2, s % 2])
            with sp.Fori(1, NE_T // 2) as pair:
                i = pair * 2
                for s in range(RAW):
                    sp.wait_ge(split_done, i * 2 + s - RAW + SP_V + 1)
                    load(s, v_rows[bass.ds(i + s // 2, 1), s % 2].rearrange("a p d -> (a p) d"))
            sp.wait_ge(x1_stored, 16)
            sp.wait_ge(sem("w_lo_done"), 16)
            sp.dma_start(X1, x1_rows).then_inc(sem("x1_loaded"), 16)
            for f in range(2):
                for t in range(TT):
                    sp.wait_ge(sem("out_ready"), f * TT + t + 1)
                    c = slice(f * STEP, (f + 1) * STEP)
                    sp.dma_start(out_rows[:, t, c], X1[:, t, c]).then_inc(out_stored, 16)
            sp.wait_ge(out_stored, 16 * 2 * TT)

        @block.gpsimd
        def _(pool):
            made = sem("constants")
            pool.memset(ident[:], 0.0).then_inc(made, 1)
            pool.memset(neg_tri, -1.0).then_inc(made, 1)
            pool.memset(before, 1.0).then_inc(made, 1)
            pool.memset(neg_ones, -1.0).then_inc(made, 1)
            pool.memset(has_block, 1.0).then_inc(made, 1)
            pool.iota(iota[:], pattern=[[1, P]], base=0, channel_multiplier=0, allow_small_or_imprecise_dtypes=True).then_inc(made, 1)
            pool.memset(minus_half, -0.5).then_inc(made, 1)
            pool.wait_ge(made, 7)
            pool.affine_select(out=ident[:], in_=ident[:], compare_op=ALU.not_equal, fill=1.0, base=0,
                               pattern=[[-1, P]], channel_multiplier=1).then_inc(made, 1)
            pool.affine_select(out=neg_tri, in_=neg_tri, compare_op=ALU.is_ge, fill=0.0, base=0,
                               pattern=[[-1, P]], channel_multiplier=1).then_inc(made, 1)
            pool.affine_select(out=before, in_=before, compare_op=ALU.is_gt, fill=0.0, base=0,
                               pattern=[[1, P]], channel_multiplier=-1).then_inc(made, 1)
            pool.affine_select(out=has_block, in_=has_block, compare_op=ALU.is_ge, fill=0.0, base=1 - CMP_BLOCK,
                               pattern=[[0, 1]], channel_multiplier=1).then_inc(made, 1)
            def power(n, v):
                pool.wait_ge(sem("mean_square"), n)
                pool.tensor_tensor(v, v, minus_half[0:v.shape[0], 0:v.shape[1]], ALU.pow).then_inc(sem("inverse_rms"), 1)

            power(1, rstd[:, 0:TT])
            pool.wait_ge(sem("rows_turned"), 1)
            pool.memset(MIX[:, :, 1024:2048], 0.0).then_inc(sem("nsa_cleared"), 1)
            pool.wait_ge(sem("bias_rows"), 1)
            pool.dma_start(bias_dram[:, :, 0:BIAS_W], ROWB.unsqueeze(1).broadcast_to([NH, P, BIAS_W])).then_inc(sem("bias_stored"), 16)
            pool.wait_ge(sem("bias_stored"), 16)
            pool.dma_start(BIAS, bass.AP(tensor=bias_dram.tensor, offset=P, ap=[[BIAS_W, P], [P * (BIAS_W + 1), NH], [1, 384]])).then_inc(sem("bias_loaded"), 16)
            power(2, nrstd[:, 0:TT * NH])
            pool.wait_ge(sem("sb_turned"), 2)
            for v in range(2):
                pool.memset(PROJ[:, v, 0:CMP_BLOCK * 64], 0.0).then_inc(sem("blocks_cleared"), 1)
            power(3, nrstd[:, TT * NH:24])
            power(4, rstd[:, 0:TT])
            power(5, krstd[0:NC])
            power(6, rstd[:, TT:2 * TT])
            power(7, rstd[:, 0:TT])
            def clear(a, b):
                pool.memset(big[:, a:b], 1.0).then_inc(sem("gates_cleared"), 1)

            pool.wait_ge(sem("scores_read"), W_CHUNKS)
            clear(A_R, A_S)
            clear(A_ROUTED, NE_T * T)
            pool.wait_ge(sem("best_shifted"), 1)
            clear(A_S, A_PICK)
            clear(A_HEAD, A_ROUTED)
            pool.wait_ge(sem("picks_turned"), 1)
            clear(A_PICK, A_HEAD)

        @block.scalar
        def _(act):
            act_step = sem("act_step")
            steps = [0]

            def link(ins):
                steps[0] += 1
                ins.then_inc(act_step, 1)
                act.wait_ge(act_step, steps[0])

            def loaded_at(slot, uses):
                act.wait_ge(raw_loaded[slot], 16 * uses)

            def hi_steps(uses0, n0, a, b):
                for s in range(a, b):
                    loaded_at(s % RAW, uses0 + (s // RAW + 1))
                    act.wait_ge(split_free, n0 + s + 1)
                    act.activation(split_hi[:, s % SPLIT, :], raw[:, s % RAW, :], ACT.Copy).then_inc(hi_done, 1)

            def hi_product(raw0, n0, chunks):
                with act.Fori(0, chunks) as c:
                    hi_steps(c * 2 + raw0 // RAW, c * STEPS_PER_CHUNK + n0, SPLIT, STEPS_PER_CHUNK + SPLIT)

            def turned_hi(use, gain0, k0=0, k1=KC):
                for k in range(k0, k1):
                    if k % 2 == 0:
                        act.wait_ge(sem("rows_turned"), (KC // 2) * use + k // 2 + 1)
                    o = turned_at(use, k)
                    act.activation(ht[:, k, 0:T], psf[:, o:o + T], ACT.Copy,
                                   scale=gain_cols[:, gain0 + k:gain0 + k + 1]).then_inc(sem("ht_hi"), 1)

            def squares(src, dst):
                act.activation(XN[:, 1, 0:src.shape[1]], src, ACT.Square, accum_out=dst).then_inc(sem("act_squares"), 1)

            def scale_rows(n, src, a=0, b=D, r=1):
                act.wait_ge(sem("inverse_rms"), n)
                act.activation(XN[:, 1, a:b], src[:, 1, a:b], ACT.Copy, scale=rstd[:, r:r + 1]).then_inc(sem("rows_normed"), 1)

            act.wait_ge(sem("x_loaded1"), 16)
            squares(X[:, 1, :], ssq[:, 1:2])
            act.wait_ge(sem("gains_turned"), 1)
            link(act.activation(gain_cols[:], psf[:, 0:G_ALL], ACT.Copy))
            act.sem_inc(sem("gains_ready"), 1)
            act.wait_ge(sem("act_squares"), 1)
            scale_rows(1, X)
            hi_steps(RAW_IN // RAW, SP_IN, 0, 1)
            turned_hi(0, G_NORM1, 0, 8)
            hi_steps(RAW_IN // RAW, SP_IN, 1, SPLIT)
            turned_hi(0, G_NORM1, 8, KC)
            hi_product(RAW_IN, SP_IN, FIRST_BESIDE)

            act.preload_act_table_set("natural_log_exp_and_others")
            for n in range(BESIDE_STEPS):
                g = FIRST_BESIDE * STEPS_PER_CHUNK + n
                if n >= SPLIT:
                    loaded(act, g % RAW, RAW_IN + g)
                    act.wait_ge(split_free, SP_IN + g + 1)
                    act.activation(split_hi[:, g % SPLIT, :], raw[:, g % RAW, :], ACT.Copy).then_inc(hi_done, 1)
                b = n // 12
                if n % 12 == 1:
                    act.wait_ge(sem("sb_turned"), b + 1)
                    act.activation(QKT[:, :, 0:T], ps[:, 4:8, 0:T], ACT.Copy, scale=SCALE).then_inc(sem("sb_q"), 1)
                if n % 12 == 3:
                    act.wait_ge(sem("sb_z"), b + 1)
                    act.activation(T1, ps[:, 4:8, 0:384], ACT.Abs).then_inc(sem("sb_abs"), 1)
                if n % 12 == 4:
                    act.wait_ge(sem("sb_abs"), b + 1)
                    act.activation(T1f, T1f, ACT.Exp, scale=-1.0).then_inc(sem("sb_exp_abs"), 1)
                if n % 12 == 5:
                    act.wait_ge(sem("sb_exp_abs"), b + 1)
                    act.activation(T1f, T1f, ACT.Ln, bias=1.0).then_inc(sem("sb_ln"), 1)
                if n % 12 == 9:
                    act.wait_ge(sem("sb_cumsum"), b + 1)
                    act.activation(T1, ps[:, 4:8, 0:384], ACT.Exp).then_inc(sem("sb_exp"), 1)
            act.wait_ge(sem("tail_loaded"), 16)
            for s in range(TAIL_STEPS):
                act.wait_ge(split_free, SP_TAIL + s + 1)
                act.activation(split_hi[:, s, 0:TAIL_K * N_GATES], tail_raw[:, s * TAIL_K * N_GATES:(s + 1) * TAIL_K * N_GATES], ACT.Copy).then_inc(hi_done, 1)

            act.wait_ge(split_free, SP_OUT + 2)
            act.activation(GATES_T, ps[0:N_GATES, 2, 0:T], ACT.Exp, scale=-1.0).then_inc(sem("gate_exp"), 1)

            def q_out(b):
                act.wait_ge(sem("q_turned"), b + 1)
                act.activation(QT.rearrange("p h n -> p (h n)")[:, b * 1024:(b + 1) * 1024], psf[:, 0:2 * 512], ACT.Copy,
                               scale=gain_cols[:, G_Q:G_Q + 1]).then_inc(sem("q_ready"), 1)

            q_out(0)
            scale_rows(4, MIX, 0, D // 2, 1)
            turned_hi(1, G_MIX, 0, 4)
            q_out(1)
            turned_hi(1, G_MIX, 4, 8)

            def round_exp(r):
                act.wait_ge(sem("ns_shifted"), r + 1)
                for h in range(2):
                    for t in range(TT):
                        v = T1r[:, r % 2, h, t * P:(1 + 2 * t) * P]
                        n = 2 * h + t
                        act.activation(v, v, ACT.Exp, bias=round_neg[:, r % 2, n:n + 1],
                                       accum_out=round_sum[:, r % 4, n:n + 1]).then_inc(sem("ns_exp"), 1)

            def round_turned(r):
                act.wait_ge(sem("ns_p_turned"), r + 1)
                if r >= 2:
                    act.wait_ge(sem("ns_pv"), r - 1)
                act.activation(T2r[:, r % 2].rearrange("p b n -> p (b n)"), psf[:, 4 * 512:4 * 512 + 6 * P], ACT.Copy).then_inc(sem("ns_pt"), 1)

            for r in range(ROUNDS + 1):
                if r < ROUNDS:
                    round_exp(r)
                if r:
                    round_turned(r - 1)
                if r == 1:
                    act.wait_ge(cmp_used, CMP_STEPS)
                    act.activation(HG[0:64].rearrange("p v n -> p (v n)"), ps[0:64, 7, :], ACT.Gelu_apprx_tanh).then_inc(sem("hidden"), 1)
                if r == 2:
                    act.wait_ge(sem("hidden_turned"), 1)
                    act.activation(HGT.rearrange("p w n -> p (w n)"), ps[:, 7, 0:256], ACT.Copy).then_inc(sem("hidden_t"), 1)
                if r == 7:
                    act.wait_ge(sem("cmp_shifted"), 1)
                    act.activation(cmp_p, cmp_p, ACT.Exp).then_inc(sem("cmp_exp"), 1)
                if r == 4:
                    hi_steps(RAW_OUT // RAW, SP_OUT, 0, SPLIT)
            act.wait_ge(sem("cmp_p_turned"), 1)
            act.activation(PCT[0:NC].rearrange("p b n -> p (b n)"), psf[0:NC, 0:2048], ACT.Copy).then_inc(sem("cmp_pt"), 1)

            def queries_turned(c):
                act.wait_ge(sem("pq_turned"), c + 1)
                act.activation(PQT.rearrange("p w n -> p (w n)")[:, c * 1024:(c + 1) * 1024],
                               psf[:, 4 * 512:6 * 512], ACT.Copy).then_inc(sem("pq_ready"), 1)

            hi_steps(RAW_OUT // RAW, SP_OUT, SPLIT, SPLIT + 1)
            act.wait_ge(sem("nsa_out"), 1)
            squares(MIX[:, 1, 1024:2048], ssq[:, 3:4])
            hi_steps(RAW_OUT // RAW, SP_OUT, SPLIT + 1, SPLIT + 2)
            act.wait_ge(sem("act_squares"), 2)
            scale_rows(6, MIX, D // 2, D, 3)
            turned_hi(1, G_MIX, KC // 2, KC)
            hi_steps(RAW_OUT // RAW, SP_OUT, SPLIT + 2, STEPS_PER_CHUNK)
            for c in range(1, W_CHUNKS):
                hi_steps(c * 2 + RAW_OUT // RAW, c * STEPS_PER_CHUNK + SP_OUT, 0, STEPS_PER_CHUNK)
            hi_steps(RAW_QUERY // RAW, SP_QUERY, 0, SPLIT)
            scale_rows(7, X)
            turned_hi(2, G_NORM2)
            hi_steps(RAW_QUERY // RAW, SP_QUERY, SPLIT, STEPS_PER_CHUNK)
            for c in range(1, W_CHUNKS):
                for n in range(STEPS_PER_CHUNK):
                    hi_steps(c * 2 + RAW_QUERY // RAW, c * STEPS_PER_CHUNK + SP_QUERY, n, n + 1)
                    if n == 1 and c == 1:
                        act.wait_ge(sem("keys_turned"), 1)
                        act.activation(SKT.rearrange("p w n -> p (w n)"), psf[:, 4 * 512:8 * 512], ACT.Copy).then_inc(sem("keys_ready"), 1)
                    if n == 4:
                        queries_turned(c - 1)
            queries_turned(W_CHUNKS - 1)

            def unit_part(i, j, u):
                n = i * UNITS + j * UNITS + u
                act.wait_ge(u_turned, n + 1)
                act.wait_ge(split_free, n + SP_U - 1)
                act.activation(unit_hi[:, u * UNIT:(u + 1) * UNIT], ps[:, u, :], ACT.Copy).then_inc(hi_done, 1)

            def gelu(i, j):
                act.wait_ge(sem("s_summed"), i + j + 3)
                act.activation(WACT[:, bass.ds(i + j, 1), :].rearrange("p a c -> p (a c)"),
                               s_sum[:, j % 2, :], ACT.Gelu_apprx_tanh).then_inc(sem("acted"), 1)

            def route_tiles(i, first):
                for j in range(TILES_PER_HEAD):
                    for u in range(UNITS):
                        unit_part(i, j, u)
                        if u == 1 and j:
                            gelu(i, j - 1)
                        if u == 1 and not j and not first:
                            gelu_before(i)

            def gelu_before(i):
                act.wait_ge(sem("s_summed"), i + 2)
                act.activation(WACT[:, bass.ds(i - 1, 1), :].rearrange("p a c -> p (a c)"),
                               s_sum[:, 1, :], ACT.Gelu_apprx_tanh).then_inc(sem("acted"), 1)

            act.preload_act_table(ACT.Gelu_apprx_tanh)
            route_tiles(0, True)
            with act.Fori(1, HEADS) as head:
                route_tiles(head * TILES_PER_HEAD, False)
            unit_part(ROUTE_TILES, 0, 0)
            unit_part(ROUTE_TILES, 0, 1)
            act.wait_ge(sem("s_summed"), ROUTE_TILES + 2)
            act.activation(WACT[:, ROUTE_TILES - 1, :], s_sum[:, 1, :], ACT.Gelu_apprx_tanh).then_inc(sem("acted"), 1)
            act.wait_ge(sem("best_shifted"), 1)
            act.activation(PICK[:, 2], PICK[:, 2], ACT.Exp).then_inc(sem("best_exp"), 1)
            unit_part(ROUTE_TILES, 0, 2)
            unit_part(ROUTE_TILES, 0, 3)
            act.preload_act_table(ACT.Gelu_apprx_tanh)

            def build_tile(s, j, first):
                i = s + ROUTE_TILES
                begun = first and not j
                if not begun:
                    unit_part(i, j, 0)
                act.wait_ge(sem("gates_mm"), s + j + 1)
                if begun:
                    act.wait_ge(sem("picked_ready"), 3)
                for c in range(TOKENS_PER_BANK):
                    col = s * TOKENS_PER_BANK + j * TOKENS_PER_BANK + c
                    ins = act.activation(one_j[j][:, c * P:(c + 1) * P], iota[:, :], ACT.Abs, scale=-1.0,
                                         bias=picked[:, 1, bass.ds(col, 1)])
                    if c == 1 and not begun:
                        unit_part(i, j, 1)
                ins.then_inc(sem("onehot_abs"), 1)
                if not begun:
                    act.wait_ge(sem("s_summed"), s + j + ROUTE_TILES + 2)
                    act.activation(s_sum[:, 1 - j, :], s_sum[:, 1 - j, :], ACT.Gelu_apprx_tanh).then_inc(sem("acted"), 1)
                    unit_part(i, j, 2)
                act.wait_ge(sem("onehot_abs"), s + j + 1)
                act.activation(one_j[j], one_j[j].bitcast(F32), ACT.Relu, scale=-1.0, bias=1.0).then_inc(sem("onehot_j"), 1)
                if not begun:
                    unit_part(i, j, 3)

            for j in range(2):
                build_tile(0, j, True)
            with act.Fori(1, BUILD_STEPS // 2) as pair:
                for j in range(2):
                    build_tile(pair * 2, j, False)
            act.wait_ge(sem("s_summed"), NE_T + 2)
            act.activation(s_sum[:, 1, :], s_sum[:, 1, :], ACT.Gelu_apprx_tanh).then_inc(sem("acted"), 1)

            def v_tile(i, j):
                act.wait_ge(split_free, i * 2 + 2 * j + SP_V)
                if j == 0:
                    act.wait_ge(sem("gates_built"), BUILD_STEPS + 2)
                act.activation(w_hi[:, j, :], WACT[:, bass.ds(i + j, 1), :].rearrange("p a c -> p (a c)"), ACT.Copy).then_inc(sem("w_hi_done"), 1)
                for f in range(2):
                    slot = 2 * j + f
                    act.wait_ge(raw_loaded[slot], i * 8 + 16 * (RAW_V // RAW + 1))
                    act.wait_ge(split_free, i * 2 + 2 * j + f + SP_V + 1)
                    act.activation(split_hi[:, f, :], raw[:, slot, :], ACT.Copy).then_inc(hi_done, 1)

            with act.Fori(0, NE_T // 2) as pair:
                i = pair * 2
                for j in range(2):
                    v_tile(i, j)

        @block.vector
        def _(dve):
            dve_step = sem("dve_step")
            steps = [0]

            def link(ins):
                steps[0] += 1
                ins.then_inc(dve_step, 1)
                dve.wait_ge(dve_step, steps[0])

            def flag(name, n=1):
                dve.sem_inc(sem(name), n)

            def lo(slot, n):
                dve.wait_ge(hi_done, n + 1)
                dve.tensor_tensor(split_lo[:, slot % SPLIT, :], raw[:, slot, :],
                                  split_hi[:, slot % SPLIT, :].bitcast(F32), ALU.subtract).then_inc(split_done, 1)

            norms = [0]

            def inverse_rms(dst, sums, n):
                norms[0] += 1
                dve.tensor_scalar(dst, sums, 1.0 / n, EPS, ALU.mult, ALU.add).then_inc(sem("mean_square"), 1)
                dve.wait_ge(sem("inverse_rms"), norms[0])

            def squares(src, dst, dump=None):
                if dump is None:
                    dump = XN[:, 0, 0:src.shape[1]]
                return dve.tensor_tensor_reduce(dump, src, src, 1.0, 0.0, ALU.mult, ALU.add, dst)

            def scale_rows(src, a=0, b=D, r=0):
                dve.tensor_scalar(XN[:, 0, a:b], src[:, 0, a:b], rstd[:, r:r + 1], None, ALU.mult).then_inc(sem("rows_normed"), 1)

            def turned_lo(use, gain0, k0=0, k1=KC):
                for k in range(k0, k1):
                    o = turned_at(use, k)
                    if k % 2 == 0:
                        dve.wait_ge(sem("ht_hi"), KC * use + k + 2)
                    dve.scalar_tensor_tensor(out=ht[:, k, T:2 * T], in0=psf[:, o:o + T],
                                             scalar=gain_cols[:, gain0 + k:gain0 + k + 1],
                                             in1=ht[:, k, 0:T].bitcast(F32), op0=ALU.mult,
                                             op1=ALU.subtract).then_inc(sem("ht_lo"), 1)

            def bank_pair(parity):
                return ps[:, 2 * parity:2 * parity + 2, :]

            def to_proj(c, parity, n_end):
                dve.wait_ge(split_free, n_end + 2)
                dve.tensor_copy(PROJ[:, :, bass.ds(c * CHUNK, CHUNK)], bank_pair(parity)).then_inc(acc_free, 1)

            dve.wait_ge(sem("x_loaded0"), 16)
            link(squares(X[:, 0, :], ssq[:, 0:1]))
            dve.wait_ge(sem("act_squares"), 1)
            inverse_rms(rstd[:, 0:TT], ssq[:, 0:TT], D)
            scale_rows(X)
            dve.memset(s_sum[:], 0.0).then_inc(acc_free, 2)
            dve.wait_ge(sem("bias_mm"), 1)
            link(dve.tensor_copy(ROWB[:, 0:T + 1], ps[0:NH, 7, 0:T + 1]))
            dve.memset(ROWB[:, T + 1:BIAS_W], NEG).then_inc(sem("bias_rows"), 1)
            lo(0, SP_IN)
            turned_lo(0, G_NORM1, 0, 8)
            lo(1, SP_IN + 1)
            turned_lo(0, G_NORM1, 8, KC)

            def in_chunk(c, parity, prev):
                for s in range(0 if prev else SPLIT, STEPS_PER_CHUNK):
                    lo(s % RAW, c * STEPS_PER_CHUNK + s + SP_IN)
                    if s == 1 and prev:
                        to_proj(c - 1, 1 - parity, c * STEPS_PER_CHUNK + SP_IN)

            q_rows = PROJ[:, :, COL_Q:COL_Q + NH * HD]
            gate = gates.rearrange("p (t h r) -> p t h r", t=TT, r=3)

            def q_squares(t):
                return dve.tensor_tensor(SQ[:, t * 1024:(t + 1) * 1024], q_rows[:, t, :], q_rows[:, t, :], ALU.mult)

            def k_squares():
                for b, col in enumerate((COL_KSLC, COL_KWIN)):
                    k_rows = PROJ[:, :, col:col + NG * HD]
                    ins = dve.tensor_tensor(SQK[:, b * 512:(b + 1) * 512].rearrange("p (t n) -> p t n", t=TT), k_rows, k_rows, ALU.mult)
                link(ins)

            def nsa_scales(a, b):
                link(dve.tensor_reduce(nssq[:, a:b], big[:, A_QT + a * HD:A_QT + b * HD].rearrange("p (h d) -> p h d", d=HD), AX_X, ALU.add))
                norms[0] += 1
                dve.tensor_scalar(nrstd[:, a:b], nssq[:, a:b], 1.0 / HD, EPS, ALU.mult, ALU.add).then_inc(sem("mean_square"), 1)

            def q_norm(t):
                v = q_rows[:, t, :].rearrange("p (h d) -> p h d", d=HD)
                dve.tensor_tensor(v, v, nrstd[:, t * NH:(t + 1) * NH].unsqueeze(2).broadcast_to([P, NH, HD]), ALU.mult)

            def k_norm():
                dve.wait_ge(sem("inverse_rms"), norms[0])
                for b, col in enumerate((COL_KSLC, COL_KWIN)):
                    for t in range(TT):
                        v = PROJ[:, t, col:col + NG * HD].rearrange("p (g d) -> p g d", d=HD)
                        o = 16 + b * 4 + t * NG
                        ins = dve.tensor_tensor(v, v, nrstd[:, o:o + NG].unsqueeze(2).broadcast_to([P, NG, HD]), ALU.mult)
                ins.then_inc(sem("nsa_normed"), 1)

            def blocks():
                pe = gain_cols[:, G_PE:G_ALL].unsqueeze(2).broadcast_to([P, CMP_BLOCK, NC])
                dve.wait_ge(sem("blocks_cleared"), 2)
                for v in range(2):
                    for g in range(NG):
                        src = KVC[:, v, g, :]
                        windows = bass.AP(tensor=src.tensor, offset=src.offset, ap=[list(src.ap[0]), [1, CMP_BLOCK], [CMP_STRIDE, NC]])
                        dve.tensor_tensor(BLK[:, v, :, 32 * g:32 * g + NC], windows, pe, ALU.add).then_inc(sem("blocks_ready"), 1)

            def diagonal(v):
                f = v.rearrange("p h (b n) -> p h b n", n=P)
                return [f[:, :, b, :] for b in (0, 2)]

            mask4 = before[:, :].unsqueeze(1).broadcast_to([P, 4, P])

            def sb_keys(b):
                dve.wait_ge(sem("sb_q"), b + 1)
                dve.tensor_copy(QKT[:, :, T:2 * T], ps[:, 4:8, T:2 * T]).then_inc(sem("sb_k"), 1)

            def sb_softplus(b):
                dve.wait_ge(sem("sb_ln"), b + 1)
                link(dve.scalar_tensor_tensor(out=T2, in0=ps[:, 4:8, 0:384], scalar=0.0, in1=T1, op0=ALU.max, op1=ALU.add))
                for v in diagonal(T2):
                    dve.tensor_tensor(v, v, mask4, ALU.mult).then_inc(sem("sb_softplus"), 1)

            def sb_weights(b):
                dve.wait_ge(sem("sb_exp"), b + 1)
                for v in diagonal(T1):
                    dve.scalar_tensor_tensor(out=v, in0=v, scalar=1.0, in1=mask4, op0=ALU.min, op1=ALU.mult).then_inc(sem("sb_a"), 1)

            def sb_out(b):
                dve.wait_ge(sem("sb_pv"), b + 1)
                dve.tensor_copy(MIX[:, :, b * 512:(b + 1) * 512].rearrange("p t (h d) -> p h t d", h=4),
                                ps[:, 4:6, :].rearrange("p b (h t d) -> p (b h) t d", h=2, t=TT)).then_inc(sem("sb_out"), 1)

            in_chunk(0, 0, False)
            with dve.Fori(0, FIRST_BESIDE // 2 - 1) as pair:
                c = pair * 2 + 1
                in_chunk(c, 1, True)
                in_chunk(c + 1, 0, True)
            in_chunk(FIRST_BESIDE - 1, 1, True)

            dve.wait_ge(sem("constants"), 11)
            for n in range(BESIDE_STEPS):
                g = FIRST_BESIDE * STEPS_PER_CHUNK + n
                lo(g % RAW, SP_IN + g)
                if n % STEPS_PER_CHUNK == 1:
                    c = g // STEPS_PER_CHUNK
                    to_proj(c - 1, (c - 1) % 2, c * STEPS_PER_CHUNK + SP_IN)
                b = n // 12
                if n % 12 == 1:
                    sb_keys(b)
                if n % 12 == 6:
                    sb_softplus(b)
                if n % 12 == 10:
                    sb_weights(b)
                if n == 11:
                    dve.wait_ge(sem("bias_loaded"), 16)
                    sb_out(0)
                if n == 3:
                    dve.wait_ge(acc_free, 2 + FIRST_BESIDE)
                    q_squares(0)
                if n == 4:
                    link(q_squares(1))
                if n == 5:
                    nsa_scales(0, TT * NH)
                if n == 14:
                    dve.wait_ge(sem("inverse_rms"), norms[0])
                if n in (14, 15):
                    q_norm(n - 14)
            dve.wait_ge(sem("cv_turned"), 1)
            dve.tensor_copy(KVC.rearrange("p b g n -> p (b g n)"), psf[:, 6 * 512:8 * 512]).then_inc(sem("kvc_ready"), 1)
            for s in range(TAIL_STEPS):
                dve.wait_ge(hi_done, SP_TAIL + s + 1)
                w = TAIL_K * N_GATES
                dve.tensor_tensor(split_lo[:, s, 0:w], tail_raw[:, s * w:(s + 1) * w],
                                  split_hi[:, s, 0:w].bitcast(F32), ALU.subtract).then_inc(split_done, 1)
            dve.wait_ge(sem("kvc_ready"), 1)
            blocks()
            to_proj(W_IN_CHUNKS - 1, (W_IN_CHUNKS - 1) % 2, SP_TAIL)
            dve.wait_ge(acc_free, 2 + W_IN_CHUNKS)
            k_squares()
            nsa_scales(TT * NH, 24)
            sb_out(1)
            dve.wait_ge(sem("gate_exp"), 1)
            link(dve.tensor_scalar(GATES_T, GATES_T, 1.0, None, ALU.add))
            dve.reciprocal(GATES_T, GATES_T).then_inc(sem("gates_ready"), 1)
            k_norm()
            dve.wait_ge(sem("sb_out"), 2)
            for t in range(TT):
                ins = squares(MIX[:, t, 0:1024], ssq[:, t:t + 1], XN[:, t, 0:1024])
            link(ins)
            norms[0] += 1
            dve.tensor_scalar(rstd[:, 0:TT], ssq[:, 0:TT], 2.0 / D, EPS, ALU.mult, ALU.add).then_inc(sem("mean_square"), 1)
            dve.wait_ge(sem("gates_turned"), 1)
            dve.tensor_copy(gates, ps[:, 2, T:T + TT * N_GATES]).then_inc(acc_free, 1)
            dve.wait_ge(acc_free, 2 + CH_TAIL + 1)
            dve.wait_ge(sem("k_turned"), 1)
            dve.tensor_scalar(KT.rearrange("p b g n -> p (b g n)"), psf[:, 2 * 512:4 * 512], gain_cols[:, G_K:G_K + 1], SCALE, ALU.mult, ALU.mult).then_inc(sem("k_ready"), 1)

            dve.wait_ge(sem("inverse_rms"), norms[0])
            scale_rows(MIX, 0, D // 2, 0)
            turned_lo(1, G_MIX, 0, 8)

            def round_scores(r):
                dve.wait_ge(sem("ns_s"), r + 1)
                if r >= 2:
                    dve.wait_ge(sem("ns_p_turned"), r - 1)
                for h in range(2):
                    for t in range(TT):
                        a, w = t * P, (1 + t) * P
                        b0 = P * (TT - 1 - t)
                        ins = dve.tensor_tensor_reduce(T1r[:, r % 2, h, a:a + w], ps[:, 2 * (r % 2) + h, a:a + w],
                                                       BIAS[:, 2 * (r % 4) + h, b0:b0 + w], 1.0, -3.0e38, ALU.add, ALU.max,
                                                       round_max[:, r % 2, 2 * h + t:2 * h + t + 1])
                link(ins)
                dve.tensor_scalar(round_neg[:, r % 2], round_max[:, r % 2], -1.0, None, ALU.mult).then_inc(sem("ns_shifted"), 1)

            def round_out(r):
                branch, p0 = r // 4, 2 * (r % 4)
                dve.wait_ge(sem("ns_exp"), 4 * r + 4)
                link(dve.reciprocal(round_coef[:, r % 2], round_sum[:, r % 4]))
                c = round_coef[:, r % 2].rearrange("p (h t) -> p h t", t=TT)
                link(dve.tensor_tensor(c, c, gate[:, :, p0:p0 + 2, 1 + branch].rearrange("p t h -> p h t"), ALU.mult))
                dve.wait_ge(sem("ns_pv"), r + 1)
                for h in range(2):
                    for t in range(TT):
                        v = MIX[:, t, 1024 + (p0 + h) * HD:1024 + (p0 + h + 1) * HD]
                        n = 2 * h + t
                        ins = dve.scalar_tensor_tensor(out=v, in0=ps[:, 6, n * P:(n + 1) * P],
                                                       scalar=round_coef[:, r % 2, n:n + 1], in1=v, op0=ALU.mult, op1=ALU.add)
                link(ins)
                flag("ns_out")

            dve.wait_ge(sem("nsa_cleared"), 1)
            round_scores(0)
            round_scores(1)
            cp = cmp_p.rearrange("p (h t c) -> p h t c", h=NH, t=TT)
            cpr = cmp_p.rearrange("p (b c) -> p b c", c=NC)
            for r in range(2, ROUNDS + 2):
                if r < ROUNDS:
                    round_scores(r)
                if r == 5:
                    dve.wait_ge(sem("inverse_rms"), norms[0])
                    dve.tensor_tensor(KCV[0:NC, 0], KCV[0:NC, 0], krstd[0:NC].unsqueeze(2).broadcast_to([NC, NG, HD]), ALU.mult).then_inc(sem("kc_ready"), 1)
                round_out(r - 2)
                if r == 4:
                    dve.wait_ge(sem("cmp_kv"), 1)
                    link(dve.tensor_copy(KCV[0:NC].rearrange("p v g n -> p (v g n)"), ps[0:NC, 7, :]))
                    link(dve.tensor_tensor(KSQ[0:NC], KCV[0:NC, 0], KCV[0:NC, 0], ALU.mult))
                    link(dve.tensor_reduce(kssq[0:NC], KSQ[0:NC], AX_X, ALU.add))
                    norms[0] += 1
                    dve.tensor_scalar(krstd[0:NC], kssq[0:NC], 1.0 / HD, EPS, ALU.mult, ALU.add).then_inc(sem("mean_square"), 1)
                if r == 6:
                    dve.wait_ge(sem("kc_turned"), 1)
                    dve.tensor_scalar(KCT.rearrange("p g n -> p (g n)"), ps[:, 7, 0:32], gain_cols[:, G_K:G_K + 1], SCALE, ALU.mult, ALU.mult).then_inc(sem("kct_ready"), 1)
                if r == 7:
                    dve.wait_ge(sem("cmp_s"), 1)
                    sc = ps[:, 7, 0:256].rearrange("p (h t c) -> p h t c", h=NH, t=TT)
                    for t in range(TT):
                        start = CMP_BLOCK - 1 + P * (TT - 1 - t)
                        ins = dve.tensor_tensor(cp[:, :, t, :], sc[:, :, t, 0:NC],
                                                BIAS[:, :, start:start + CMP_STRIDE * (NC - 1) + 1:CMP_STRIDE], ALU.add)
                    link(ins)
                    link(dve.tensor_reduce(row_max, cpr, AX_X, ALU.max))
                    dve.tensor_tensor(cpr, cpr, row_max.unsqueeze(2).broadcast_to([P, 16, NC]), ALU.subtract).then_inc(sem("cmp_shifted"), 1)
                if r == 8:
                    dve.wait_ge(sem("cmp_exp"), 1)
                    link(dve.tensor_reduce(row_sum, cpr, AX_X, ALU.add))
                    link(dve.reciprocal(row_sum, row_sum))
                    rs = row_sum.rearrange("p (h t) -> p h t", t=TT)
                    cf = coef.rearrange("p (h t) -> p h t", t=TT)
                    link(dve.tensor_tensor(cf, rs, gate[:, :, :, 0].rearrange("p t h -> p h t"), ALU.mult))
                    link(dve.tensor_scalar(cf[:, :, 0], cf[:, :, 0], has_block, None, ALU.mult))
            for n in range(SPLIT):
                lo(n, SP_OUT + n)
            dve.wait_ge(sem("cmp_pv"), 1)
            for n in range(16):
                v = MIX[:, n % TT, 1024 + n // TT * HD:1024 + (n // TT + 1) * HD]
                ins = dve.scalar_tensor_tensor(out=v, in0=psf[:, 2048 + n * P:2048 + (n + 1) * P],
                                               scalar=coef[:, n:n + 1], in1=v, op0=ALU.mult, op1=ALU.add)
            link(ins)
            flag("nsa_out")

            link(squares(MIX[:, 0, 1024:2048], ssq[:, 2:3]))
            dve.wait_ge(sem("act_squares"), 2)
            norms[0] += 1
            dve.tensor_scalar(rstd[:, TT:2 * TT], ssq[:, TT:2 * TT], 2.0 / D, EPS, ALU.mult, ALU.add).then_inc(sem("mean_square"), 1)
            lo(SPLIT, SP_OUT + SPLIT)
            dve.wait_ge(sem("inverse_rms"), norms[0])
            scale_rows(MIX, D // 2, D, 2)
            lo(SPLIT + 1, SP_OUT + SPLIT + 1)
            turned_lo(1, G_MIX, KC // 2, KC)

            def to_x1(c):
                dve.wait_ge(split_free, SP_OUT + (c + 1) * STEPS_PER_CHUNK + 2)
                v = X[:, :, c * CHUNK:(c + 1) * CHUNK]
                dve.tensor_tensor(v, v, bank_pair((CH_OUT + c) % 2), ALU.add).then_inc(sem("x1_ready"), 1)
                dve.wait_ge(sem("x1_ready"), c + 1)
                dve.sem_inc(acc_free, 1)

            def x1_squares(c):
                for t in range(TT):
                    ins = squares(X[:, t, c * CHUNK:(c + 1) * CHUNK], x1_ssq[:, t * W_CHUNKS + c:t * W_CHUNKS + c + 1],
                                  XN[:, 0, t * CHUNK:(t + 1) * CHUNK])
                if c == W_CHUNKS - 1:
                    link(ins)

            for c in range(W_CHUNKS):
                for s in range(0 if c else SPLIT + 2, STEPS_PER_CHUNK):
                    lo(s % RAW, SP_OUT + c * STEPS_PER_CHUNK + s)
                    if s == 1 and c:
                        to_x1(c - 1)
                    if s == 4 and c:
                        x1_squares(c - 1)
            for s in range(SPLIT):
                lo(s, SP_QUERY + s)
            to_x1(W_CHUNKS - 1)
            x1_squares(W_CHUNKS - 1)
            link(dve.tensor_reduce(ssq[:, 0:TT], x1_ssq.rearrange("p (t c) -> p t c", t=TT), AX_X, ALU.add))
            inverse_rms(rstd[:, 0:TT], ssq[:, 0:TT], D)
            scale_rows(X)
            turned_lo(2, G_NORM2)

            def to_q(c):
                dve.wait_ge(split_free, SP_QUERY + (c + 1) * STEPS_PER_CHUNK + 2)
                dve.tensor_copy(Q[:, :, c * CHUNK:(c + 1) * CHUNK], bank_pair((CH_QUERY + c) % 2)).then_inc(acc_free, 1)

            def scores_out(c):
                dve.wait_ge(sem("scores"), c + 1)
                ins = dve.tensor_copy(S[:, :, 4 * c:4 * c + 4, :], ps[:, 6:8, :].rearrange("p t (w n) -> p t w n", n=NKEYS))
                ins.then_inc(sem("scores_read"), 1)

            for c in range(W_CHUNKS):
                for s in range(0 if c else SPLIT, STEPS_PER_CHUNK):
                    lo(s % RAW, SP_QUERY + c * STEPS_PER_CHUNK + s)
                    if s == 1 and c:
                        to_q(c - 1)
                    if s == 6 and c:
                        scores_out(c - 1)
            to_q(W_CHUNKS - 1)

            scores_out(W_CHUNKS - 1)
            dve.wait_ge(sem("scores_read"), W_CHUNKS)

            def unit_part(i, j, u):
                dve.wait_ge(hi_done, i * UNITS + j * UNITS + u + SP_U + 1)
                dve.tensor_tensor(unit_lo[:, u * UNIT:(u + 1) * UNIT], ps[:, u, :],
                                  unit_hi[:, u * UNIT:(u + 1) * UNIT].bitcast(F32), ALU.subtract).then_inc(split_done, 1)

            def head_part(head, part):
                def done(ins):
                    ins.then_inc(sem("head_step"), 1)

                def after(k):
                    dve.wait_ge(sem("head_step"), head * HEAD_OPS + k)

                def after_apart(k):
                    after(k)
                    dve.sem_inc(sem("head_waits"), 1)

                picks = [PICK[:, s].rearrange("p t h k -> p (t h k)")[:, bass.ds(head * TOPK, TOPK)] for s in range(3)]
                lo8, hi8 = slice(0, 8), slice(8, 16)
                if part == 0:
                    done(dve.tensor_copy(head_s.rearrange("p s n -> p (s n)"),
                                         S.rearrange("p t w n -> p (t w n)")[:, bass.ds(head * (2 * NKEYS), 2 * NKEYS)]))
                    after_apart(1)
                    for s in range(2):
                        done(dve.max(head_top[:, s, lo8], head_s[:, s, :]))
                elif part == 1:
                    after_apart(3)
                    for s in range(2):
                        done(dve.max_index(head_topi[:, s, lo8], head_top[:, s, lo8], head_s[:, s, :]))
                    after_apart(5)
                    for s in range(2):
                        done(dve.match_replace(head_s[:, s, :], head_top[:, s, lo8], head_s[:, s, :], -3.0e38))
                elif part == 2:
                    after_apart(7)
                    for s in range(2):
                        done(dve.max(head_top[:, s, hi8], head_s[:, s, :]))
                    after_apart(9)
                    for s in range(2):
                        done(dve.max_index(head_topi[:, s, hi8], head_top[:, s, hi8], head_s[:, s, :]))
                elif part == 3:
                    after(11)
                    done(dve.tensor_copy(head_topf, head_topi))
                    done(dve.tensor_tensor(head_sums.rearrange("p (a b) -> p a b", a=TOPK),
                                           head_top[:, 0, :].unsqueeze(2).broadcast_to([P, TOPK, TOPK]),
                                           head_top[:, 1, :].unsqueeze(1).broadcast_to([P, TOPK, TOPK]), ALU.add))
                elif part == 4:
                    after_apart(13)
                    done(dve.max(head_best[:, lo8], head_sums))
                    after_apart(14)
                    done(dve.max_index(head_pos[:, lo8], head_best[:, lo8], head_sums))
                    after_apart(15)
                    done(dve.match_replace(head_sums, head_best[:, lo8], head_sums, -3.0e38))
                elif part == 5:
                    after_apart(16)
                    done(dve.max(head_best[:, hi8], head_sums))
                    after_apart(17)
                    done(dve.max_index(head_pos[:, hi8], head_best[:, hi8], head_sums))
                elif part == 6:
                    after(18)
                    done(dve.tensor_scalar(head_ab[:, 0, :], head_pos, 4, None, ALU.logical_shift_right))
                    done(dve.tensor_scalar(head_ab[:, 1, :], head_pos, 15, None, ALU.bitwise_and))
                    done(dve.tensor_tensor(picks[2], head_best, head_best[:, 0:1].broadcast_to([P, TOPK]), ALU.subtract))
                    after(20)
                    done(dve.tensor_copy(head_abf, head_ab))
                else:
                    after(22)
                    for s in range(2):
                        done(dve.tensor_tensor(head_eq[:, s], head_abf[:, s, :].unsqueeze(2).broadcast_to([P, TOPK, TOPK]),
                                               iota[:, 0:TOPK].unsqueeze(1).broadcast_to([P, TOPK, TOPK]), ALU.is_equal))
                    after(24)
                    for s in range(2):
                        done(dve.tensor_tensor(head_eq[:, s], head_eq[:, s], head_topf[:, s, :].unsqueeze(1).broadcast_to([P, TOPK, TOPK]), ALU.mult))
                    after(26)
                    for s in range(2):
                        done(dve.tensor_reduce(picks[s], head_eq[:, s], AX_X, ALU.add))

            def route_tiles(head, first):
                i = head * TILES_PER_HEAD
                for j in range(TILES_PER_HEAD):
                    for u in range(UNITS):
                        unit_part(i, j, u)
                        if u == 1:
                            if not (first and not j):
                                s_sum_before(i, j)
                            head_part(head, 2 * j)
                        if u == 3:
                            head_part(head, 2 * j + 1)

            def s_sum_before(i, j):
                dve.wait_ge(split_free, i * UNITS + j * UNITS + SP_U + 2)
                dve.wait_ge(sem("acted"), i + j)
                k = (j + 1) % 2
                dve.tensor_copy(s_sum[:, k, :], ps[:, 4 + k, 0:T]).then_inc(sem("s_copied"), 1)
                dve.wait_ge(sem("s_copied"), i + j)
                dve.tensor_tensor(s_sum[:, k, :], s_sum[:, k, :], ps[:, 4 + k, T:2 * T], ALU.add).then_inc(sem("s_summed"), 1)

            route_tiles(0, True)
            with dve.Fori(1, HEADS) as head:
                route_tiles(head, False)
            unit_part(ROUTE_TILES, 0, 0)
            s_sum_before(ROUTE_TILES, 0)
            unit_part(ROUTE_TILES, 0, 1)
            dve.wait_ge(sem("head_step"), HEADS * HEAD_OPS)
            dve.sem_inc(sem("best_shifted"), 1)
            dve.wait_ge(sem("best_exp"), 1)
            pick_g = PICK[:, 2].rearrange("p t h k -> p (t h) k")
            gsum = GSUM.rearrange("p t h -> p (t h)")
            link(dve.tensor_reduce(gsum, pick_g, AX_X, ALU.add))
            link(dve.reciprocal(gsum, gsum))
            link(dve.tensor_tensor(pick_g, pick_g, gsum.unsqueeze(2).broadcast_to([P, HEADS, TOPK]), ALU.mult))
            flag("picks")
            unit_part(ROUTE_TILES, 0, 2)
            unit_part(ROUTE_TILES, 0, 3)
            dve.wait_ge(sem("picks_turned"), 1)
            dve.tensor_copy(picked[:, 0, :], ps[:, 6, 0:T]).then_inc(sem("picked_ready"), 1)
            dve.tensor_copy(picked[:, 2, :], ps[:, 6, T:2 * T]).then_inc(sem("picked_ready"), 1)
            dve.tensor_copy(picked[:, 1, :], ps[:, 7, 0:T]).then_inc(sem("picked_ready"), 1)
            dve.wait_ge(sem("picked_ready"), 3)

            def first_onehot(s, j):
                dve.wait_ge(sem("gates_mm"), s + j + 1)
                for c in range(TOKENS_PER_BANK):
                    col = s * TOKENS_PER_BANK + j * TOKENS_PER_BANK + c
                    ins = dve.tensor_scalar(one_i[:, j, c * P:(c + 1) * P], iota[:, :], picked[:, 0, bass.ds(col, 1)],
                                            picked[:, 2, bass.ds(col, 1)], ALU.is_equal, ALU.mult)
                ins.then_inc(sem("onehot_i"), 1)

            def apply_gates(s, j):
                dve.wait_ge(sem("gates_mm"), s + j + 2)
                v = WACT_C[:, bass.ds(s * TOKENS_PER_BANK + (j - 1) * TOKENS_PER_BANK, TOKENS_PER_BANK), :]
                dve.tensor_tensor(v, v, ps[:, 6 + (j + 1) % 2, :].rearrange("p (c i) -> p c i", c=TOKENS_PER_BANK), ALU.mult).then_inc(sem("gates_built"), 1)

            def apply_act(s, j):
                dve.wait_ge(sem("acted"), s + j + ROUTE_TILES + 2)
                v = WACT[:, bass.ds(s + j + (ROUTE_TILES - 1), 1), :].rearrange("p a c -> p (a c)")
                dve.wait_ge(sem("gates_built"), s + j + 2)
                dve.tensor_tensor(v, v, s_sum[:, (j + 1) % 2, :], ALU.mult).then_inc(sem("act_applied"), 1)

            def build_tile(s, j, first):
                i = s + ROUTE_TILES
                unit_part(i, j, 0)
                first_onehot(s, j)
                unit_part(i, j, 1)
                s_sum_before(i, j)
                unit_part(i, j, 2)
                if first:
                    dve.wait_ge(sem("gates_cleared"), 5)
                else:
                    dve.wait_ge(sem("act_applied"), s + j - 1)
                apply_gates(s, j)
                unit_part(i, j, 3)
                apply_act(s, j)

            first_onehot(0, 0)
            build_tile(0, 1, True)
            with dve.Fori(1, BUILD_STEPS // 2) as pair:
                for j in range(2):
                    build_tile(pair * 2, j, False)
            s_sum_before(NE_T, 0)
            dve.wait_ge(sem("act_applied"), BUILD_STEPS - 1)
            apply_gates(BUILD_STEPS, 0)
            apply_act(BUILD_STEPS, 0)

            with dve.Fori(0, NE_T // 2) as pair:
                i = pair * 2
                for j in range(2):
                    dve.wait_ge(sem("w_hi_done"), i + j + 1)
                    dve.tensor_tensor(w_lo[:, j, :], WACT[:, bass.ds(i + j, 1), :].rearrange("p a c -> p (a c)"),
                                      w_hi[:, j, :].bitcast(F32), ALU.subtract).then_inc(sem("w_lo_done"), 1)
                    for f in range(2):
                        dve.wait_ge(hi_done, i * 2 + 2 * j + f + SP_V + 1)
                        dve.tensor_tensor(split_lo[:, f, :], raw[:, 2 * j + f, :],
                                          split_hi[:, f, :].bitcast(F32), ALU.subtract).then_inc(split_done, 1)
            dve.wait_ge(sem("x1_loaded"), 16)
            for f in range(2):
                dve.wait_ge(split_free, SP_V + E_STEPS + 1 + f)
                for t in range(TT):
                    v = X1[:, t, f * STEP:(f + 1) * STEP]
                    dve.tensor_tensor(v, v, psf[:, t * D + f * STEP:t * D + (f + 1) * STEP], ALU.add).then_inc(sem("out_ready"), 1)

        @block.tensor
        def _(pe):
            def turn_rows(use, normed, k0=0, k1=KC):
                pe.wait_ge(sem("rows_normed"), normed)
                for k in range(k0, k1):
                    for t in range(TT):
                        o = turned_at(use, k) + t * P
                        ins = pe.transpose(psf[:, o:o + P], XN[:, t, k * P:(k + 1) * P], ident[:, :])
                    if k % 2:
                        ins.then_inc(sem("rows_turned"), 1)

            def gemm_step(acc, slot, ks, n):
                pe.wait_ge(split_done, n + 1)
                for j, k in enumerate(ks):
                    w_h = split_hi[:, slot, j * CHUNK:(j + 1) * CHUNK]
                    w_l = split_lo[:, slot, j * CHUNK:(j + 1) * CHUNK]
                    for t in range(TT):
                        h_h = ht[:, k, t * P:(t + 1) * P]
                        h_l = ht[:, k, T + t * P:T + (t + 1) * P]
                        pe.matmul(acc[t], h_h, w_h, start=k == 0, stop=False)
                        pe.matmul(acc[t], h_h, w_l, start=False, stop=False)
                        ins = pe.matmul(acc[t], h_l, w_h, start=False, stop=k == KC - 1)
                ins.then_inc(split_free, 1)

            def rows_turned_lo(use, s):
                pe.wait_ge(sem("ht_lo"), KC * use + max(2 * s + 2, 4))

            def gemm_chunk(ch, parity, n0, use):
                pe.wait_ge(acc_free, ch + 1)
                acc = [ps[:, 2 * parity + t, :] for t in range(TT)]
                for s in range(STEPS_PER_CHUNK):
                    if parity == (CH_IN, CH_OUT, CH_QUERY)[use] % 2:
                        rows_turned_lo(use, s)
                    gemm_step(acc, s % SPLIT, (2 * s, 2 * s + 1), n0 + s)

            def turn_head(bank, o, col):
                for t in range(TT):
                    ins = pe.transpose(ps[:, bank, o + t * P:o + (t + 1) * P], PROJ[:, t, col:col + HD], ident[:, :])
                return ins

            def sb_turn(b):
                for h in range(4):
                    for s, col in enumerate((COL_QSB, COL_KSB)):
                        ins = turn_head(4 + h, s * T, col + (4 * b + h) * HD)
                ins.then_inc(sem("sb_turned"), 1)

            def sb_scores(b):
                pe.wait_ge(sem("sb_q"), b + 1)
                pe.wait_ge(sem("sb_k"), b + 1)
                for h in range(4):
                    pe.matmul(ps[:, 4 + h, 0:T], QKT[:, h, T:T + P], QKT[:, h, 0:T], start=True, stop=False, skip_group_check=True)
                    ins = pe.matmul(ps[:, 4 + h, T:T + P], QKT[:, h, T + P:2 * T], QKT[:, h, P:T], start=False, stop=False, skip_group_check=True)
                ins.then_inc(sem("sb_z"), 1)

            def sb_cumsum(b):
                pe.wait_ge(sem("sb_softplus"), 2 * b + 2)
                for h in range(4):
                    pe.matmul(ps[:, 4 + h, 0:T], neg_tri[:, :], T2[:, h, 0:T], start=False, stop=False, skip_group_check=True)
                    pe.matmul(ps[:, 4 + h, P:T], neg_ones[:, :], T2[:, h, T:T + P], start=False, stop=False, skip_group_check=True)
                    ins = pe.matmul(ps[:, 4 + h, T:T + P], neg_tri[:, :], T2[:, h, T:T + P], start=False, stop=True, skip_group_check=True)
                ins.then_inc(sem("sb_cumsum"), 1)

            def sb_values(b):
                pe.wait_ge(sem("sb_a"), 2 * b + 2)
                for h in range(4):
                    c = COL_VSB + (4 * b + h) * HD
                    o = ps[:, 4 + h // 2, (h % 2) * T:(h % 2 + 1) * T]
                    pe.matmul(o[:, 0:P], T1[:, h, 0:P], PROJ[:, 0, c:c + HD], start=True, stop=True)
                    pe.matmul(o[:, P:T], T1[:, h, P:T], PROJ[:, 0, c:c + HD], start=True, stop=False)
                    ins = pe.matmul(o[:, P:T], T1[:, h, T:T + P], PROJ[:, 1, c:c + HD], start=False, stop=True)
                ins.then_inc(sem("sb_pv"), 1)

            def compress(v, a, b):
                pe.wait_ge(sem("blocks_ready"), 2 * v + 2)
                for s in range(a, b):
                    g = v * CMP_STEPS // 2 + s
                    loaded(pe, g % RAW, RAW_CMP + g)
                    for j in range(CMP_L):
                        l = CMP_L * s + j
                        ins = pe.matmul(ps[0:64, 7, v * CMP_HIDDEN:(v + 1) * CMP_HIDDEN], BLK[:, v, l, :], raw[:, g % RAW, j * CMP_HIDDEN:(j + 1) * CMP_HIDDEN],
                                        start=l == 0, stop=l == CMP_BLOCK - 1)
                    ins.then_inc(cmp_used, 1)

            def turn_queries(b):
                for h in range(4):
                    ins = turn_head(h // 2, (h % 2) * T, COL_Q + (4 * b + h) * HD)
                ins.then_inc(sem("q_turned"), 1)

            pe.sem_inc(split_free, 2)
            pe.wait_ge(sem("constants"), 11)
            pe.wait_ge(sem("gains_loaded"), 16 * 7)
            pe.transpose(psf[:, 0:G_ALL], gain_rows[0:G_ALL, :], ident[0:G_ALL, 0:G_ALL]).then_inc(sem("gains_turned"), 1)
            pe.wait_ge(sem("table_loaded"), 32)
            pe.matmul(ps[0:NH, 7, :], TABLE, ONEHOT, start=True, stop=True).then_inc(sem("bias_mm"), 1)
            pe.wait_ge(sem("gains_ready"), 1)
            pe.wait_ge(sem("bias_rows"), 1)
            turn_rows(0, 2)
            with pe.Fori(0, FIRST_BESIDE // 2) as pair:
                c = pair * 2
                gemm_chunk(c, 0, c * STEPS_PER_CHUNK + SP_IN, 0)
                gemm_chunk(c + 1, 1, c * STEPS_PER_CHUNK + STEPS_PER_CHUNK + SP_IN, 0)

            for n in range(BESIDE_STEPS):
                g = FIRST_BESIDE * STEPS_PER_CHUNK + n
                c, s = g // STEPS_PER_CHUNK, g % STEPS_PER_CHUNK
                if s == 0:
                    pe.wait_ge(acc_free, c + 1)
                b = n // 12
                if n % 12 == 0:
                    if b:
                        pe.wait_ge(sem("sb_out"), b)
                    sb_turn(b)
                if n % 12 == 2:
                    sb_scores(b)
                if n % 12 == 8:
                    sb_cumsum(b)
                if n % 12 == 11:
                    sb_values(b)
                if n == BESIDE_STEPS - 1:
                    for v, col in enumerate((COL_KCMP, COL_VCMP)):
                        for g2 in range(NG):
                            ins = turn_head(6 + v, g2 * T, col + g2 * HD)
                    ins.then_inc(sem("cv_turned"), 1)
                gemm_step([ps[:, 2 * (c % 2) + t, :] for t in range(TT)], s % SPLIT, (2 * s, 2 * s + 1),
                          SP_IN + g)
            pe.wait_ge(acc_free, CH_TAIL + 1)
            for s in range(TAIL_STEPS):
                pe.wait_ge(split_done, SP_TAIL + s + 1)
                for j in range(TAIL_K):
                    k = TAIL_K * s + j
                    w_h = split_hi[:, s, j * N_GATES:(j + 1) * N_GATES]
                    w_l = split_lo[:, s, j * N_GATES:(j + 1) * N_GATES]
                    acc = ps[0:N_GATES, 2, 0:T]
                    pe.matmul(acc, w_h, ht[:, k, 0:T], start=k == 0, stop=False)
                    pe.matmul(acc, w_h, ht[:, k, T:2 * T], start=False, stop=False)
                    ins = pe.matmul(acc, w_l, ht[:, k, 0:T], start=False, stop=k == KC - 1)
                ins.then_inc(split_free, 1)

            pe.wait_ge(acc_free, 2 + W_IN_CHUNKS)
            compress(0, 0, 4)
            pe.wait_ge(sem("gates_ready"), 1)
            for t in range(TT):
                ins = pe.transpose(ps[:, 2, T + t * N_GATES:T + (t + 1) * N_GATES], GATES_T[:, t * P:(t + 1) * P], ident[0:N_GATES, 0:N_GATES])
            ins.then_inc(sem("gates_turned"), 1)
            pe.wait_ge(sem("kvc_ready"), 1)
            pe.wait_ge(sem("nsa_normed"), 1)
            turn_queries(0)
            pe.wait_ge(acc_free, 2 + CH_TAIL + 1)
            for b, col in enumerate((COL_KSLC, COL_KWIN)):
                for g in range(NG):
                    ins = turn_head(2 + b, g * T, col + g * HD)
            ins.then_inc(sem("k_turned"), 1)
            compress(0, 4, 8)
            pe.wait_ge(sem("sb_out"), 2)
            turn_rows(1, 4, 0, 4)
            pe.wait_ge(sem("q_ready"), 1)
            turn_queries(1)
            compress(1, 0, 4)
            pe.wait_ge(sem("ht_lo"), KC + 4)
            turn_rows(1, 4, 4, 8)

            def round_scores(r):
                if r >= 2:
                    pe.wait_ge(sem("ns_shifted"), r - 1)
                for h in range(2):
                    hh = 2 * (r % 4) + h
                    bank = 2 * (r % 2) + h
                    pe.matmul(ps[:, bank, 0:P], QT[:, hh, 0:P], KT[:, r // 4, hh // GROUP, 0:P], start=True, stop=True)
                    ins = pe.matmul(ps[:, bank, P:3 * P], QT[:, hh, P:T], KT[:, r // 4, hh // GROUP, :], start=True, stop=True)
                ins.then_inc(sem("ns_s"), 1)

            def round_turn(r):
                pe.wait_ge(sem("ns_exp"), 4 * r + 4)
                if r:
                    pe.wait_ge(sem("ns_pt"), r)
                for j in range(6):
                    ins = pe.transpose(psf[:, 4 * 512 + j * P:4 * 512 + (j + 1) * P], T1r[:, r % 2, j // 3, (j % 3) * P:(j % 3 + 1) * P], ident[:, :])
                ins.then_inc(sem("ns_p_turned"), 1)

            def round_values(r):
                pe.wait_ge(sem("ns_pt"), r + 1)
                if r:
                    pe.wait_ge(sem("ns_out"), r)
                for h in range(2):
                    c = (COL_VSLC, COL_VWIN)[r // 4] + (2 * (r % 4) + h) // GROUP * HD
                    o = ps[:, 6, h * T:(h + 1) * T]
                    pe.matmul(o[:, 0:P], T2r[:, r % 2, 3 * h, :], PROJ[:, 0, c:c + HD], start=True, stop=True)
                    pe.matmul(o[:, P:T], T2r[:, r % 2, 3 * h + 1, :], PROJ[:, 0, c:c + HD], start=True, stop=False)
                    ins = pe.matmul(o[:, P:T], T2r[:, r % 2, 3 * h + 2, :], PROJ[:, 1, c:c + HD], start=False, stop=True)
                ins.then_inc(sem("ns_pv"), 1)

            def cmp_stage(r):
                if r == 1:
                    pe.wait_ge(sem("hidden"), 1)
                    for v in range(2):
                        for f in range(2):
                            ins = pe.transpose(ps[:, 7, (2 * v + f) * 64:(2 * v + f + 1) * 64], HG[0:64, v, f * P:(f + 1) * P], ident[0:64, 0:64])
                    ins.then_inc(sem("hidden_turned"), 1)
                if r == 2:
                    pe.wait_ge(sem("hidden_t"), 1)
                    pe.wait_ge(sem("w2_loaded"), 32)
                    for v in range(2):
                        for g in range(NG):
                            for f in range(2):
                                ins = pe.matmul(ps[0:NC, 7, (v * NG + g) * HD:(v * NG + g + 1) * HD], HGT[:, 2 * v + f, 32 * g:32 * g + NC],
                                                W2S[:, 2 * v + f, :], start=f == 0, stop=f == 1)
                    ins.then_inc(sem("cmp_kv"), 1)
                if r == 4:
                    pe.wait_ge(sem("kc_ready"), 1)
                    for g in range(NG):
                        ins = pe.transpose(ps[:, 7, 16 * g:16 * g + NC], KCV[0:NC, 0, g, :], ident[0:NC, 0:NC])
                    ins.then_inc(sem("kc_turned"), 1)
                if r == 5:
                    pe.wait_ge(sem("kct_ready"), 1)
                    for h in range(NH):
                        for t in range(TT):
                            o = (h * TT + t) * 16
                            ins = pe.matmul(ps[:, 7, o:o + NC], QT[:, h, t * P:(t + 1) * P], KCT[:, h // GROUP, 0:NC], start=True, stop=True)
                    ins.then_inc(sem("cmp_s"), 1)

            pe.wait_ge(sem("k_ready"), 1)
            pe.wait_ge(sem("q_ready"), 2)
            round_scores(0)
            round_scores(1)
            compress(1, 4, 8)
            pe.wait_ge(sem("ht_lo"), KC + 8)
            for r in range(ROUNDS):
                round_turn(r)
                if r + 2 < ROUNDS:
                    round_scores(r + 2)
                round_values(r)
                cmp_stage(r)
            pe.wait_ge(sem("cmp_exp"), 1)
            for b in range(16):
                ins = pe.transpose(psf[0:NC, b * P:(b + 1) * P], cmp_p[:, b * NC:(b + 1) * NC], ident[:, :])
            ins.then_inc(sem("cmp_p_turned"), 1)
            pe.wait_ge(sem("cmp_pt"), 1)
            pe.wait_ge(sem("ns_out"), ROUNDS)
            for b in range(16):
                ins = pe.matmul(psf[:, 2048 + b * P:2048 + (b + 1) * P], PCT[0:NC, b, :], KCV[0:NC, 1, b // TT // GROUP, :], start=True, stop=True)
            ins.then_inc(sem("cmp_pv"), 1)

            acc = [ps[:, 2 * (CH_OUT % 2) + t, :] for t in range(TT)]
            for n in range(STEPS_PER_CHUNK):
                if n == 3:
                    pe.wait_ge(sem("nsa_out"), 1)
                    turn_rows(1, 6, KC // 2, KC)
                pe.wait_ge(sem("ht_lo"), KC + 2 * n + 2)
                gemm_step(acc, n % SPLIT, (2 * n, 2 * n + 1), SP_OUT + n)
            for c in range(1, W_CHUNKS):
                gemm_chunk(CH_OUT + c, (CH_OUT + c) % 2, c * STEPS_PER_CHUNK + SP_OUT, 1)
            turn_rows(2, 8)
            def turn_chunk(c):
                pe.wait_ge(acc_free, 2 + CH_QUERY + c + 1)
                for w in range(4):
                    for t in range(TT):
                        ins = pe.transpose(psf[:, 4 * 512 + w * T + t * P:4 * 512 + w * T + (t + 1) * P],
                                           Q[:, t, (4 * c + w) * P:(4 * c + w + 1) * P], ident[:, :])
                ins.then_inc(sem("pq_turned"), 1)

            def chunk_scores(c):
                pe.wait_ge(sem("pq_ready"), c + 1)
                if c:
                    pe.wait_ge(sem("scores_read"), c)
                for t in range(TT):
                    for w in range(4):
                        ins = pe.matmul(ps[:, 6 + t, w * P:(w + 1) * P], PQT[:, 4 * c + w, t * P:(t + 1) * P], SKT[:, 4 * c + w, :],
                                        start=True, stop=True)
                ins.then_inc(sem("scores"), 1)

            gemm_chunk(CH_QUERY, CH_QUERY % 2, SP_QUERY, 2)
            for c in range(1, W_CHUNKS):
                pe.wait_ge(acc_free, CH_QUERY + c + 1)
                for n in range(STEPS_PER_CHUNK):
                    if n == 0 and c == 1:
                        pe.wait_ge(sem("keys_loaded"), 16)
                        pe.wait_ge(sem("ht_lo"), 3 * KC)
                        for w in range(HP):
                            ins = pe.transpose(psf[:, 4 * 512 + w * P:4 * 512 + (w + 1) * P], SK[:, w, :], ident[:, :])
                        ins.then_inc(sem("keys_turned"), 1)
                    if n == 3:
                        if c == 1:
                            pe.wait_ge(sem("keys_ready"), 1)
                        turn_chunk(c - 1)
                    if n == 5:
                        chunk_scores(c - 1)
                    gemm_step([ps[:, 2 * ((CH_QUERY + c) % 2) + t, :] for t in range(TT)], n % SPLIT, (2 * n, 2 * n + 1),
                              SP_QUERY + c * STEPS_PER_CHUNK + n)
            pe.sem_inc(sem("s_summed"), 2)
            pe.sem_inc(sem("acted"), 2)

            def turn_unit(i, j, u):
                slot = 2 * (j % 2) + u // 2
                if u % 2 == 0:
                    pe.wait_ge(raw_loaded[slot], i * 8 + 16 * (j // 2 + RAW_U // RAW + 1))
                pe.wait_ge(split_done, i * UNITS + j * UNITS + u + SP_U - 3)
                for k in range(UNIT_K):
                    c = (u % 2) * UNIT + k * P
                    ins = pe.transpose(ps[:, u, k * P:(k + 1) * P], raw[:, slot, c:c + P], ident[:, :])
                ins.then_inc(u_turned, 1)

            def u_tile(i, j, last=False):
                for u in range(UNITS):
                    if not (last and u >= 2):
                        turn_unit(i, j + (u + 2) // UNITS, (u + 2) % UNITS)
                    if u == 0:
                        pe.wait_ge(sem("s_summed"), i + j + 1)
                    pe.wait_ge(split_done, i * UNITS + j * UNITS + u + SP_U + 1)
                    acc = ps[:, 4 + j % 2, :]
                    for k in range(UNIT_K):
                        kk = UNIT_K * u + k
                        c = u * UNIT + k * P
                        pe.matmul(acc, unit_hi[:, c:c + P], ht[:, kk, :], start=kk == 0, stop=False, skip_group_check=True)
                        ins = pe.matmul(acc[:, T:2 * T], unit_lo[:, c:c + P], ht[:, kk, 0:T], start=False, stop=kk == KC - 1, skip_group_check=True)
                    ins.then_inc(split_free, 1)

            turn_unit(0, 0, 0)
            turn_unit(0, 0, 1)
            turn_chunk(W_CHUNKS - 1)
            chunk_scores(W_CHUNKS - 1)
            with pe.Fori(0, HEADS) as head:
                for j in range(TILES_PER_HEAD):
                    u_tile(head * TILES_PER_HEAD, j)
            u_tile(ROUTE_TILES, 0)
            pe.wait_ge(sem("picks"), 1)
            for s, (bank, o) in enumerate(((6, 0), (7, 0), (6, T))):
                for t in range(TT):
                    ins = pe.transpose(ps[:, bank, o + t * P:o + (t + 1) * P], PICK[:, s, t].rearrange("p h k -> p (h k)"), ident[:, :])
            ins.then_inc(sem("picks_turned"), 1)
            pe.wait_ge(sem("picked_ready"), 3)

            pe.sem_inc(sem("gates_mm"), 2)
            pe.sem_inc(sem("gates_built"), 2)

            def build_step(s, j):
                pe.wait_ge(sem("onehot_i"), s + j + 1)
                pe.wait_ge(sem("onehot_j"), s + j + 1)
                pe.wait_ge(sem("gates_built"), s + j + 1)
                for c in range(TOKENS_PER_BANK):
                    ins = pe.matmul(ps[:, 6 + j, c * P:(c + 1) * P], one_j[j][:, c * P:(c + 1) * P].bitcast(F32),
                                    one_i[:, j, c * P:(c + 1) * P], start=True, stop=True)
                ins.then_inc(sem("gates_mm"), 1)

            build_step(0, 0)
            u_tile(ROUTE_TILES, 1)
            build_step(0, 1)
            with pe.Fori(1, BUILD_STEPS // 2 - 1) as pair:
                for j in range(2):
                    u_tile(pair * 2 + ROUTE_TILES, j)
                    build_step(pair * 2, j)
            for j in range(2):
                u_tile(NE_T - 2, j, last=j == 1)
                build_step(BUILD_STEPS - 2, j)
            pe.wait_ge(sem("gates_built"), BUILD_STEPS + 2)

            def v_tile(i, j, first, last):
                pe.wait_ge(sem("w_lo_done"), i + j + 1)
                for f in range(2):
                    pe.wait_ge(split_done, i * 2 + 2 * j + f + SP_V + 1)
                    for t in range(TT):
                        g_h = w_hi[:, j, t * P:(t + 1) * P]
                        g_l = w_lo[:, j, t * P:(t + 1) * P]
                        for c in range(2):
                            acc = ps[:, 4 * t + 2 * f + c, :]
                            v_h = split_hi[:, f, c * 512:(c + 1) * 512]
                            v_l = split_lo[:, f, c * 512:(c + 1) * 512]
                            pe.matmul(acc, g_h, v_h, start=first, stop=False)
                            pe.matmul(acc, g_h, v_l, start=False, stop=False)
                            ins = pe.matmul(acc, g_l, v_h, start=False, stop=last)
                    ins.then_inc(split_free, 1)

            v_tile(0, 0, True, False)
            v_tile(0, 1, False, False)
            with pe.Fori(1, NE_T // 2 - 1) as pair:
                i = pair * 2
                v_tile(i, 0, False, False)
                v_tile(i, 1, False, False)
            v_tile(NE_T - 2, 0, False, False)
            v_tile(NE_T - 2, 1, False, True)


_INS = ['x', 'norm1_g', 'w_in', 'cmp_pe', 'cmp_k_w1', 'cmp_k_w2', 'cmp_v_w1', 'cmp_v_w2', 'q_norm_g', 'k_norm_g',
        'rel_bias_table', 'sb_out_g', 'nsa_out_g', 'w_out', 'norm2_g', 'peer_w_query', 'peer_sub_keys',
        'peer_expert_u', 'peer_expert_v']


def kernel(**inputs):
    import numpy as _np
    import concourse.bacc as _bacc
    from concourse import mybir as _mybir
    from concourse.bass_utils import run_bass_kernel_spmd as _run

    nc = _bacc.Bacc("TRN2", target_bir_lowering=False, num_devices=1)
    arrays, args = {}, []
    for name in _INS:
        a = _np.ascontiguousarray(inputs[name])
        arrays[f"in_{name}"] = a
        args.append(nc.dram_tensor(f"in_{name}", a.shape, _mybir.dt.from_np(a.dtype), kind="ExternalInput").ap())
    a = bucket_onehot()
    arrays["bucket_onehot"] = a
    args.append(nc.dram_tensor("bucket_onehot", a.shape, _mybir.dt.from_np(a.dtype), kind="ExternalInput").ap())
    args.append(nc.dram_tensor("out_0", (1, T, D), _mybir.dt.float32, kind="ExternalOutput").ap())
    layer(nc, *args)
    r = _run(nc, [arrays], core_ids=[0])
    return r.results[0]["out_0"]
```
